# Optimizing a Trainium2 kernel written in Bass

```python
import jax, jax.numpy as jnp
from jax import lax
import numpy as np

D_MODEL = 1024
BATCH = 1
SEQ = 1024
DEPTH = 1

HEAD_DIM = 64
NSA_HEADS = 8
NSA_KV = 2
SWA_HEADS = 8
SWA_KV = 2
SWA_WINDOW = 128
NSA_CMP_LEN = 32
NSA_CMP_STRIDE = 16
NSA_CMP_HIDDEN = 4 * HEAD_DIM
NSA_SEL_LEN = 64
NSA_TOP_N = 16
NSA_WINDOW = 512
BLOCK_Q = 128
SEL_Q_BLOCK = 64
D_FF = 4 * D_MODEL
LN_EPS = 1e-5
NEG_INF = -1e30
FORCE_SCORE = 1e9

NSA_Q = NSA_HEADS * HEAD_DIM
NSA_KVW = NSA_KV * HEAD_DIM
SWA_Q = SWA_HEADS * HEAD_DIM
SWA_KVW = SWA_KV * HEAD_DIM
IN_SIZES = (NSA_Q, NSA_KVW, NSA_KVW, NSA_KVW, NSA_KVW, NSA_KVW, NSA_KVW, 3 * NSA_HEADS, SWA_Q, SWA_KVW, SWA_KVW, D_MODEL, D_MODEL)
IN_COLS = sum(IN_SIZES)

kernel_name = "nsa_swa_sink_hybrid_deepnorm"

def split_offsets():
    offs, acc = [], 0
    for s in IN_SIZES[:-1]:
        acc += s
        offs.append(acc)
    return offs

def layer_norm(x, g, b):
    xf = x.astype(jnp.float32)
    mu = jnp.mean(xf, -1, keepdims=True)
    var = jnp.mean(jnp.square(xf - mu), -1, keepdims=True)
    y = (xf - mu) * lax.rsqrt(var + LN_EPS)
    return (y * g.astype(jnp.float32) + b.astype(jnp.float32)).astype(x.dtype)

def alibi_slopes(n):
    return jnp.exp2(-8.0 * jnp.arange(1, n + 1, dtype=jnp.float32) / n)

def banded_attention(q, k, v, slopes, window, sinks=None):
    B, S, H, dh = q.shape
    G = k.shape[2]
    R = H // G
    nb = S // BLOCK_Q
    nprev = window // BLOCK_Q
    pad = nprev * BLOCK_Q

    def band(z):
        zp = jnp.pad(z, ((0, 0), (pad, 0), (0, 0), (0, 0))).reshape(B, nb + nprev, BLOCK_Q, G, dh)
        return jnp.concatenate([zp[:, i:i + nb] for i in range(nprev + 1)], axis=2)

    kb, vb = band(k), band(v)
    qb = q.reshape(B, nb, BLOCK_Q, G, R, dh)
    scores = jnp.einsum('bnqgrd,bnkgd->bgrnqk', qb, kb).astype(jnp.float32) * (dh ** -0.5)
    blk = jnp.arange(nb)[:, None] * BLOCK_Q
    t = blk + jnp.arange(BLOCK_Q)[None, :]
    s = blk - pad + jnp.arange((nprev + 1) * BLOCK_Q)[None, :]
    dist = t[:, :, None] - s[:, None, :]
    valid = (dist >= 0) & (dist < window) & (s[:, None, :] >= 0)
    scores = scores - slopes.reshape(G, R, 1, 1, 1) * dist
    scores = jnp.where(valid, scores, NEG_INF)
    if sinks is not None:
        sink = jnp.broadcast_to(sinks.astype(jnp.float32).reshape(1, G, R, 1, 1, 1), scores.shape[:-1] + (1,))
        probs = jax.nn.softmax(jnp.concatenate([scores, sink], -1), -1)[..., :-1]
    else:
        probs = jax.nn.softmax(scores, -1)
    out = jnp.einsum('bgrnqk,bnkgd->bnqgrd', probs.astype(v.dtype), vb)
    return out.reshape(B, S, G, R, dh)

def compress_blocks(blocks, pos, w1, w2):
    h = jax.nn.gelu(jnp.einsum('bclgd,ldf->bcgf', blocks + pos[:, None, :], w1))
    return jnp.einsum('bcgf,fd->bcgd', h, w2)

def selection_overlap(n_c, n_sel):
    ci = jnp.arange(n_c)[:, None] * NSA_CMP_STRIDE
    sj = jnp.arange(n_sel)[None, :] * NSA_SEL_LEN
    ov = jnp.minimum(ci + NSA_CMP_LEN, sj + NSA_SEL_LEN) - jnp.maximum(ci, sj)
    return jnp.clip(ov, 0, None).astype(jnp.float32) / NSA_CMP_LEN

def selected_attention(q, k, v, sel, slopes):
    B, S, G, R, dh = q.shape
    k_top = sel.shape[-1]
    nq = S // SEL_Q_BLOCK
    n_keys = k_top * NSA_SEL_LEN
    k_t = k.transpose(0, 2, 1, 3)
    v_t = v.transpose(0, 2, 1, 3)
    bi = jnp.arange(B)[:, None, None]
    gi = jnp.arange(G)[None, :, None]
    offs = jnp.arange(NSA_SEL_LEN)
    scale = dh ** -0.5

    def one_block(args):
        qb, ib, tb = args
        pos = (ib[..., None] * NSA_SEL_LEN + offs).reshape(B, G, -1)
        kg = k_t[bi, gi, pos].reshape(B, G, SEL_Q_BLOCK, n_keys, dh)
        vg = v_t[bi, gi, pos].reshape(B, G, SEL_Q_BLOCK, n_keys, dh)
        sc = jnp.einsum('bqgrd,bgqnd->bgrqn', qb, kg).astype(jnp.float32) * scale
        dist = tb[:, None] - pos.reshape(B, G, 1, SEL_Q_BLOCK, n_keys)
        sc = sc - slopes.reshape(1, G, R, 1, 1) * dist
        p = jax.nn.softmax(jnp.where(dist >= 0, sc, NEG_INF), -1)
        return jnp.einsum('bgrqn,bgqnd->bqgrd', p.astype(vg.dtype), vg)

    qs = q.reshape(B, nq, SEL_Q_BLOCK, G, R, dh).transpose(1, 0, 2, 3, 4, 5)
    ids = sel.reshape(B, G, nq, SEL_Q_BLOCK, k_top).transpose(2, 0, 1, 3, 4)
    ts = jnp.arange(S).reshape(nq, SEL_Q_BLOCK)
    out = lax.map(one_block, (qs, ids, ts))
    return out.transpose(1, 0, 2, 3, 4, 5).reshape(B, S, G, R, dh)

def nsa_attention(q, kc, vc, ks, vs, kw, vw, gates, slopes, pos_k, w1k, w2k, pos_v, w1v, w2v):
    B, S, G, R, dh = q.shape
    scale = dh ** -0.5
    n_c = (S - NSA_CMP_LEN) // NSA_CMP_STRIDE + 1
    n_sel = S // NSA_SEL_LEN
    k_top = min(NSA_TOP_N, n_sel)
    t = jnp.arange(S)
    idx = jnp.arange(n_c)[:, None] * NSA_CMP_STRIDE + jnp.arange(NSA_CMP_LEN)[None, :]
    k_cmp = compress_blocks(kc[:, idx], pos_k, w1k, w2k)
    v_cmp = compress_blocks(vc[:, idx], pos_v, w1v, w2v)
    sc = jnp.einsum('bsgrd,bcgd->bgrsc', q, k_cmp).astype(jnp.float32) * scale
    blk_end = jnp.arange(n_c) * NSA_CMP_STRIDE + NSA_CMP_LEN - 1
    c_valid = blk_end[None, :] <= t[:, None]
    has_block = (t >= NSA_CMP_LEN - 1).astype(jnp.float32)[:, None]
    p_cmp = jax.nn.softmax(jnp.where(c_valid, sc, NEG_INF), -1) * has_block
    o_cmp = jnp.einsum('bgrsc,bcgd->bsgrd', p_cmp.astype(v_cmp.dtype), v_cmp)
    imp = jnp.einsum('bgrsc,cj->bgsj', p_cmp, selection_overlap(n_c, n_sel))
    j = jnp.arange(n_sel)[None, :]
    cur = (t // NSA_SEL_LEN)[:, None]
    forced = (j == 0) | (j == cur) | (j == cur - 1)
    causal = j * NSA_SEL_LEN <= t[:, None]
    imp = jnp.where(forced, FORCE_SCORE, jnp.where(causal, imp, -FORCE_SCORE))
    _, sel = lax.top_k(imp, k_top)
    o_slc = selected_attention(q, ks, vs, sel, slopes)
    o_win = banded_attention(q.reshape(B, S, G * R, dh), kw, vw, slopes, NSA_WINDOW)
    g = jax.nn.sigmoid(gates.astype(jnp.float32)).astype(q.dtype).reshape(B, S, G, R, 3)
    return g[..., 0:1] * o_cmp + g[..., 1:2] * o_slc + g[..., 2:3] * o_win

def hybrid_mixer(u, w_in, pos_k, w1k, w2k, pos_v, w1v, w2v, sinks, w_branch_a, w_branch_b, w_out):
    B, S, _ = u.shape
    q_a, kc, vc, ks, vs, kw, vw, g_a, q_b, k_b, v_b, gate_a, gate_b = jnp.split(u @ w_in, split_offsets(), axis=-1)

    def heads(z, n):
        return z.reshape(B, S, n, HEAD_DIM)

    slopes = alibi_slopes(SWA_HEADS + NSA_HEADS)
    o_a = nsa_attention(q_a.reshape(B, S, NSA_KV, NSA_HEADS // NSA_KV, HEAD_DIM),
                        heads(kc, NSA_KV), heads(vc, NSA_KV), heads(ks, NSA_KV), heads(vs, NSA_KV),
                        heads(kw, NSA_KV), heads(vw, NSA_KV), g_a, slopes[SWA_HEADS:],
                        pos_k, w1k, w2k, pos_v, w1v, w2v)
    o_b = banded_attention(heads(q_b, SWA_HEADS), heads(k_b, SWA_KV), heads(v_b, SWA_KV),
                           slopes[:SWA_HEADS], SWA_WINDOW, sinks)
    y_a = o_a.reshape(B, S, NSA_Q) @ w_branch_a
    y_b = o_b.reshape(B, S, SWA_Q) @ w_branch_b
    merged = jax.nn.sigmoid(gate_a) * y_a + jax.nn.sigmoid(gate_b) * y_b
    return merged @ w_out

def setup_inputs(seed: int = 0) -> dict:
    key = jax.random.key(seed)
    ks = jax.random.split(key, 18)
    beta = (8.0 * DEPTH) ** -0.25

    def nrm(k, shape, scale):
        return jax.random.normal(k, shape, jnp.float32) * scale

    return {
        "x": nrm(ks[0], (BATCH, SEQ, D_MODEL), 1.0),
        "w_in": nrm(ks[1], (DEPTH, D_MODEL, IN_COLS), D_MODEL ** -0.5),
        "cmp_pos_k": nrm(ks[2], (DEPTH, NSA_CMP_LEN, HEAD_DIM), 0.02),
        "cmp_w1_k": nrm(ks[3], (DEPTH, NSA_CMP_LEN, HEAD_DIM, NSA_CMP_HIDDEN), (NSA_CMP_LEN * HEAD_DIM) ** -0.5),
        "cmp_w2_k": nrm(ks[4], (DEPTH, NSA_CMP_HIDDEN, HEAD_DIM), NSA_CMP_HIDDEN ** -0.5),
        "cmp_pos_v": nrm(ks[5], (DEPTH, NSA_CMP_LEN, HEAD_DIM), 0.02),
        "cmp_w1_v": nrm(ks[6], (DEPTH, NSA_CMP_LEN, HEAD_DIM, NSA_CMP_HIDDEN), (NSA_CMP_LEN * HEAD_DIM) ** -0.5),
        "cmp_w2_v": nrm(ks[7], (DEPTH, NSA_CMP_HIDDEN, HEAD_DIM), NSA_CMP_HIDDEN ** -0.5),
        "sink_logits": nrm(ks[8], (DEPTH, SWA_HEADS), 0.5),
        "w_branch_a": nrm(ks[9], (DEPTH, NSA_Q, D_MODEL), beta * NSA_Q ** -0.5),
        "w_branch_b": nrm(ks[10], (DEPTH, SWA_Q, D_MODEL), beta * SWA_Q ** -0.5),
        "w_out": nrm(ks[11], (DEPTH, D_MODEL, D_MODEL), beta * D_MODEL ** -0.5),
        "ln1_g": 1.0 + nrm(ks[12], (DEPTH, D_MODEL), 0.02),
        "ln1_b": nrm(ks[13], (DEPTH, D_MODEL), 0.02),
        "w_up": nrm(ks[14], (DEPTH, D_MODEL, D_FF), D_MODEL ** -0.5),
        "w_down": nrm(ks[15], (DEPTH, D_FF, D_MODEL), beta * D_FF ** -0.5),
        "ln2_g": 1.0 + nrm(ks[16], (DEPTH, D_MODEL), 0.02),
        "ln2_b": nrm(ks[17], (DEPTH, D_MODEL), 0.02),
    }

def reference(x, w_in, cmp_pos_k, cmp_w1_k, cmp_w2_k, cmp_pos_v, cmp_w1_v, cmp_w2_v, sink_logits,
              w_branch_a, w_branch_b, w_out, ln1_g, ln1_b, w_up, w_down, ln2_g, ln2_b):
    alpha = (2.0 * DEPTH) ** 0.25
    h = x
    for l in range(DEPTH):
        mix = hybrid_mixer(h, w_in[l], cmp_pos_k[l], cmp_w1_k[l], cmp_w2_k[l], cmp_pos_v[l], cmp_w1_v[l],
                           cmp_w2_v[l], sink_logits[l], w_branch_a[l], w_branch_b[l], w_out[l])
        h = layer_norm(alpha * h + mix, ln1_g[l], ln1_b[l])
        ff = jnp.square(jax.nn.relu(h @ w_up[l])) @ w_down[l]
        h = layer_norm(alpha * h + ff, ln2_g[l], ln2_b[l])
    return h


_drawn_inputs = setup_inputs


def setup_inputs(seed=0):
    import zlib

    import numpy as np

    out = dict(_drawn_inputs(seed))
    spreads = {}
    factors = {'cmp_pos_k': 8.0,
     'cmp_w1_k': 8.0,
     'cmp_w2_k': 7.933,
     'cmp_pos_v': 8.0,
     'cmp_w1_v': 3.642,
     'sink_logits': 8.0,
     'ln1_g': 2.774,
     'ln2_g': 8.172,
     'ln2_b': 8.219,
     'ln1_b': 6.667}
    for name, (base, spread) in spreads.items():
        noise = np.random.default_rng([zlib.crc32(name.encode()), seed]).standard_normal(out[name].shape)
        drawn = base * np.exp(spread * noise) if base else spread * noise
        out[name] = __import__('jax').numpy.asarray(drawn.astype(out[name].dtype))
    for name, factor in factors.items():
        out[name] = (out[name] * factor).astype(out[name].dtype)
    return out
```

```python
from contextlib import ExitStack

import numpy as np
import concourse.bass as bass
from concourse import mybir

F32 = mybir.dt.float32
F32R = mybir.dt.float32r
ALU = mybir.AluOpType
ACT = mybir.ActivationFunctionType

P = 128
SEQ = 1024
D_MODEL = 1024
HEAD_DIM = 64
HEADS = 8
KV = 2
R = HEADS // KV
CMP_LEN = 32
CMP_STRIDE = 16
CMP_HIDDEN = 4 * HEAD_DIM
SWA_WINDOW = 128
NSA_WINDOW = 512
D_FF = 4 * D_MODEL
LN_EPS = 1e-5
MASKED = -2.0 ** 100
ALPHA = 2.0 ** 0.25
QB = SEQ // P
KT = D_MODEL // P
HALF = 512
CB = 64
CT = CMP_LEN * HEAD_DIM // P
BRANCHES = 3
CHUNK = 2
CHUNKS = D_FF // (CHUNK * P)

KVW = KV * HEAD_DIM
COL_QA = 0
COL_KC = HEADS * HEAD_DIM
COL_VC = COL_KC + KVW
COL_KS = COL_VC + KVW
COL_VS = COL_KS + KVW
COL_KW = COL_VS + KVW
COL_VW = COL_KW + KVW
COL_GA = COL_VW + KVW
COL_QB = COL_GA + BRANCHES * HEADS
COL_KB = COL_QB + HEADS * HEAD_DIM
COL_VB = COL_KB + KVW
COL_GATE_A = COL_VB + KVW
COL_GATE_B = COL_GATE_A + D_MODEL

SLOPES = [2.0 ** (-8.0 * (i + 1) / (2 * HEADS)) for i in range(2 * HEADS)]
GELU_IN = (2.0 / np.pi) ** 0.5


def at_least(engine, sem, count):
    if not (isinstance(count, int) and count <= 0):
        engine.wait_ge(sem, count)


def attention_units():
    units, step, part, seg, block = [], 0, 0, 0, 0
    for kind, g, qb in ([("swa", g, qb) for g in range(KV) for qb in range(QB)]
                        + [(kind, g, qb) for g in range(KV) for qb in range(QB) for kind in ("slc", "wc")]):
        u = {"kind": kind, "g": g, "qb": qb, "step": step, "number": len(units), "parts": [], "blocks": []}
        if kind == "swa":
            first = max(0, qb - SWA_WINDOW // P)
            keys = (qb + 1 - first) * P
            u["parts"] = [[{"r": r, "what": "swa", "key0": first * P, "keys": keys, "score0": r * 2 * P,
                            "table0": 2 * P - keys, "at": 0} for r in range(R)]]
            u["blocks"] = [("swa", kb, (kb - first) * P) for kb in range(first, qb + 1)]
        elif kind == "slc":
            keys = (qb + 1) * P
            u["parts"] = [[{"r": r, "what": "slc", "key0": 0, "keys": keys, "score0": 0,
                            "table0": SEQ + P - keys, "at": 0}] for r in range(R)]
            u["blocks"] = [("slc", kb, kb * P) for kb in range(qb + 1)]
        else:
            first = max(0, qb - NSA_WINDOW // P)
            keys = (qb + 1 - first) * P
            width = NSA_WINDOW + P
            u["parts"] = [[{"r": r, "what": "win", "key0": first * P, "keys": keys, "score0": 0,
                            "table0": width - keys, "at": 0},
                           {"r": r, "what": "cmp", "key0": 0, "keys": CB, "score0": width,
                            "table0": 0, "at": width}] for r in range(R)]
            u["blocks"] = [("win", kb, (kb - first) * P) for kb in range(first, qb + 1)] + [("cmp", 0, width)]
        u["part0"], u["seg0"], u["block0"] = part, seg, block
        part += len(u["parts"])
        for segs in u["parts"]:
            for s in segs:
                s["number"], s["column"] = seg, seg - u["seg0"]
                seg += 1
        block += len(u["blocks"])
        u["segs"] = [s for segs in u["parts"] for s in segs]
        u["first_of_step"] = kind != "wc"
        u["last_of_step"] = kind != "slc"
        step += u["last_of_step"]
        units.append(u)
    return units, step, seg, block


def interleave(blocks, parts):
    items = [((i + 1) / (len(blocks) + 1), 1, "block", i) for i in range(len(blocks))]
    items += [((i + 0.5) / len(parts), 0, "part", i) for i in range(len(parts))] if parts else []
    return [(what, i) for _, _, what, i in sorted(items)]


def layer(nc, x, w_in, pos_k, w1_k, w2_k, pos_v, w1_v, w2_v, sinks, w_branch_a, w_branch_b, w_out,
          ln1_g, ln1_b, w_up, w_down, ln2_g, ln2_b, out):
    ctx = ExitStack()
    kb_ = 1024
    base = 16512

    def sb(name, at, shape, dt=F32):
        return nc.alloc_sbuf_tensor_at(name, shape, dt, offset=base + int(at * kb_))

    def sem(name):
        return ctx.enter_context(nc.semaphore(name))

    ident = sb("ident", 0, [P, P])
    slope_inv = sb("slope_inv", 0.5, [P, 16])
    sink_row = sb("sink_row", 0.5625, [P, HEADS])
    sink_y = sb("sink_y", 0.59375, [P, HEADS])
    eps = sb("eps", 0.625, [P, 1])
    bn = sb("bn", 0.75, [P, 2, 2, 6])
    mv = sb("mv", 0.875, [P, 2, 2])
    rstd = sb("rstd", 0.9375, [P, 2, 2])
    seen = sb("seen", 1.0, [P, 1])
    posT = sb("posT", 1.125, [P, 2 * CT])
    pos_nat = sb("pos_nat", 1.25, [2 * CT, P])
    qa = sb("qa", 2, [P, 4, SEQ])
    qb_ = sb("qb", 18, [P, 4, SEQ])
    merged = sb("merged", 2, [P, KT, SEQ])
    uh = [sb(f"uh{i}", 2 + 16 * i, [P, CHUNK, SEQ], F32R) for i in range(2)]
    ul = [sb(f"ul{i}", 10 + 16 * i, [P, CHUNK, SEQ], F32R) for i in range(2)]
    w_raw = [sb(f"w_raw{i}", 34 + 4 * i, [P, KT, P]) for i in range(2)]
    w_hi = [sb(f"w_hi{i}", 42 + 4 * i, [P, KT, P], F32R) for i in range(2)]
    w_lo = [sb(f"w_lo{i}", 50 + 4 * i, [P, KT, P], F32R) for i in range(2)]
    xh = sb("xh", 58, [P, KT, SEQ], F32R)
    xl = sb("xl", 90, [P, KT, SEQ], F32R)
    t_slc = sb("t_slc", 58, [P, SEQ + P])
    t_win = sb("t_win", 62.5, [P, NSA_WINDOW + P])
    t_swa = sb("t_swa", 65, [P, 2 * P])
    t_cmp = sb("t_cmp", 66, [P, QB, CB])
    p_slc = sb("p_slc", 68, [P, R, SEQ])
    p_wc = sb("p_wc", 84, [P, R, NSA_WINDOW + 2 * P])
    p_swa = [sb(f"p_swa{i}", 84 + 4 * i, [P, R, 2 * P]) for i in range(2)]
    pt_hi = [sb(f"pt_hi{i}", 96 + 4 * i, [P, R, P], F32R) for i in range(3)]
    pt_lo = [sb(f"pt_lo{i}", 98 + 4 * i, [P, R, P], F32R) for i in range(3)]
    q_st = [sb(f"q_st{i}", 108 + 2 * i, [P, R, P], F32R) for i in range(2)]
    o_sum = sb("o_sum", 112, [P, R, P])
    m_y = sb("m_y", 114, [P, 2, 8])
    m_neg = sb("m_neg", 114.125, [P, 2, 8])
    row_l = sb("row_l", 114.25, [P, 2, 8])
    row_s = sb("row_s", 114.375, [P, 2, 8])
    sink_e = sb("sink_e", 114.5, [P, 2, 8])
    slope_neg = sb("slope_neg", 114.625, [P, 8])
    wo_hi = sb("wo_hi", 58, [P, KT, D_MODEL], F32R)
    wo_lo = sb("wo_lo", 90, [P, KT, D_MODEL], F32R)
    hh = sb("hh", 58, [P, KT, SEQ], F32R)
    hl = sb("hl", 90, [P, KT, SEQ], F32R)
    kcs = [sb(f"kcs{i}", 122 + 4 * i, [P, SEQ]) for i in range(2 * KV)]
    cx = [sb(f"cx{i}", 138 + 8 * i, [P, CT, KV, CB]) for i in range(2)]
    cw1 = [sb(f"cw1{i}", 154 + 16 * i, [P, CT, CMP_HIDDEN]) for i in range(2)]
    cw2k = sb("cw2k", 186, [P, 2, 2, HEAD_DIM])
    cw2v = sb("cw2v", 187, [P, 2, HEAD_DIM])
    k_hi, k_lo, v_hl = {}, {}, {}
    for i, what in enumerate(("slc", "win", "swa")):
        k_hi[what] = sb(f"k_hi_{what}", 122 + 16 * i, [P, KV, SEQ], F32R)
        k_lo[what] = sb(f"k_lo_{what}", 130 + 16 * i, [P, KV, SEQ], F32R)
        v_hl[what] = sb(f"v_hl_{what}", 170 + 8 * i, [P, QB, KV, 2 * HEAD_DIM], F32R)
    oah = sb("oah", 122, [P, 4, SEQ], F32R)
    oal = sb("oal", 138, [P, 4, SEQ], F32R)
    obh = sb("obh", 154, [P, 4, SEQ], F32R)
    obl = sb("obl", 170, [P, 4, SEQ], F32R)
    sg_a = sb("sg_a", 186, [P, SEQ])
    sg_b = sb("sg_b", 190, [P, SEQ])
    acc = sb("acc", 122, [P, QB, D_MODEL])
    mst_hi = [sb(f"mst_hi{i}", 154 + 4 * i, [P, KT, P], F32R) for i in range(2)]
    mst_lo = [sb(f"mst_lo{i}", 162 + 4 * i, [P, KT, P], F32R) for i in range(2)]
    relu = [sb(f"relu{i}", 154 + 4 * i, [P, SEQ]) for i in range(2)]
    usq = [sb(f"usq{i}", 162 + 4 * i, [P, SEQ]) for i in range(2)]
    row_raw = [sb(f"row_raw{i}", 170 + 4 * i, [P, D_MODEL]) for i in range(2)]
    ln_g = sb("ln_g", 178, [P, D_MODEL])
    ln_b = sb("ln_b", 182, [P, D_MODEL])
    wd_hi = [sb(f"wd_hi{i}", 186 + 4 * i, [P, D_MODEL], F32R) for i in range(2)]
    x_raw = [sb(f"x_raw{i}", 194 + 4 * i, [P, D_MODEL]) for i in range(2)]
    g_in = sb("g_in", 194, [P, 2 * 2 * P])
    g_t = sb("g_t", 196, [P, 2 * 2 * P])
    g_u = sb("g_u", 198, [P, 2 * 2 * P])
    g_out = sb("g_out", 200, [P, 2, 2, KV, CB])
    vT = sb("vT", 194, [P, SEQ])
    gaT = sb("gaT", 198, [P, SEQ])
    wb_raw = sb("wb_raw", 194, [P, KT, P])
    wb_hi = sb("wb_hi", 198, [P, KT, P], F32R)
    wd_lo = [sb(f"wd_lo{i}", 194 + 4 * i, [P, D_MODEL], F32R) for i in range(2)]
    k_hi["cmp"] = sb("k_hi_cmp", 202, [P, KV, CB], F32R)
    k_lo["cmp"] = sb("k_lo_cmp", 202.5, [P, KV, CB], F32R)
    v_hl["cmp"] = sb("v_hl_cmp", 203, [P, 1, KV, 2 * HEAD_DIM], F32R)
    gate = sb("gate", 204, [P, QB, BRANCHES * HEADS])
    wb_lo = sb("wb_lo", 202, [P, KT, P], F32R)

    ps = ctx.enter_context(nc.psum_tensor("ps", [P, 8, HALF], F32))

    def wide(bank):
        return ps[:, bank:bank + 2, :].rearrange("p a b -> p (a b)")

    def tiles(bank):
        return ps[:, bank:bank + 2, :].rearrange("p a (b c) -> p (a b) c", c=P)

    SCORES, TURN, OUTS = (0, 2), (4, 5), (6, 7)
    HIDDEN_BANK, SMALL_BANK = 6, 7
    Y_A, Y_B = 4, 6

    const_ready = sem("const_ready")
    masks_ready = sem("masks_ready")
    pool_step = sem("pool_step")
    small_in = sem("small_in")
    sinks_in = sem("sinks_in")
    cmp_w_in = sem("cmp_w_in")
    x_in = [sem(f"x_in{i}") for i in range(2)]
    x_turned = [sem(f"x_turned{i}") for i in range(2)]
    xh_ready = [sem(f"xh_ready{i}") for i in range(2)]
    xl_ready = [sem(f"xl_ready{i}") for i in range(2)]
    w_loaded = [sem(f"w_loaded{i}") for i in range(2)]
    w_hi_ready = [sem(f"w_hi_ready{i}") for i in range(2)]
    w_lo_ready = [sem(f"w_lo_ready{i}") for i in range(2)]
    product_done = [sem(f"product_done{i}") for i in range(2)]
    product_taken = [sem(f"product_taken{i}") for i in range(2)]
    pos_turned = sem("pos_turned")
    pos_ready = sem("pos_ready")
    kc_ready = sem("kc_ready")
    vc_ready = sem("vc_ready")
    cx_ready = sem("cx_ready")
    hidden_done = sem("hidden_done")
    hidden_copied = sem("hidden_copied")
    tanh_done = sem("tanh_done")
    gelu_step = sem("gelu_step")
    gelu_ready = sem("gelu_ready")
    cmp_done = sem("cmp_done")
    cmp_hi_ready = sem("cmp_hi_ready")
    cmp_lo_ready = sem("cmp_lo_ready")
    kv_hi_ready = sem("kv_hi_ready")
    kv_lo_ready = sem("kv_lo_ready")
    v_turned = sem("v_turned")
    v_hi_ready = sem("v_hi_ready")
    v_lo_ready = sem("v_lo_ready")
    gate_ready = sem("gate_ready")
    gate_fixed = sem("gate_fixed")
    consts_done = sem("consts_done")
    q_hi_ready = sem("q_hi_ready")
    q_lo_ready = sem("q_lo_ready")
    scores_done = sem("scores_done")
    row_max = sem("row_max")
    shift_ready = sem("shift_ready")
    exp_done = sem("exp_done")
    sink_exp = sem("sink_exp")
    scale_step = sem("scale_step")
    probs_ready = sem("probs_ready")
    probs_turned = sem("probs_turned")
    pt_hi_ready = sem("pt_hi_ready")
    pt_lo_ready = sem("pt_lo_ready")
    values_done = sem("values_done")
    o_low_ready = sem("o_low_ready")
    o_ready = sem("o_ready")
    o_split_hi = sem("o_split_hi")
    o_split_lo = sem("o_split_lo")
    wb_loaded = sem("wb_loaded")
    wb_hi_ready = sem("wb_hi_ready")
    wb_lo_ready = sem("wb_lo_ready")
    sg_ready = [sem(f"sg_ready{i}") for i in range(2)]
    y_done = [sem(f"y_done{i}") for i in range(2)]
    gated = sem("gated")
    merged_ready = sem("merged_ready")
    row_loaded = [sem(f"row_loaded{i}") for i in range(2)]
    row_hi_ready = [sem(f"row_hi_ready{i}") for i in range(2)]
    row_lo_ready = [sem(f"row_lo_ready{i}") for i in range(2)]
    mst_hi_ready = [sem(f"mst_hi_ready{i}") for i in range(2)]
    mst_lo_ready = [sem(f"mst_lo_ready{i}") for i in range(2)]
    mix_done = [sem(f"mix_done{i}") for i in range(2)]
    xres_in = [sem(f"xres_in{i}") for i in range(2)]
    z_ready = [sem(f"z_ready{i}") for i in range(2)]
    ln_step = sem("ln_step")
    var_ready = sem("var_ready")
    std_ready = sem("std_ready")
    normed = sem("normed")
    ln_scaled = sem("ln_scaled")
    ln_done = sem("ln_done")
    ln_in = sem("ln_in")
    h_turned = sem("h_turned")
    hh_ready = sem("hh_ready")
    hl_ready = sem("hl_ready")
    residual_ready = sem("residual_ready")
    relu_ready = [sem(f"relu_ready{i}") for i in range(2)]
    usq_ready = [sem(f"usq_ready{i}") for i in range(2)]
    uh_ready = [sem(f"uh_ready{i}") for i in range(2)]
    ul_ready = [sem(f"ul_ready{i}") for i in range(2)]
    down_done = sem("down_done")
    down_added = sem("down_added")
    stored = sem("stored")

    units, STEPS, SEGS, BLOCKS = attention_units()
    last_unit_of = {}
    for u in units:
        u["buffer"] = {"swa": f"swa{u['step'] % 2}", "slc": "slc", "wc": "wc"}[u["kind"]]
        shares = {"slc": ("slc",), "wc": ("wc", "swa0", "swa1")}.get(u["kind"], (u["buffer"],))
        before = [last_unit_of[b] for b in shares if b in last_unit_of]
        u["buffer_free"] = max((b["block0"] + len(b["blocks"]) for b in before), default=0)
        last_unit_of[u["buffer"]] = u

    parts_of = [sum(len(u["parts"]) for u in units if u["step"] <= step) for step in range(STEPS)]
    q_free = [0, 0] + parts_of[:STEPS - 2]

    part_end = [p[-1]["number"] + 1 for u in units for p in u["parts"]]

    def probs(u):
        return {"swa": p_swa[u["step"] % 2], "slc": p_slc, "wc": p_wc}[u["kind"]]

    def slope(u, s):
        return float(SLOPES[(0 if u["kind"] == "swa" else HEADS) + R * u["g"] + s["r"]])

    def table(u, s):
        if s["what"] == "cmp":
            return t_cmp[:, u["qb"], :]
        t = {"slc": t_slc, "win": t_win, "swa": t_swa}[s["what"]]
        return t[:, s["table0"]:s["table0"] + s["keys"]]

    def heads_out(u):
        return qb_ if u["kind"] == "swa" else qa

    N_BEFORE_MERGE = 17
    W_COLS = {0: COL_KC, 1: COL_VC, 10: COL_KS, 11: COL_VS, 12: COL_KW, 13: COL_VW, 14: COL_KB, 15: COL_VB,
              16: COL_GA}
    GATE_USE = (9, 8)
    UP_USE = (GATE_USE[0] + KT, GATE_USE[1] + KT)
    ROW_OUT = KT // 2

    def columns(w, col):
        return w[0, :, bass.ds(col, P)].rearrange("(k p) c -> p k c", p=P)

    block = ctx.enter_context(nc.Block())

    @block.sync
    def _(sp):
        def load_x(n, slot, tile, loaded, used):
            at_least(sp, used[slot], n)
            sp.dma_start(x_raw[slot][:, :], x[0, bass.ds(tile * P, P), :]).then_inc(loaded[slot], 16)

        def load_w(slot, n, src):
            at_least(sp, w_lo_ready[slot], n)
            sp.dma_start(w_raw[slot][:, :, :], src).then_inc(w_loaded[slot], 16)

        def load_row(slot, n, src):
            at_least(sp, row_lo_ready[slot], n)
            sp.dma_start(row_raw[slot][:, :], src).then_inc(row_loaded[slot], 16)

        load_x(0, 0, 0, x_in, x_turned)
        load_x(0, 1, 1, x_in, x_turned)
        sp.dma_start(pos_nat[0:CT, :], pos_k[0].rearrange("(t l) d -> t (l d)", l=2)).then_inc(small_in, 16)
        sp.dma_start(pos_nat[CT:2 * CT, :], pos_v[0].rearrange("(t l) d -> t (l d)", l=2)).then_inc(small_in, 16)
        load_w(0, 0, columns(w_in, W_COLS[0]))
        load_w(1, 0, columns(w_in, W_COLS[1]))
        with sp.Fori(1, QB // 2) as i:
            for slot in range(2):
                load_x(i, slot, i * 2 + slot, x_in, x_turned)
        for kind, w1 in enumerate((w1_k, w1_v)):
            sp.dma_start(cw1[kind][:, :, :], w1[0].rearrange("(t l) d f -> (l d) t f", l=2)).then_inc(cmp_w_in, 16)
        for copy in range(2):
            sp.dma_start(cw2k[:, :, copy, :], w2_k[0].rearrange("(a f) d -> f a d", f=P)).then_inc(cmp_w_in, 16)
        sp.dma_start(cw2v[:, :, :], w2_v[0].rearrange("(a f) d -> f a d", f=P)).then_inc(cmp_w_in, 16)
        sp.dma_start(sink_row[:, :], sinks[0].partition_broadcast(P)).then_inc(sinks_in, 16)
        with sp.Fori(0, 4) as j:
            load_w(0, j + 1, columns(w_in, j * P + COL_QA))
            load_w(1, j + 1, columns(w_in, j * P + COL_QB))
        for b in range(10, N_BEFORE_MERGE):
            load_w(b % 2, b // 2, columns(w_in, W_COLS[b]))
        sp.wait_ge(v_turned, 4)
        uses = QB // 2
        load_x(uses, 0, 0, x_in, x_turned)
        load_x(uses, 1, 1, x_in, x_turned)
        load_w(1, GATE_USE[1], columns(w_in, COL_GATE_B))
        load_w(0, GATE_USE[0], columns(w_in, COL_GATE_A))
        with sp.Fori(1, QB // 2) as i:
            for slot in range(2):
                load_x(i + uses, slot, i * 2 + slot, x_in, x_turned)

        def load_branches(j):
            for half, w in enumerate((w_branch_a, w_branch_b)):
                sp.dma_start(wb_raw[:, 4 * half:4 * half + 4, :], columns(w, j * P)).then_inc(wb_loaded, 16)

        sp.wait_ge(x_turned[0], 2 * uses)
        sp.wait_ge(x_turned[1], 2 * uses)
        load_branches(0)
        for j in range(1, KT):
            sp.wait_ge(wb_lo_ready, j)
            load_w(0, j + GATE_USE[0], columns(w_in, j * P + COL_GATE_A))
            load_w(1, j + GATE_USE[1], columns(w_in, j * P + COL_GATE_B))
            load_branches(j)
        load_w(0, UP_USE[0], columns(w_up, 0))
        load_w(1, UP_USE[1], columns(w_up, P))
        sp.wait_ge(merged_ready, KT)
        sp.wait_ge(y_done[1], KT)
        load_row(0, 0, w_out[0, 0:P, :])
        load_row(1, 0, w_out[0, P:2 * P, :])
        load_x(0, 0, 0, xres_in, z_ready)
        load_x(0, 1, 1, xres_in, z_ready)
        with sp.Fori(1, KT // 2) as i:
            for slot in range(2):
                load_row(slot, i, w_out[0, bass.ds((i * 2 + slot) * P, P), :])
        sp.dma_start(ln_g[:, :], ln1_g[0].partition_broadcast(P)).then_inc(ln_in, 16)
        sp.dma_start(ln_b[:, :], ln1_b[0].partition_broadcast(P)).then_inc(ln_in, 16)
        with sp.Fori(1, QB // 2) as i:
            for slot in range(2):
                load_x(i, slot, i * 2 + slot, xres_in, z_ready)
        for slot in range(CHUNK):
            load_row(slot, ROW_OUT, w_down[0, slot * P:(slot + 1) * P, :])
        for slot in range(CHUNK):
            load_w(slot, UP_USE[slot] + 1, columns(w_up, (CHUNK + slot) * P))
        sp.wait_ge(ln_done, QB)
        sp.dma_start(ln_g[:, :], ln2_g[0].partition_broadcast(P)).then_inc(ln_in, 16)
        sp.dma_start(ln_b[:, :], ln2_b[0].partition_broadcast(P)).then_inc(ln_in, 16)
        with sp.Fori(0, CHUNKS - 2) as c:
            for slot in range(CHUNK):
                load_w(slot, c + (UP_USE[slot] + 2), columns(w_up, (c * CHUNK + (2 * CHUNK + slot)) * P))
            for slot in range(CHUNK):
                load_row(slot, c + (ROW_OUT + 1), w_down[0, bass.ds((c * CHUNK + (CHUNK + slot)) * P, P), :])
        for slot in range(CHUNK):
            load_row(slot, ROW_OUT + CHUNKS - 1, w_down[0, ((CHUNKS - 1) * CHUNK + slot) * P:((CHUNKS - 1) * CHUNK + slot + 1) * P, :])
        for t in range(QB):
            sp.wait_ge(ln_done, QB + t + 1)
            sp.dma_start(out[0, t * P:(t + 1) * P, :], acc[:, t, :]).then_inc(stored, 16)
        sp.wait_ge(stored, 16 * QB)

    @block.gpsimd
    def _(pool):
        pool.memset(ident[:, :], 0.0).then_inc(pool_step, 1)
        pool.wait_ge(pool_step, 1)
        pool.affine_select(out=ident[:, :], in_=ident[:, :], pattern=[[-1, P]], compare_op=ALU.not_equal,
                           fill=1.0, base=0, channel_multiplier=1).then_inc(const_ready, 1)
        pool.memset(eps[:, :], LN_EPS).then_inc(const_ready, 1)
        pool.memset(seen[:, :], 1.0).then_inc(pool_step, 1)
        for i, s in enumerate(SLOPES):
            pool.memset(slope_inv[:, i:i + 1], 1.0 / s).then_inc(const_ready, 1)
        for kind in range(2):
            pool.memset(cx[kind][:, :, :, CB - 1:CB], 0.0).then_inc(pool_step, 1)
        pool.wait_ge(pool_step, 2)
        pool.affine_select(out=seen[:, :], in_=seen[:, :], pattern=[[0, 1]], compare_op=ALU.is_ge,
                           fill=0.0, base=-(CMP_LEN - 1), channel_multiplier=1).then_inc(const_ready, 1)

        pool.wait_ge(pos_ready, 1)
        pool.wait_ge(kc_ready, 3)
        pool.wait_ge(product_taken[0], 1)
        pool.wait_ge(vc_ready, 3)
        pool.wait_ge(product_taken[1], 1)
        for kind in range(2):
            for g in range(KV):
                seq = kcs[2 * kind + g][:, :].rearrange("p (c t two) -> p two t c", t=CT // 2, two=2)
                for late in range(2):
                    rows = slice(late * CT // 2, (late + 1) * CT // 2)
                    pos = posT[:, kind * CT + late * CT // 2:kind * CT + (late + 1) * CT // 2]
                    pool.tensor_tensor(cx[kind][:, rows, g, 0:CB - 1], seq[:, 0, :, late:late + CB - 1],
                                       pos.unsqueeze(2).to_broadcast([P, CT // 2, CB - 1]),
                                       ALU.add).then_inc(cx_ready, 1)

        pool.wait_ge(product_done[0], GATE_USE[0])
        pool.iota(t_swa[:, :], [[1, 2 * P]], base=-P, channel_multiplier=-1,
                  allow_small_or_imprecise_dtypes=True).then_inc(masks_ready, 1)
        pool.iota(t_slc[:, :], [[1, SEQ + P]], base=-SEQ, channel_multiplier=-1,
                  allow_small_or_imprecise_dtypes=True).then_inc(masks_ready, 1)
        pool.iota(t_win[:, :], [[1, NSA_WINDOW + P]], base=-NSA_WINDOW, channel_multiplier=-1,
                  allow_small_or_imprecise_dtypes=True).then_inc(masks_ready, 1)
        pool.memset(t_cmp[:, :, :], 0.0).then_inc(masks_ready, 1)
        pool.wait_ge(masks_ready, 4)
        for t, width, back in ((t_swa, 2 * P, P), (t_slc, SEQ + P, SEQ), (t_win, NSA_WINDOW + P, NSA_WINDOW)):
            pool.affine_select(out=t[:, :], in_=t[:, :], pattern=[[-1, width]], compare_op=ALU.is_ge,
                               fill=MASKED, base=back, channel_multiplier=1).then_inc(masks_ready, 1)
        pool.affine_select(out=t_cmp[:, :, :], in_=t_cmp[:, :, :], pattern=[[P, QB], [-CMP_STRIDE, CB]],
                           compare_op=ALU.is_ge, fill=MASKED, base=-(CMP_LEN - 1),
                           channel_multiplier=1).then_inc(masks_ready, 1)
        pool.wait_ge(masks_ready, 8)
        for t, width in ((t_swa, 2 * P), (t_win, NSA_WINDOW + P)):
            pool.affine_select(out=t[:, :], in_=t[:, :], pattern=[[1, width]], compare_op=ALU.is_gt,
                               fill=MASKED, base=0, channel_multiplier=-1).then_inc(masks_ready, 1)

        for j in range(KT):
            pool.wait_ge(gated, j * 2 + 2)
            pool.tensor_tensor(merged[:, j, :], sg_a[:, :], sg_b[:, :], ALU.add).then_inc(merged_ready, 1)

        def norm_affine(t, count, done):
            pool.wait_ge(normed, count + 1)
            pool.tensor_tensor(acc[:, t, :], acc[:, t, :], ln_g[:, :], ALU.mult).then_inc(ln_scaled, 1)
            pool.wait_ge(ln_scaled, count + 1)
            pool.tensor_tensor(acc[:, t, :], acc[:, t, :], ln_b[:, :], ALU.add).then_inc(ln_done, 1)

        pool.wait_ge(ln_in, 32)
        for t in range(QB):
            norm_affine(t, t, ln_done)
        for t in range(QB):
            pool.wait_ge(h_turned, t + 1)
            pool.tensor_scalar(acc[:, t, :], acc[:, t, :], ALPHA, 1.0, ALU.mult, ALU.mult).then_inc(residual_ready, 1)

        with pool.Fori(0, CHUNKS) as c:
            for slot in range(CHUNK):
                pool.wait_ge(relu_ready[slot], c + 1)
                pool.wait_ge(ul_ready[slot], c + 1)
                pool.tensor_tensor(usq[slot][:, :], relu[slot][:, :], relu[slot][:, :],
                                   ALU.mult).then_inc(usq_ready[slot], 1)
        pool.wait_ge(ln_in, 64)
        for t in range(QB):
            norm_affine(t, t + QB, ln_done)

    @block.scalar
    def _(act):
        def split_x(n, slot, tile):
            act.wait_ge(x_turned[slot], n + 1)
            act.activation(xh[:, :, bass.ds(tile * P, P)], tiles(4 + 2 * slot), ACT.Copy).then_inc(xh_ready[slot], 1)

        def split_w(slot, n):
            act.wait_ge(w_loaded[slot], (n + 1) * 16)
            at_least(act, product_done[slot], n)
            act.activation(w_hi[slot][:, :, :], w_raw[slot][:, :, :], ACT.Copy).then_inc(w_hi_ready[slot], 1)

        split_x(0, 0, 0)
        split_x(0, 1, 1)
        with act.Fori(1, QB // 2) as i:
            for slot in range(2):
                split_x(i, slot, i * 2 + slot)
        split_w(0, 0)
        split_w(1, 0)
        split_w(0, 1)
        act.wait_ge(product_done[0], 1)
        for g in range(KV):
            rows = slice(g * HEAD_DIM, (g + 1) * HEAD_DIM)
            act.activation(kcs[g][0:HEAD_DIM, :], wide(0)[rows, :], ACT.Copy).then_inc(kc_ready, 1)
            act.activation(kcs[g][HEAD_DIM:P, 0:SEQ - 1], wide(0)[rows, 1:SEQ],
                           ACT.Copy).then_inc(kc_ready if g == 0 else product_taken[0], 1)
        with act.Fori(0, 4) as j:
            split_w(1, j + 1)
            act.wait_ge(product_done[0], j + 2)
            act.activation(qa[:, j, :], wide(0), ACT.Copy).then_inc(product_taken[0], 1)
            split_w(0, j + 2)
        act.wait_ge(hidden_done, 1)
        act.activation(g_in[:, :], ps[:, HIDDEN_BANK, :], ACT.Copy).then_inc(hidden_copied, 1)
        act.wait_ge(gelu_step, 3)
        act.activation(g_u[:, :], g_t[:, :], ACT.Tanh, scale=float(GELU_IN)).then_inc(tanh_done, 1)

        def keys_high(what, slot, n):
            act.wait_ge(product_done[slot], n + 1)
            for g in range(KV):
                rows = slice(g * HEAD_DIM, (g + 1) * HEAD_DIM)
                for to in range(2):
                    act.activation(k_hi[what][to * HEAD_DIM:(to + 1) * HEAD_DIM, g, :], wide(2 * slot)[rows, :],
                                   ACT.Copy).then_inc(kv_hi_ready, 1)

        def values_high(what, i):
            act.wait_ge(v_turned, i + 1)
            for g in range(KV):
                act.activation(v_hl[what][:, :, g, 0:HEAD_DIM], tiles(4)[:, :, g * HEAD_DIM:(g + 1) * HEAD_DIM],
                               ACT.Copy).then_inc(v_hi_ready, 1)

        def values_out(dst, slot, n):
            act.wait_ge(product_done[slot], n + 1)
            act.activation(dst[:, :], wide(2 * slot), ACT.Copy).then_inc(product_taken[slot], 1)

        split_w(1, 5)
        keys_high("slc", 0, 5)
        split_w(0, 6)
        act.wait_ge(cmp_done, 1)
        act.activation(k_hi["cmp"][:, :, :], ps[:, SMALL_BANK, 0:P].rearrange("p (g c) -> p g c", g=KV),
                       ACT.Copy).then_inc(cmp_hi_ready, 1)
        act.activation(v_hl["cmp"][0:CB, 0, :, 0:HEAD_DIM],
                       ps[0:CB, SMALL_BANK, P:2 * P].rearrange("p (g d) -> p g d", g=KV),
                       ACT.Copy).then_inc(cmp_hi_ready, 1)
        values_out(vT, 1, 5)
        split_w(1, 6)
        keys_high("win", 0, 6)
        values_high("slc", 0)
        split_w(0, 7)
        values_out(vT, 1, 6)
        split_w(1, 7)
        keys_high("swa", 0, 7)
        values_high("win", 1)
        split_w(0, 8)
        values_out(vT, 1, 7)
        values_out(gaT, 0, 8)
        values_high("swa", 2)
        act.wait_ge(v_turned, 4)
        act.activation(gate[:, :, :], tiles(4)[:, :, 0:BRANCHES * HEADS], ACT.Sigmoid).then_inc(gate_ready, 1)

        def stage_queries(u):
            step = u["step"]
            at_least(act, scores_done, q_free[step])
            for r in range(R):
                rows = slice((r % 2) * HEAD_DIM, (r % 2 + 1) * HEAD_DIM)
                act.activation(q_st[step % 2][rows, r, :],
                               heads_out(u)[rows, 2 * u["g"] + r // 2, u["qb"] * P:(u["qb"] + 1) * P],
                               ACT.Copy, scale=float(np.float32(HEAD_DIM ** -0.5 / slope(u, {"r": r})))).then_inc(q_hi_ready, 1)

        def exps(u, part):
            p = probs(u)
            for s in u["parts"][part]:
                n = u["number"] % 2
                c = s["column"]
                act.wait_ge(shift_ready, s["number"] + 1)
                row = p[:, s["r"], s["at"]:s["at"] + s["keys"]]
                act.activation(row, row, ACT.Exp, scale=slope(u, s), bias=m_neg[:, n, c:c + 1],
                               accum_out=row_l[:, n, c:c + 1]).then_inc(exp_done, 1)
            if u["kind"] == "swa":
                for s in u["parts"][part]:
                    n, c = u["number"] % 2, s["column"]
                    h = R * u["g"] + s["r"]
                    act.activation(sink_e[:, n, c:c + 1], sink_row[:, h:h + 1], ACT.Exp,
                                   bias=m_neg[:, n, c:c + 1]).then_inc(sink_exp, 1)

        def turned_high(u, i):
            t = u["block0"] + i
            rows = CB if u["blocks"][i][0] == "cmp" else P
            act.wait_ge(probs_turned, t + 1)
            at_least(act, values_done, t - 2)
            act.activation(pt_hi[t % 3][0:rows, :, :], ps[0:rows, TURN[t % 2], :].rearrange("p (r q) -> p r q", r=R),
                           ACT.Copy).then_inc(pt_hi_ready, 1)

        def outputs_low(u):
            act.wait_ge(values_done, u["block0"] + len(u["blocks"]))
            at_least(act, o_ready, 2 * u["step"])
            act.activation(o_sum[0:HEAD_DIM, :, :],
                           ps[HEAD_DIM:P, OUTS[u["step"] % 2], :].rearrange("p (r q) -> p r q", r=R),
                           ACT.Copy).then_inc(o_low_ready, 1)

        act.wait_ge(product_done[0], GATE_USE[0])
        act.wait_ge(sinks_in, 16)
        stage_queries(units[0])
        exps(units[0], 0)
        for k, u in enumerate(units):
            after = units[k + 1] if k + 1 < len(units) else None
            if after and after["first_of_step"]:
                stage_queries(after)
            for what, i in interleave(u["blocks"], after["parts"] if after else []):
                if what == "part":
                    exps(after, i)
                else:
                    turned_high(u, i)
            if u["last_of_step"]:
                outputs_low(u)

        act.wait_ge(o_ready, 2 * STEPS)
        for tile in range(2):
            split_x(QB // 2, tile, tile)
        with act.Fori(1, QB // 2) as i:
            for slot in range(2):
                split_x(i + QB // 2, slot, i * 2 + slot)
        act.activation(oah[:, :, :], qa[:, :, :], ACT.Copy).then_inc(o_split_hi, 1)
        act.activation(obh[:, :, :], qb_[:, :, :], ACT.Copy).then_inc(o_split_hi, 1)
        split_w(0, GATE_USE[0])

        def merge(j):
            split_w(1, j + GATE_USE[1])
            act.wait_ge(wb_loaded, j * 32 + 32)
            at_least(act, y_done[1], j)
            act.activation(wb_hi[:, :, :], wb_raw[:, :, :], ACT.Copy).then_inc(wb_hi_ready, 1)
            for slot, sg, use in ((0, sg_a, j + GATE_USE[0]), (1, sg_b, j + GATE_USE[1])):
                act.wait_ge(product_done[slot], use + 1)
                at_least(act, merged_ready, j)
                act.activation(sg[:, :], wide(2 * slot), ACT.Sigmoid).then_inc(sg_ready[slot], 1)
                if slot == 0:
                    split_w(0, j + (GATE_USE[0] + 1))

        merge(0)
        with act.Fori(1, KT) as j:
            merge(j)

        def split_row(slot, n, hi):
            act.wait_ge(row_loaded[slot], (n + 1) * 16)
            act.activation(hi, row_raw[slot][:, :], ACT.Copy).then_inc(row_hi_ready[slot], 1)

        def stage_merged(slot, n, tile):
            at_least(act, mix_done[slot], n)
            act.activation(mst_hi[slot][:, :, :], merged[:, :, bass.ds(tile * P, P)],
                           ACT.Copy).then_inc(mst_hi_ready[slot], 1)

        def deviation(slot, count):
            act.wait_ge(var_ready, count + 1)
            act.activation(rstd[:, slot, 0:1], mv[:, slot, 1:2], ACT.Sqrt, bias=eps[:, :]).then_inc(std_ready, 1)

        act.wait_ge(merged_ready, KT)
        act.wait_ge(y_done[1], KT)
        stage_merged(0, 0, 0)
        for kt in range(KT):
            split_row(kt % 2, kt // 2, wo_hi[:, kt, :])
        stage_merged(1, 0, 1)
        with act.Fori(0, QB // 2 - 1) as i:
            for slot in range(2):
                deviation(slot, i * 2 + slot)
                stage_merged(slot, i + 1, (i + 1) * 2 + slot)
        for slot in range(2):
            deviation(slot, QB - 2 + slot)
        split_w(1, UP_USE[1])
        act.wait_ge(mix_done[1], QB // 2)
        for t in range(QB):
            act.wait_ge(h_turned, t + 1)
            act.activation(hh[:, :, t * P:(t + 1) * P], tiles(4 + 2 * (t % 2)), ACT.Copy).then_inc(hh_ready, 1)

        def relu_out(slot, c):
            act.wait_ge(product_done[slot], c + (UP_USE[slot] + 1))
            at_least(act, usq_ready[slot], c)
            act.activation(relu[slot][:, :], wide(2 * slot), ACT.Relu).then_inc(relu_ready[slot], 1)

        def hidden_high(slot, c, parity):
            act.wait_ge(usq_ready[slot], c + 1)
            at_least(act, down_done, (c - 1) * 16)
            act.activation(uh[parity][:, slot, :], usq[slot][:, :], ACT.Copy).then_inc(uh_ready[slot], 1)

        def down_weights(c):
            for slot in range(CHUNK):
                act.wait_ge(row_loaded[slot], (c + (ROW_OUT + 1)) * 16)
                at_least(act, down_done, c * 16)
                act.activation(wd_hi[slot][:, :], row_raw[slot][:, :], ACT.Copy).then_inc(row_hi_ready[slot], 1)

        def mlp_step(c, parity, ups, splits):
            down_weights(c)
            if ups:
                for slot in range(CHUNK):
                    if splits:
                        split_w(slot, c + (UP_USE[slot] + 2))
                    relu_out(slot, c + 1)
                for slot in range(CHUNK):
                    hidden_high(slot, c + 1, 1 - parity)

        for slot in range(CHUNK):
            split_w(slot, UP_USE[slot] + 1)
            relu_out(slot, 0)
        for slot in range(CHUNK):
            hidden_high(slot, 0, 0)
        mlp_step(0, 0, True, True)
        mlp_step(1, 1, True, True)
        with act.Fori(1, CHUNKS // 2 - 1) as i:
            mlp_step(i * 2, 0, True, True)
            mlp_step(i * 2 + 1, 1, True, True)
        mlp_step(CHUNKS - 2, 0, True, False)
        mlp_step(CHUNKS - 1, 1, False, False)
        for t in range(QB):
            deviation(t % 2, QB + t)

    @block.vector
    def _(dve):
        def split_x(n, slot, tile):
            dve.wait_ge(xh_ready[slot], n + 1)
            cols = bass.ds(tile * P, P)
            dve.tensor_tensor(xl[:, :, cols], tiles(4 + 2 * slot), xh[:, :, cols],
                              ALU.subtract).then_inc(xl_ready[slot], 1)

        def split_w(slot, n):
            dve.wait_ge(w_hi_ready[slot], n + 1)
            dve.tensor_tensor(w_lo[slot][:, :, :], w_raw[slot][:, :, :], w_hi[slot][:, :, :],
                              ALU.subtract).then_inc(w_lo_ready[slot], 1)

        dve.wait_ge(pos_turned, 1)
        dve.tensor_copy(posT[:, :], ps[:, SMALL_BANK, 0:2 * CT]).then_inc(pos_ready, 1)
        split_x(0, 0, 0)
        split_x(0, 1, 1)
        with dve.Fori(1, QB // 2) as i:
            for slot in range(2):
                split_x(i, slot, i * 2 + slot)
        split_w(0, 0)
        split_w(1, 0)
        split_w(0, 1)
        dve.wait_ge(product_done[1], 1)
        for g in range(KV):
            rows = slice(g * HEAD_DIM, (g + 1) * HEAD_DIM)
            dve.tensor_copy(kcs[KV + g][0:HEAD_DIM, :], wide(2)[rows, :]).then_inc(vc_ready, 1)
            dve.tensor_copy(kcs[KV + g][HEAD_DIM:P, 0:SEQ - 1],
                            wide(2)[rows, 1:SEQ]).then_inc(vc_ready if g == 0 else product_taken[1], 1)
        with dve.Fori(0, 4) as j:
            split_w(1, j + 1)
            dve.wait_ge(product_done[1], j + 2)
            dve.tensor_copy(qb_[:, j, :], wide(2)).then_inc(product_taken[1], 1)
            split_w(0, j + 2)
        dve.wait_ge(hidden_copied, 1)
        dve.tensor_tensor(g_t[:, :], g_in[:, :], g_in[:, :], ALU.mult).then_inc(gelu_step, 1)
        dve.wait_ge(gelu_step, 1)
        dve.tensor_scalar(g_t[:, :], g_t[:, :], 0.044715, 1.0, ALU.mult, ALU.add).then_inc(gelu_step, 1)
        dve.wait_ge(gelu_step, 2)
        dve.tensor_tensor(g_t[:, :], g_t[:, :], g_in[:, :], ALU.mult).then_inc(gelu_step, 1)
        dve.wait_ge(tanh_done, 1)
        dve.tensor_scalar(g_u[:, :], g_u[:, :], 1.0, 0.5, ALU.add, ALU.mult).then_inc(gelu_step, 1)
        dve.wait_ge(gelu_step, 4)
        dve.tensor_tensor(g_out[:, :, :, :, :].rearrange("p a b g c -> p (a b g c)"), g_u[:, :], g_in[:, :],
                          ALU.mult).then_inc(gelu_ready, 1)

        def keys_low(what, slot, number):
            dve.wait_ge(kv_hi_ready, 4 * number + 4)
            for g in range(KV):
                rows = slice(g * HEAD_DIM, (g + 1) * HEAD_DIM)
                for to in range(2):
                    last = dve.tensor_tensor(k_lo[what][to * HEAD_DIM:(to + 1) * HEAD_DIM, g, :], wide(2 * slot)[rows, :],
                                             k_hi[what][rows, g, :], ALU.subtract)
                    last.then_inc(product_taken[slot] if g and to else kv_lo_ready, 1)

        def values_low(what, number):
            dve.wait_ge(v_hi_ready, 2 * number + 2)
            for g in range(KV):
                dve.tensor_tensor(v_hl[what][:, :, g, HEAD_DIM:P], tiles(4)[:, :, g * HEAD_DIM:(g + 1) * HEAD_DIM],
                                  v_hl[what][:, :, g, 0:HEAD_DIM], ALU.subtract).then_inc(v_lo_ready, 1)

        split_w(1, 5)
        keys_low("slc", 0, 0)
        split_w(0, 6)
        dve.wait_ge(cmp_hi_ready, 2)
        dve.tensor_tensor(k_lo["cmp"][:, :, :], ps[:, SMALL_BANK, 0:P].rearrange("p (g c) -> p g c", g=KV),
                          k_hi["cmp"][:, :, :], ALU.subtract).then_inc(cmp_lo_ready, 1)
        dve.tensor_tensor(v_hl["cmp"][0:CB, 0, :, HEAD_DIM:P],
                          ps[0:CB, SMALL_BANK, P:2 * P].rearrange("p (g d) -> p g d", g=KV),
                          v_hl["cmp"][0:CB, 0, :, 0:HEAD_DIM], ALU.subtract).then_inc(cmp_lo_ready, 1)
        split_w(1, 6)
        keys_low("win", 0, 1)
        values_low("slc", 0)
        split_w(0, 7)
        split_w(1, 7)
        keys_low("swa", 0, 2)
        values_low("win", 1)
        split_w(0, 8)
        values_low("swa", 2)
        dve.wait_ge(const_ready, 19)
        dve.wait_ge(sinks_in, 16)
        dve.tensor_tensor(sink_y[:, :], sink_row[:, :], slope_inv[:, 0:HEADS], ALU.mult).then_inc(consts_done, 1)
        dve.wait_ge(gate_ready, 1)
        cmp_gates = gate[:, 0, :].rearrange("p (h b) -> p h b", b=BRANCHES)[:, :, 0]
        dve.tensor_scalar(cmp_gates, cmp_gates, seen[:, :], None, ALU.mult).then_inc(consts_done, 1)
        dve.wait_ge(consts_done, 2)

        def stage_queries(u):
            step = u["step"]
            for r in range(R):
                rows = slice((r % 2) * HEAD_DIM, (r % 2 + 1) * HEAD_DIM)
                other = slice((1 - r % 2) * HEAD_DIM, (2 - r % 2) * HEAD_DIM)
                dve.wait_ge(q_hi_ready, R * step + r + 1)
                dve.scalar_tensor_tensor(
                    out=q_st[step % 2][other, r, :],
                    in0=heads_out(u)[rows, 2 * u["g"] + r // 2, u["qb"] * P:(u["qb"] + 1) * P],
                    scalar=float(np.float32(HEAD_DIM ** -0.5 / slope(u, {"r": r}))), in1=q_st[step % 2][rows, r, :],
                    op0=ALU.mult, op1=ALU.subtract).then_inc(q_lo_ready, 1)

        def maxima(u, part):
            p = probs(u)
            n = u["number"] % 2
            at_least(dve, probs_turned, u["buffer_free"])
            dve.wait_ge(scores_done, u["part0"] + part + 1)
            slot = SCORES[(u["part0"] + part) % 2]
            segs = u["parts"][part]
            for s in segs:
                c = s["column"]
                start = sink_y[:, R * u["g"] + s["r"]:R * u["g"] + s["r"] + 1] if u["kind"] == "swa" else -3e38
                dve.tensor_tensor_reduce(out=p[:, s["r"], s["at"]:s["at"] + s["keys"]],
                                         in0=wide(slot)[:, s["score0"]:s["score0"] + s["keys"]],
                                         in1=table(u, s), scale=1.0, scalar=start, op0=ALU.add, op1=ALU.max,
                                         accum_out=m_y[:, n, c:c + 1]).then_inc(row_max, 1)
            for s in segs:
                c = s["column"]
                dve.wait_ge(row_max, s["number"] + 1)
                dve.tensor_scalar(m_neg[:, n, c:c + 1], m_y[:, n, c:c + 1], -slope(u, s), None,
                                  ALU.mult).then_inc(shift_ready, 1)

        def scales(u):
            n = u["number"] % 2
            count = len(u["segs"])
            dve.wait_ge(exp_done, u["seg0"] + count)
            total = row_l[:, n, 0:count]
            if u["kind"] == "swa":
                dve.wait_ge(sink_exp, R * (u["step"] + 1))
                dve.tensor_tensor(total, total, sink_e[:, n, 0:count], ALU.add).then_inc(scale_step, 1)
                S[0] += 1
                dve.wait_ge(scale_step, S[0])
            dve.reciprocal(row_s[:, n, 0:count], total).then_inc(scale_step, 1)
            S[0] += 1
            dve.wait_ge(scale_step, S[0])
            if u["kind"] != "swa":
                gates = gate[:, u["qb"], R * BRANCHES * u["g"]:R * BRANCHES * (u["g"] + 1)]
                gates = gates.rearrange("p (r b) -> p r b", b=BRANCHES)
                if u["kind"] == "slc":
                    dve.tensor_tensor(row_s[:, n, 0:R], row_s[:, n, 0:R], gates[:, :, 1],
                                      ALU.mult).then_inc(scale_step, 1)
                    S[0] += 1
                else:
                    pairs = row_s[:, n, 0:2 * R].rearrange("p (r b) -> p r b", b=2)
                    for b, branch in ((0, 2), (1, 0)):
                        dve.tensor_tensor(pairs[:, :, b], pairs[:, :, b], gates[:, :, branch],
                                          ALU.mult).then_inc(scale_step, 1)
                        S[0] += 1
                dve.wait_ge(scale_step, S[0])
            p = probs(u)
            for s in u["segs"]:
                row = p[:, s["r"], s["at"]:s["at"] + s["keys"]]
                dve.tensor_scalar(row, row, row_s[:, n, s["column"]:s["column"] + 1], None,
                                  ALU.mult).then_inc(probs_ready, 1)

        def turned_low(u, i):
            t = u["block0"] + i
            rows = CB if u["blocks"][i][0] == "cmp" else P
            dve.wait_ge(pt_hi_ready, t + 1)
            dve.tensor_tensor(pt_lo[t % 3][0:rows, :, :], ps[0:rows, TURN[t % 2], :].rearrange("p (r q) -> p r q", r=R),
                              pt_hi[t % 3][0:rows, :, :], ALU.subtract).then_inc(pt_lo_ready, 1)

        def outputs(u):
            dve.wait_ge(o_low_ready, u["step"] + 1)
            both = ps[0:HEAD_DIM, OUTS[u["step"] % 2], :].rearrange("p (a b q) -> p b a q", b=2, q=P)
            low = o_sum[0:HEAD_DIM, :, :].rearrange("p (a b) q -> p b a q", b=2)
            for odd in range(2):
                dve.tensor_tensor(heads_out(u)[odd * HEAD_DIM:(odd + 1) * HEAD_DIM, 2 * u["g"]:2 * u["g"] + 2,
                                               u["qb"] * P:(u["qb"] + 1) * P],
                                  both[:, odd], low[:, odd], ALU.add).then_inc(o_ready, 1)

        S = [0]
        dve.wait_ge(masks_ready, 10)
        stage_queries(units[0])
        maxima(units[0], 0)
        for k, u in enumerate(units):
            after = units[k + 1] if k + 1 < len(units) else None
            scales(u)
            if after and after["first_of_step"]:
                stage_queries(after)
            for what, i in interleave(u["blocks"], after["parts"] if after else []):
                if what == "part":
                    maxima(after, i)
                else:
                    turned_low(u, i)
            if u["last_of_step"]:
                outputs(u)

        for tile in range(2):
            split_x(QB // 2, tile, tile)
        with dve.Fori(1, QB // 2) as i:
            for slot in range(2):
                split_x(i + QB // 2, slot, i * 2 + slot)
        dve.wait_ge(o_split_hi, 2)
        dve.tensor_tensor(oal[:, :, :], qa[:, :, :], oah[:, :, :], ALU.subtract).then_inc(o_split_lo, 1)
        dve.tensor_tensor(obl[:, :, :], qb_[:, :, :], obh[:, :, :], ALU.subtract).then_inc(o_split_lo, 1)
        split_w(0, GATE_USE[0])
        with dve.Fori(0, KT) as j:
            split_w(1, j + GATE_USE[1])
            dve.wait_ge(wb_hi_ready, j + 1)
            dve.tensor_tensor(wb_lo[:, :, :], wb_raw[:, :, :], wb_hi[:, :, :], ALU.subtract).then_inc(wb_lo_ready, 1)
            split_w(0, j + (GATE_USE[0] + 1))
            for slot, sg, bank in ((0, sg_a, Y_A), (1, sg_b, Y_B)):
                dve.wait_ge(sg_ready[slot], j + 1)
                dve.wait_ge(y_done[slot], j + 1)
                dve.tensor_tensor(sg[:, :], sg[:, :], wide(bank), ALU.mult).then_inc(gated, 1)

        def split_row(slot, n, lo, hi):
            dve.wait_ge(row_hi_ready[slot], n + 1)
            dve.tensor_tensor(lo, row_raw[slot][:, :], hi, ALU.subtract).then_inc(row_lo_ready[slot], 1)

        def stage_merged(slot, n, tile):
            dve.wait_ge(mst_hi_ready[slot], n + 1)
            dve.tensor_tensor(mst_lo[slot][:, :, :], merged[:, :, bass.ds(tile * P, P)], mst_hi[slot][:, :, :],
                              ALU.subtract).then_inc(mst_lo_ready[slot], 1)

        STEPS_OF_NORM = 3

        def norm(t, slot, count):
            for half in range(2):
                dve.bn_stats(bn[:, slot, half, :], acc[:, t, half * HALF:(half + 1) * HALF]).then_inc(ln_step, 1)
            dve.wait_ge(ln_step, count * STEPS_OF_NORM + 2)
            dve.bn_aggr(mv[:, slot, :], bn[:, slot, :, :].rearrange("p a b -> p (a b)")).then_inc(var_ready, 1)
            dve.wait_ge(std_ready, count + 1)
            dve.reciprocal(rstd[:, slot, 1:2], rstd[:, slot, 0:1]).then_inc(ln_step, 1)
            dve.wait_ge(ln_step, count * STEPS_OF_NORM + 3)
            dve.tensor_scalar(acc[:, t, :], acc[:, t, :], mv[:, slot, 0:1], rstd[:, slot, 1:2],
                              ALU.subtract, ALU.mult).then_inc(normed, 1)

        def add_residual(slot, n, t):
            dve.wait_ge(xres_in[slot], (n + 1) * 16)
            dve.wait_ge(mix_done[slot], n + 1)
            dve.scalar_tensor_tensor(out=acc[:, t, :], in0=x_raw[slot][:, :], scalar=ALPHA, in1=wide(2 * slot),
                                     op0=ALU.mult, op1=ALU.add).then_inc(z_ready[slot], 1)
            dve.wait_ge(z_ready[slot], n + 1)

        stage_merged(0, 0, 0)
        for kt in range(KT):
            split_row(kt % 2, kt // 2, wo_lo[:, kt, :], wo_hi[:, kt, :])
        stage_merged(1, 0, 1)
        for i in range(QB // 2 - 1):
            for slot in range(2):
                add_residual(slot, i, i * 2 + slot)
                norm(i * 2 + slot, slot, i * 2 + slot)
                stage_merged(slot, i + 1, (i + 1) * 2 + slot)
        for slot in range(2):
            add_residual(slot, QB // 2 - 1, QB - 2 + slot)
            norm(QB - 2 + slot, slot, QB - 2 + slot)
        split_w(1, UP_USE[1])
        for t in range(QB):
            dve.wait_ge(hh_ready, t + 1)
            dve.tensor_tensor(hl[:, :, t * P:(t + 1) * P], tiles(4 + 2 * (t % 2)), hh[:, :, t * P:(t + 1) * P],
                              ALU.subtract).then_inc(hl_ready, 1)

        def hidden_low(slot, c, parity):
            dve.wait_ge(uh_ready[slot], c + 1)
            dve.tensor_tensor(ul[parity][:, slot, :], usq[slot][:, :], uh[parity][:, slot, :],
                              ALU.subtract).then_inc(ul_ready[slot], 1)

        def add_down(c, q):
            dve.wait_ge(down_done, c * 16 + (q + 1))
            cols = acc[:, q // 2, (q % 2) * HALF:(q % 2 + 1) * HALF]
            dve.tensor_tensor(cols, cols, ps[:, 4 + q % 4, :], ALU.add).then_inc(down_added, 1)

        def mlp_step(c, parity, ups, splits):
            for slot in range(CHUNK):
                split_row(slot, c + ROW_OUT, wd_lo[slot][:, :], wd_hi[slot][:, :])
            if splits:
                for slot in range(CHUNK):
                    split_w(slot, c + (UP_USE[slot] + 2))
            if ups:
                hidden_low(0, c + 1, 1 - parity)
            for q in range(16):
                if ups and q == 3:
                    hidden_low(1, c + 1, 1 - parity)
                add_down(c, q)

        for slot in range(CHUNK):
            dve.sem_inc(ul_ready[slot], 1)
        for slot in range(CHUNK):
            split_w(slot, UP_USE[slot] + 1)
        for slot in range(CHUNK):
            hidden_low(slot, 0, 0)
        dve.wait_ge(residual_ready, QB)
        with dve.Fori(0, CHUNKS // 2 - 1) as i:
            mlp_step(i * 2, 0, True, True)
            mlp_step(i * 2 + 1, 1, True, True)
        mlp_step(CHUNKS - 2, 0, True, False)
        mlp_step(CHUNKS - 1, 1, False, False)
        for t in range(QB):
            dve.wait_ge(down_added, 16 * (CHUNKS - 1) + 2 * t + 2)
            norm(t, t % 2, QB + t)

    @block.tensor
    def _(pe):
        def turn_x(n, slot):
            pe.wait_ge(x_in[slot], (n + 1) * 16)
            at_least(pe, xl_ready[slot], n)
            for k in range(KT):
                last = pe.transpose(tiles(4 + 2 * slot)[:, k, :], x_raw[slot][:, k * P:(k + 1) * P], ident[:, :])
            last.then_inc(x_turned[slot], 1)

        def product(slot, n, hi, lo, taken):
            pe.wait_ge(w_lo_ready[slot], n + 1)
            at_least(pe, product_taken[slot], taken)
            for k in range(KT):
                for p, (w, a) in enumerate(((w_hi, hi), (w_hi, lo), (w_lo, hi))):
                    for half in range(2):
                        last = pe.matmul(ps[:, 2 * slot + half, :], w[slot][:, k, :],
                                         a[:, k, half * HALF:(half + 1) * HALF],
                                         start=(k == 0 and p == 0), stop=(k == KT - 1 and p == 2))
            last.then_inc(product_done[slot], 1)

        pe.wait_ge(const_ready, 1)
        pe.wait_ge(small_in, 32)
        pe.transpose(ps[:, SMALL_BANK, 0:2 * CT], pos_nat[:, :], ident[0:2 * CT, 0:2 * CT]).then_inc(pos_turned, 1)
        turn_x(0, 0)
        pe.wait_ge(pos_ready, 1)
        turn_x(0, 1)
        with pe.Fori(1, QB // 2) as i:
            for slot in range(2):
                turn_x(i, slot)
        for slot in range(2):
            pe.wait_ge(xl_ready[slot], QB // 2)
        product(0, 0, xh, xl, 0)
        product(1, 0, xh, xl, 0)
        with pe.Fori(0, 4) as j:
            for slot in range(2):
                product(slot, j + 1, xh, xl, j + 1)

        pe.wait_ge(cx_ready, 8)
        pe.wait_ge(pool_step, 4)
        pe.wait_ge(cmp_w_in, 80)
        for kind in range(2):
            for f in range(2):
                col = (2 * kind + f) * P
                for t in range(CT):
                    last = pe.matmul(ps[:, HIDDEN_BANK, col:col + P], cw1[kind][:, t, f * P:(f + 1) * P],
                                     cx[kind][:, t, :, :].rearrange("p g c -> p (g c)"),
                                     start=(t == 0), stop=(t == CT - 1))
        last.then_inc(hidden_done, 1)
        product(0, 5, xh, xl, 5)
        pe.wait_ge(gelu_ready, 1)
        for f in range(2):
            pe.matmul(ps[:, SMALL_BANK, 0:P], cw2k[:, f, :, :].rearrange("p a d -> p (a d)"),
                      g_out[:, 0, f, :, :].rearrange("p g c -> p (g c)"), start=(f == 0), stop=(f == 1))
        for g in range(KV):
            for f in range(2):
                last = pe.matmul(ps[0:CB, SMALL_BANK, P + g * HEAD_DIM:P + (g + 1) * HEAD_DIM],
                                 g_out[:, 1, f, g, :], cw2v[:, f, :], start=(f == 0), stop=(f == 1))
        last.then_inc(cmp_done, 1)

        def turn_values(src, number, slot, n):
            pe.wait_ge(product_taken[slot], n + 1)
            at_least(pe, v_lo_ready, 2 * number)
            for k in range(QB):
                last = pe.transpose(tiles(4)[:, k, :], src[:, k * P:(k + 1) * P], ident[:, :])
            last.then_inc(v_turned, 1)

        product(1, 5, xh, xl, 5)
        product(0, 6, xh, xl, 6)
        turn_values(vT, 0, 1, 5)
        product(1, 6, xh, xl, 6)
        product(0, 7, xh, xl, 7)
        turn_values(vT, 1, 1, 6)
        product(1, 7, xh, xl, 7)
        product(0, 8, xh, xl, 8)
        turn_values(vT, 2, 1, 7)
        turn_values(gaT, 3, 0, 8)

        def scores(u, part):
            number = u["part0"] + part
            slot = SCORES[number % 2]
            pe.wait_ge(q_lo_ready, R * (u["step"] + 1))
            at_least(pe, row_max, part_end[number - 2] if number >= 2 else 0)
            for s in u["parts"][part]:
                for c in range(0, s["keys"], HALF):
                    n = min(HALF, s["keys"] - c)
                    for k in (k_hi, k_lo):
                        last = pe.matmul(wide(slot)[:, s["score0"] + c:s["score0"] + c + n],
                                         q_st[u["step"] % 2][:, s["r"], :],
                                         k[s["what"]][:, u["g"], s["key0"] + c:s["key0"] + c + n],
                                         start=(k is k_hi), stop=(k is k_lo))
            last.then_inc(scores_done, 1)

        def turn_probs(u, i):
            t = u["block0"] + i
            what, _, at = u["blocks"][i]
            rows = CB if what == "cmp" else P
            pe.wait_ge(probs_ready, u["seg0"] + len(u["segs"]))
            at_least(pe, pt_lo_ready, t - 1)
            for r in range(R):
                last = pe.transpose(ps[0:rows, TURN[t % 2], r * P:(r + 1) * P], probs(u)[:, r, at:at + rows],
                                    ident[:, :])
            last.then_inc(probs_turned, 1)

        def weigh_values(u, i):
            t = u["block0"] + i
            what, kb, _ = u["blocks"][i]
            rows = CB if what == "cmp" else P
            pe.wait_ge(pt_lo_ready, t + 1)
            first = u["first_of_step"] and i == 0
            if first:
                at_least(pe, o_ready, 2 * (u["step"] - 1))
            last_block = u["last_of_step"] and i == len(u["blocks"]) - 1
            for n, pt in enumerate((pt_hi, pt_lo)):
                last = pe.matmul(ps[:, OUTS[u["step"] % 2], :], v_hl[what][0:rows, kb, u["g"], :],
                                 pt[t % 3][0:rows, :, :].rearrange("p r q -> p (r q)"),
                                 start=(first and n == 0), stop=(last_block and n == 1))
            last.then_inc(values_done, 1)

        pe.wait_ge(kv_lo_ready, 9)
        pe.wait_ge(cmp_lo_ready, 2)
        pe.wait_ge(v_lo_ready, 6)
        pe.wait_ge(gate_ready, 1)
        pe.wait_ge(product_taken[0], GATE_USE[0])
        pe.wait_ge(product_taken[1], GATE_USE[1])
        scores(units[0], 0)
        waiting = []
        for k, u in enumerate(units):
            after = units[k + 1] if k + 1 < len(units) else None
            for what, i in interleave(u["blocks"], after["parts"] if after else []):
                if what == "part":
                    scores(after, i)
                else:
                    turn_probs(u, i)
                    waiting.append((u, i))
                    if len(waiting) > 1:
                        weigh_values(*waiting.pop(0))
            if u["last_of_step"]:
                while waiting:
                    weigh_values(*waiting.pop(0))

        pe.wait_ge(o_ready, 2 * STEPS)
        pe.wait_ge(pt_lo_ready, BLOCKS)
        pe.wait_ge(row_max, SEGS)
        for slot in range(2):
            turn_x(QB // 2, slot)
        with pe.Fori(1, QB // 2) as i:
            for slot in range(2):
                turn_x(i + QB // 2, slot)
        for slot in range(2):
            pe.wait_ge(xl_ready[slot], QB)
        pe.wait_ge(o_split_lo, 2)

        def merge(j):
            at_least(pe, sg_ready[0], j)
            product(0, j + GATE_USE[0], xh, xl, 0)
            at_least(pe, sg_ready[1], j)
            product(1, j + GATE_USE[1], xh, xl, 0)
            pe.wait_ge(wb_lo_ready, j + 1)
            at_least(pe, gated, j * 2)
            for side, (bank, hi, lo) in enumerate(((Y_A, oah, oal), (Y_B, obh, obl))):
                for k in range(4):
                    for p, (w, a) in enumerate(((wb_hi, hi), (wb_hi, lo), (wb_lo, hi))):
                        for half in range(2):
                            last = pe.matmul(ps[:, bank + half, :], w[:, 4 * side + k, :],
                                             a[:, k, half * HALF:(half + 1) * HALF],
                                             start=(k == 0 and p == 0), stop=(k == 3 and p == 2))
                last.then_inc(y_done[side], 1)

        merge(0)
        with pe.Fori(1, KT) as j:
            merge(j)

        def mix(n, slot):
            pe.wait_ge(mst_lo_ready[slot], n + 1)
            at_least(pe, z_ready[slot], n)
            for k in range(KT):
                for p, (a, w) in enumerate(((mst_hi, wo_hi), (mst_hi, wo_lo), (mst_lo, wo_hi))):
                    for half in range(2):
                        last = pe.matmul(ps[:, 2 * slot + half, :], a[slot][:, k, :],
                                         w[:, k, half * HALF:(half + 1) * HALF],
                                         start=(k == 0 and p == 0), stop=(k == KT - 1 and p == 2))
            last.then_inc(mix_done[slot], 1)

        for slot in range(2):
            pe.wait_ge(sg_ready[slot], KT)
            pe.wait_ge(row_lo_ready[slot], KT // 2)
        mix(0, 0)
        mix(0, 1)
        with pe.Fori(1, QB // 2) as i:
            for slot in range(2):
                mix(i, slot)
        for t in range(QB):
            pe.wait_ge(ln_done, t + 1)
            at_least(pe, hl_ready, t - 1)
            for k in range(KT):
                last = pe.transpose(tiles(4 + 2 * (t % 2))[:, k, :], acc[:, t, k * P:(k + 1) * P], ident[:, :])
            last.then_inc(h_turned, 1)

        def up(c):
            for slot in range(CHUNK):
                at_least(pe, relu_ready[slot], c)
                product(slot, c + UP_USE[slot], hh, hl, 0)

        def down(c, parity):
            for slot in range(CHUNK):
                pe.wait_ge(row_lo_ready[slot], c + (ROW_OUT + 1))
                pe.wait_ge(ul_ready[slot], c + 2)
            for q in range(16):
                if q >= 4:
                    pe.wait_ge(down_added, c * 16 + (q - 3))
                else:
                    at_least(pe, down_added, c * 16 + (q - 3) if not isinstance(c, int) or c else 0)
                tile, half = q // 2, q % 2
                for f in range(CHUNK):
                    for p, (a, w) in enumerate(((uh, wd_hi), (uh, wd_lo), (ul, wd_hi))):
                        last = pe.matmul(ps[:, 4 + q % 4, :], a[parity][:, f, tile * P:(tile + 1) * P],
                                         w[f][:, half * HALF:(half + 1) * HALF],
                                         start=(f == 0 and p == 0), stop=(f == CHUNK - 1 and p == 2))
                last.then_inc(down_done, 1)

        pe.wait_ge(hl_ready, QB)
        for slot in range(2):
            pe.wait_ge(z_ready[slot], QB // 2)
        up(0)
        up(1)
        down(0, 0)
        up(2)
        down(1, 1)
        with pe.Fori(1, CHUNKS // 2 - 1) as i:
            up(i * 2 + 1)
            down(i * 2, 0)
            up(i * 2 + 2)
            down(i * 2 + 1, 1)
        up(CHUNKS - 1)
        down(CHUNKS - 2, 0)
        down(CHUNKS - 1, 1)

    ctx.close()


_INS = ["x", "w_in", "cmp_pos_k", "cmp_w1_k", "cmp_w2_k", "cmp_pos_v", "cmp_w1_v", "cmp_w2_v", "sink_logits",
        "w_branch_a", "w_branch_b", "w_out", "ln1_g", "ln1_b", "w_up", "w_down", "ln2_g", "ln2_b"]


def kernel(**inputs):
    import concourse.bacc as bacc
    from concourse.bass_utils import run_bass_kernel_spmd

    nc = bacc.Bacc("TRN2", target_bir_lowering=False, num_devices=1)
    arrays = {f"in_{name}": np.ascontiguousarray(inputs[name]) for name in _INS}
    args = [nc.dram_tensor(name, a.shape, mybir.dt.from_np(a.dtype), kind="ExternalInput").ap()
            for name, a in arrays.items()]
    args.append(nc.dram_tensor("out_h", (1, SEQ, D_MODEL), F32, kind="ExternalOutput").ap())
    layer(nc, *args)
    return run_bass_kernel_spmd(nc, [arrays], core_ids=[0]).results[0]["out_h"]
```

```python
from contextlib import ExitStack

import numpy as np
import concourse.bass as bass
from concourse import mybir

F32 = mybir.dt.float32
F32R = mybir.dt.float32r
ALU = mybir.AluOpType
ACT = mybir.ActivationFunctionType

P = 128
SEQ = 1024
D_MODEL = 1024
HEAD_DIM = 64
HEADS = 8
KV = 2
R = HEADS // KV
CMP_LEN = 32
CMP_STRIDE = 16
CMP_HIDDEN = 4 * HEAD_DIM
SWA_WINDOW = 128
NSA_WINDOW = 512
D_FF = 4 * D_MODEL
LN_EPS = 1e-5
MASKED = 2.0 ** 100
ALPHA = 2.0 ** 0.25
QB = SEQ // P
KT = D_MODEL // P
HALF = 512
CB = 64
CT = CMP_LEN * HEAD_DIM // P
BRANCHES = 3
CHUNK = 2
CHUNKS = D_FF // (CHUNK * P)

KVW = KV * HEAD_DIM
COL_QA = 0
COL_KC = HEADS * HEAD_DIM
COL_VC = COL_KC + KVW
COL_KS = COL_VC + KVW
COL_VS = COL_KS + KVW
COL_KW = COL_VS + KVW
COL_VW = COL_KW + KVW
COL_GA = COL_VW + KVW
COL_QB = COL_GA + BRANCHES * HEADS
COL_KB = COL_QB + HEADS * HEAD_DIM
COL_VB = COL_KB + KVW
COL_GATE_A = COL_VB + KVW
COL_GATE_B = COL_GATE_A + D_MODEL

SLOPES = [2.0 ** (-8.0 * (i + 1) / (2 * HEADS)) for i in range(2 * HEADS)]
PT_RING = 4
LEAD = 2
GELU_IN = (2.0 / np.pi) ** 0.5


def at_least(engine, sem, count):
    if not (isinstance(count, int) and count <= 0):
        engine.wait_ge(sem, count)


def attention_units():
    units, step, part, seg, block = [], 0, 0, 0, 0
    for kind, g, qb in ([("swa", g, qb) for g in range(KV) for qb in range(QB)]
                        + [(kind, g, qb) for g in range(KV) for qb in range(QB) for kind in ("slc", "wc")]):
        u = {"kind": kind, "g": g, "qb": qb, "step": step, "number": len(units), "parts": [], "blocks": []}
        if kind == "swa":
            first = max(0, qb - SWA_WINDOW // P)
            keys = (qb + 1 - first) * P
            u["parts"] = [[{"r": r, "what": "swa", "key0": first * P, "keys": keys, "score0": 0,
                            "table0": 2 * P - keys, "at": 0}] for r in range(R)]
            u["blocks"] = [("swa", kb, (kb - first) * P) for kb in range(first, qb + 1)]
        elif kind == "slc":
            keys = (qb + 1) * P
            u["parts"] = [[{"r": r, "what": "slc", "key0": 0, "keys": keys, "score0": 0,
                            "table0": SEQ + P - keys, "at": 0}] for r in range(R)]
            u["blocks"] = [("slc", kb, kb * P) for kb in range(qb + 1)]
        else:
            first = max(0, qb - NSA_WINDOW // P)
            keys = (qb + 1 - first) * P
            width = NSA_WINDOW + P
            u["parts"] = [[{"r": r, "what": "cmp", "key0": 0, "keys": CB, "score0": keys,
                            "table0": 0, "at": width},
                           {"r": r, "what": "win", "key0": first * P, "keys": keys, "score0": 0,
                            "table0": width - keys, "at": 0}] for r in range(R)]
            u["blocks"] = [("win", kb, (kb - first) * P) for kb in range(first, qb + 1)] + [("cmp", 0, width)]
        u["part0"], u["seg0"], u["block0"] = part, seg, block
        part += len(u["parts"])
        for segs in u["parts"]:
            for s in segs:
                s["number"], s["column"] = seg, seg - u["seg0"]
                seg += 1
        block += len(u["blocks"])
        u["segs"] = [s for segs in u["parts"] for s in segs]
        u["first_of_step"] = kind != "wc"
        u["last_of_step"] = kind != "slc"
        step += u["last_of_step"]
        units.append(u)
    return units, step, seg, block


def attention_order(units):
    order = [("part", units[0], i) for i in range(len(units[0]["parts"]))]
    for u, after in zip(units, units[1:] + [None]):
        parts = after["parts"] if after else []
        items = [((i + 0.5) / len(u["blocks"]), 1, "block", u, i) for i in range(len(u["blocks"]))]
        items += [((i - LEAD) / max(1, len(parts) - LEAD), 0, "part", after, i) for i in range(len(parts))]
        order += [x[2:] for x in sorted(items, key=lambda x: x[:2])]
    return [(place, *item) for place, item in enumerate(order)]


def in_turn(order, lags):
    work = []
    for place, kind, u, i in order:
        work += [(place + lag, n, what, u, i) for n, (what, (of, lag)) in enumerate(lags.items()) if of == kind]
        if kind == "part" and i == 0 and u["first_of_step"] and "stage" in lags:
            work.append((place + lags["stage"][1], -1, "stage", u, 0))
        if kind == "block" and i == len(u["blocks"]) - 1 and u["last_of_step"] and "outputs" in lags:
            work.append((place + lags["outputs"][1], -1, "outputs", u, 0))
    return [x[2:] for x in sorted(work, key=lambda x: x[:2])]


def layer(nc, x, w_in, pos_k, w1_k, w2_k, pos_v, w1_v, w2_v, sinks, w_branch_a, w_branch_b, w_out,
          ln1_g, ln1_b, w_up, w_down, ln2_g, ln2_b, out):
    ctx = ExitStack()
    kb_ = 1024
    base = 16512

    def sb(name, at, shape, dt=F32):
        return nc.alloc_sbuf_tensor_at(name, shape, dt, offset=base + int(at * kb_))

    def sem(name):
        return ctx.enter_context(nc.semaphore(name))

    ident = sb("ident", 0, [P, P])
    sink_row = sb("sink_row", 0.5625, [P, HEADS])
    sink_neg = sb("sink_neg", 0.59375, [P, HEADS])
    eps = sb("eps", 0.625, [P, 1])
    bn = sb("bn", 0.75, [P, 2, 2, 6])
    mv = sb("mv", 0.875, [P, 2, 2])
    rstd = sb("rstd", 0.9375, [P, 2, 2])
    seen = sb("seen", 1.0, [P, 1])
    posT = sb("posT", 1.125, [P, 2 * CT])
    pos_nat = sb("pos_nat", 1.25, [2 * CT, P])
    qa = sb("qa", 2, [P, 4, SEQ])
    qb_ = sb("qb", 18, [P, 4, SEQ])
    merged = sb("merged", 2, [P, KT, SEQ])
    uh = [sb(f"uh{i}", 2 + 16 * i, [P, CHUNK, SEQ], F32R) for i in range(2)]
    ul = [sb(f"ul{i}", 10 + 16 * i, [P, CHUNK, SEQ], F32R) for i in range(2)]
    w_raw = [sb(f"w_raw{i}", 34 + 4 * i, [P, KT, P]) for i in range(2)]
    w_hi = [sb(f"w_hi{i}", 42 + 4 * i, [P, KT, P], F32R) for i in range(2)]
    w_lo = [sb(f"w_lo{i}", 50 + 4 * i, [P, KT, P], F32R) for i in range(2)]
    xh = sb("xh", 58, [P, KT, SEQ], F32R)
    xl = sb("xl", 90, [P, KT, SEQ], F32R)
    t_slc = sb("t_slc", 58, [P, SEQ + P])
    t_win = sb("t_win", 62.5, [P, NSA_WINDOW + P])
    t_swa = sb("t_swa", 65, [P, 2 * P])
    t_cmp = sb("t_cmp", 66, [P, QB, CB])
    p_slc = sb("p_slc", 68, [P, R, SEQ])
    p_wc = sb("p_wc", 84, [P, R, NSA_WINDOW + 2 * P])
    p_swa = [sb(f"p_swa{i}", 84 + 4 * i, [P, R, 2 * P]) for i in range(2)]
    pt_hi = [sb(f"pt_hi{i}", 96 + 4 * i, [P, R, P], F32R) for i in range(PT_RING)]
    pt_lo = [sb(f"pt_lo{i}", 98 + 4 * i, [P, R, P], F32R) for i in range(PT_RING)]
    q_st = [sb(f"q_st{i}", 112 + 2 * i, [P, R, P], F32R) for i in range(2)]
    o_sum = sb("o_sum", 116, [P, R, P])
    m_neg = sb("m_neg", 118, [P, 2, 8])
    row_l = sb("row_l", 118.25, [P, 2, 8])
    row_s = sb("row_s", 118.375, [P, 2, 8])
    sink_e = sb("sink_e", 118.5, [P, 2, 8])
    wo_hi = sb("wo_hi", 58, [P, KT, D_MODEL], F32R)
    wo_lo = sb("wo_lo", 90, [P, KT, D_MODEL], F32R)
    hh = sb("hh", 58, [P, KT, SEQ], F32R)
    hl = sb("hl", 90, [P, KT, SEQ], F32R)
    kcs = [sb(f"kcs{i}", 122 + 4 * i, [P, SEQ]) for i in range(2 * KV)]
    cx = [sb(f"cx{i}", 138 + 8 * i, [P, CT, KV, CB]) for i in range(2)]
    cw1 = [sb(f"cw1{i}", 154 + 16 * i, [P, CT, CMP_HIDDEN]) for i in range(2)]
    cw2k = sb("cw2k", 186, [P, 2, 2, HEAD_DIM])
    cw2v = sb("cw2v", 187, [P, 2, HEAD_DIM])
    k_hi, k_lo, v_hl = {}, {}, {}
    for i, what in enumerate(("slc", "win", "swa")):
        k_hi[what] = sb(f"k_hi_{what}", 122 + 16 * i, [P, KV, SEQ], F32R)
        k_lo[what] = sb(f"k_lo_{what}", 130 + 16 * i, [P, KV, SEQ], F32R)
        v_hl[what] = sb(f"v_hl_{what}", 170 + 8 * i, [P, QB, KV, 2 * HEAD_DIM], F32R)
    oah = sb("oah", 122, [P, 4, SEQ], F32R)
    oal = sb("oal", 138, [P, 4, SEQ], F32R)
    obh = sb("obh", 154, [P, 4, SEQ], F32R)
    obl = sb("obl", 170, [P, 4, SEQ], F32R)
    sg_a = sb("sg_a", 186, [P, SEQ])
    sg_b = sb("sg_b", 190, [P, SEQ])
    acc = sb("acc", 122, [P, QB, D_MODEL])
    mst_hi = [sb(f"mst_hi{i}", 154 + 4 * i, [P, KT, P], F32R) for i in range(2)]
    mst_lo = [sb(f"mst_lo{i}", 162 + 4 * i, [P, KT, P], F32R) for i in range(2)]
    relu = [sb(f"relu{i}", 154 + 4 * i, [P, SEQ]) for i in range(2)]
    usq = [sb(f"usq{i}", 162 + 4 * i, [P, SEQ]) for i in range(2)]
    row_raw = [sb(f"row_raw{i}", 170 + 4 * i, [P, D_MODEL]) for i in range(2)]
    ln_g = sb("ln_g", 178, [P, D_MODEL])
    ln_b = sb("ln_b", 182, [P, D_MODEL])
    wd_hi = [sb(f"wd_hi{i}", 186 + 4 * i, [P, D_MODEL], F32R) for i in range(2)]
    x_raw = [sb(f"x_raw{i}", 194 + 4 * i, [P, D_MODEL]) for i in range(2)]
    g_in = sb("g_in", 194, [P, 2 * 2 * P])
    g_t = sb("g_t", 196, [P, 2 * 2 * P])
    g_u = sb("g_u", 198, [P, 2 * 2 * P])
    g_out = sb("g_out", 200, [P, 2, 2, KV, CB])
    vT = sb("vT", 194, [P, SEQ])
    gaT = sb("gaT", 198, [P, SEQ])
    wb_raw = sb("wb_raw", 194, [P, KT, P])
    wb_hi = sb("wb_hi", 198, [P, KT, P], F32R)
    wd_lo = [sb(f"wd_lo{i}", 194 + 4 * i, [P, D_MODEL], F32R) for i in range(2)]
    k_hi["cmp"] = sb("k_hi_cmp", 202, [P, KV, CB], F32R)
    k_lo["cmp"] = sb("k_lo_cmp", 202.5, [P, KV, CB], F32R)
    v_hl["cmp"] = sb("v_hl_cmp", 203, [P, 1, KV, 2 * HEAD_DIM], F32R)
    gate = sb("gate", 204, [P, QB, BRANCHES * HEADS])
    wb_lo = sb("wb_lo", 202, [P, KT, P], F32R)

    ps = ctx.enter_context(nc.psum_tensor("ps", [P, 8, HALF], F32))

    def wide(bank):
        return ps[:, bank:bank + 2, :].rearrange("p a b -> p (a b)")

    def score_row(part):
        b = score_bank[part]
        return ps[:, b:min(b + 2, SCORE_BANKS), :].rearrange("p a b -> p (a b)")

    def tiles(bank):
        return ps[:, bank:bank + 2, :].rearrange("p a (b c) -> p (a b) c", c=P)

    TURN, OUT_BANK = (4, 5, 6), 7
    HIDDEN_BANK, SMALL_BANK = 6, 7
    Y_A, Y_B = 4, 6

    const_ready = sem("const_ready")
    masks_ready = sem("masks_ready")
    pool_step = sem("pool_step")
    small_in = sem("small_in")
    sinks_in = sem("sinks_in")
    cmp_w_in = sem("cmp_w_in")
    x_in = [sem(f"x_in{i}") for i in range(2)]
    x_turned = [sem(f"x_turned{i}") for i in range(2)]
    xh_ready = [sem(f"xh_ready{i}") for i in range(2)]
    xl_ready = [sem(f"xl_ready{i}") for i in range(2)]
    w_loaded = [sem(f"w_loaded{i}") for i in range(2)]
    w_hi_ready = [sem(f"w_hi_ready{i}") for i in range(2)]
    w_lo_ready = [sem(f"w_lo_ready{i}") for i in range(2)]
    product_done = [sem(f"product_done{i}") for i in range(2)]
    product_taken = [sem(f"product_taken{i}") for i in range(2)]
    pos_turned = sem("pos_turned")
    pos_ready = sem("pos_ready")
    kc_ready = sem("kc_ready")
    vc_ready = sem("vc_ready")
    cx_ready = sem("cx_ready")
    hidden_done = sem("hidden_done")
    hidden_copied = sem("hidden_copied")
    tanh_done = sem("tanh_done")
    gelu_step = sem("gelu_step")
    gelu_ready = sem("gelu_ready")
    cmp_done = sem("cmp_done")
    cmp_hi_ready = sem("cmp_hi_ready")
    cmp_lo_ready = sem("cmp_lo_ready")
    kv_hi_ready = sem("kv_hi_ready")
    kv_lo_ready = sem("kv_lo_ready")
    v_turned = sem("v_turned")
    v_hi_ready = sem("v_hi_ready")
    v_lo_ready = sem("v_lo_ready")
    gate_ready = sem("gate_ready")
    gate_fixed = sem("gate_fixed")
    consts_done = sem("consts_done")
    q_hi_ready = sem("q_hi_ready")
    q_lo_ready = sem("q_lo_ready")
    scores_done = sem("scores_done")
    row_max = sem("row_max")
    exp_done = sem("exp_done")
    sink_exp = sem("sink_exp")
    scale_step = sem("scale_step")
    scale_ready = sem("scale_ready")
    probs_ready = sem("probs_ready")
    probs_turned = sem("probs_turned")
    pt_hi_ready = sem("pt_hi_ready")
    pt_lo_ready = sem("pt_lo_ready")
    values_done = sem("values_done")
    o_low_ready = sem("o_low_ready")
    o_ready = sem("o_ready")
    o_split_hi = sem("o_split_hi")
    o_split_lo = sem("o_split_lo")
    wb_loaded = sem("wb_loaded")
    wb_hi_ready = sem("wb_hi_ready")
    wb_lo_ready = sem("wb_lo_ready")
    sg_ready = [sem(f"sg_ready{i}") for i in range(2)]
    y_done = [sem(f"y_done{i}") for i in range(2)]
    gated = sem("gated")
    merged_ready = sem("merged_ready")
    row_loaded = [sem(f"row_loaded{i}") for i in range(2)]
    row_hi_ready = [sem(f"row_hi_ready{i}") for i in range(2)]
    row_lo_ready = [sem(f"row_lo_ready{i}") for i in range(2)]
    mst_hi_ready = [sem(f"mst_hi_ready{i}") for i in range(2)]
    mst_lo_ready = [sem(f"mst_lo_ready{i}") for i in range(2)]
    mix_done = [sem(f"mix_done{i}") for i in range(2)]
    xres_in = [sem(f"xres_in{i}") for i in range(2)]
    z_ready = [sem(f"z_ready{i}") for i in range(2)]
    ln_step = sem("ln_step")
    var_ready = sem("var_ready")
    std_ready = sem("std_ready")
    normed = sem("normed")
    ln_scaled = sem("ln_scaled")
    ln_done = sem("ln_done")
    ln_in = sem("ln_in")
    h_turned = sem("h_turned")
    hh_ready = sem("hh_ready")
    hl_ready = sem("hl_ready")
    residual_ready = sem("residual_ready")
    relu_ready = [sem(f"relu_ready{i}") for i in range(2)]
    usq_ready = [sem(f"usq_ready{i}") for i in range(2)]
    uh_ready = [sem(f"uh_ready{i}") for i in range(2)]
    ul_ready = [sem(f"ul_ready{i}") for i in range(2)]
    down_done = sem("down_done")
    down_added = sem("down_added")
    stored = sem("stored")

    units, STEPS, SEGS, BLOCKS = attention_units()
    last_unit_of = {}
    for u in units:
        u["buffer"] = {"swa": f"swa{u['step'] % 2}", "slc": "slc", "wc": "wc"}[u["kind"]]
        shares = {"slc": ("slc",), "wc": ("wc", "swa0", "swa1")}.get(u["kind"], (u["buffer"],))
        before = [last_unit_of[b] for b in shares if b in last_unit_of]
        u["buffer_free"] = max((b["block0"] + len(b["blocks"]) for b in before), default=0)
        last_unit_of[u["buffer"]] = u

    parts_of = [sum(len(u["parts"]) for u in units if u["step"] <= step) for step in range(STEPS)]
    q_free = [0, 0] + parts_of[:STEPS - 2]

    SCORE_BANKS = 4
    score_bank, scores_free, holds, at_bank = [], [], [0] * SCORE_BANKS, 0
    for u in units:
        for p in u["parts"]:
            banks = -(-max(s["score0"] + s["keys"] for s in p) // HALF)
            at_bank += at_bank % banks
            score_bank.append(at_bank % SCORE_BANKS)
            scores_free.append(max(holds[score_bank[-1]:score_bank[-1] + banks]))
            holds[score_bank[-1]:score_bank[-1] + banks] = [p[-1]["number"] + 1] * banks
            at_bank += banks
    order = attention_order(units)

    def probs(u):
        return {"swa": p_swa[u["step"] % 2], "slc": p_slc, "wc": p_wc}[u["kind"]]

    def slope(u, s):
        return float(SLOPES[(0 if u["kind"] == "swa" else HEADS) + R * u["g"] + s["r"]])

    def query_scale(u, r):
        return float(np.float32(-HEAD_DIM ** -0.5 / slope(u, {"r": r})))

    def table(u, s):
        if s["what"] == "cmp":
            return t_cmp[:, u["qb"], :]
        t = {"slc": t_slc, "win": t_win, "swa": t_swa}[s["what"]]
        return t[:, s["table0"]:s["table0"] + s["keys"]]

    def heads_out(u):
        return qb_ if u["kind"] == "swa" else qa

    N_BEFORE_MERGE = 17
    W_COLS = {0: COL_KC, 1: COL_VC, 10: COL_KS, 11: COL_VS, 12: COL_KW, 13: COL_VW, 14: COL_KB, 15: COL_VB,
              16: COL_GA}
    GATE_USE = (9, 8)
    UP_USE = (GATE_USE[0] + KT, GATE_USE[1] + KT)
    ROW_OUT = KT // 2

    def columns(w, col):
        return w[0, :, bass.ds(col, P)].rearrange("(k p) c -> p k c", p=P)

    block = ctx.enter_context(nc.Block())

    @block.sync
    def _(sp):
        def load_x(n, slot, tile, loaded, used):
            at_least(sp, used[slot], n)
            sp.dma_start(x_raw[slot][:, :], x[0, bass.ds(tile * P, P), :]).then_inc(loaded[slot], 16)

        def load_w(slot, n, src):
            at_least(sp, w_lo_ready[slot], n)
            sp.dma_start(w_raw[slot][:, :, :], src).then_inc(w_loaded[slot], 16)

        def load_row(slot, n, src):
            at_least(sp, row_lo_ready[slot], n)
            sp.dma_start(row_raw[slot][:, :], src).then_inc(row_loaded[slot], 16)

        load_x(0, 0, 0, x_in, x_turned)
        load_x(0, 1, 1, x_in, x_turned)
        sp.dma_start(pos_nat[0:CT, :], pos_k[0].rearrange("(t l) d -> t (l d)", l=2)).then_inc(small_in, 16)
        sp.dma_start(pos_nat[CT:2 * CT, :], pos_v[0].rearrange("(t l) d -> t (l d)", l=2)).then_inc(small_in, 16)
        load_w(0, 0, columns(w_in, W_COLS[0]))
        load_w(1, 0, columns(w_in, W_COLS[1]))
        with sp.Fori(1, QB // 2) as i:
            for slot in range(2):
                load_x(i, slot, i * 2 + slot, x_in, x_turned)
        for kind, w1 in enumerate((w1_k, w1_v)):
            sp.dma_start(cw1[kind][:, :, :], w1[0].rearrange("(t l) d f -> (l d) t f", l=2)).then_inc(cmp_w_in, 16)
        for copy in range(2):
            sp.dma_start(cw2k[:, :, copy, :], w2_k[0].rearrange("(a f) d -> f a d", f=P)).then_inc(cmp_w_in, 16)
        sp.dma_start(cw2v[:, :, :], w2_v[0].rearrange("(a f) d -> f a d", f=P)).then_inc(cmp_w_in, 16)
        sp.dma_start(sink_row[:, :], sinks[0].partition_broadcast(P)).then_inc(sinks_in, 16)
        with sp.Fori(0, 4) as j:
            load_w(0, j + 1, columns(w_in, j * P + COL_QA))
            load_w(1, j + 1, columns(w_in, j * P + COL_QB))
        for b in range(10, N_BEFORE_MERGE):
            load_w(b % 2, b // 2, columns(w_in, W_COLS[b]))
        sp.wait_ge(v_turned, 4)
        uses = QB // 2
        load_x(uses, 0, 0, x_in, x_turned)
        load_x(uses, 1, 1, x_in, x_turned)
        load_w(1, GATE_USE[1], columns(w_in, COL_GATE_B))
        load_w(0, GATE_USE[0], columns(w_in, COL_GATE_A))
        with sp.Fori(1, QB // 2) as i:
            for slot in range(2):
                load_x(i + uses, slot, i * 2 + slot, x_in, x_turned)

        def load_branches(j):
            for half, w in enumerate((w_branch_a, w_branch_b)):
                sp.dma_start(wb_raw[:, 4 * half:4 * half + 4, :], columns(w, j * P)).then_inc(wb_loaded, 16)

        sp.wait_ge(x_turned[0], 2 * uses)
        sp.wait_ge(x_turned[1], 2 * uses)
        load_branches(0)
        for j in range(1, KT):
            sp.wait_ge(wb_lo_ready, j)
            load_w(0, j + GATE_USE[0], columns(w_in, j * P + COL_GATE_A))
            load_w(1, j + GATE_USE[1], columns(w_in, j * P + COL_GATE_B))
            load_branches(j)
        load_w(0, UP_USE[0], columns(w_up, 0))
        load_w(1, UP_USE[1], columns(w_up, P))
        sp.wait_ge(merged_ready, KT)
        sp.wait_ge(y_done[1], KT)
        load_row(0, 0, w_out[0, 0:P, :])
        load_row(1, 0, w_out[0, P:2 * P, :])
        load_x(0, 0, 0, xres_in, z_ready)
        load_x(0, 1, 1, xres_in, z_ready)
        with sp.Fori(1, KT // 2) as i:
            for slot in range(2):
                load_row(slot, i, w_out[0, bass.ds((i * 2 + slot) * P, P), :])
        sp.dma_start(ln_g[:, :], ln1_g[0].partition_broadcast(P)).then_inc(ln_in, 16)
        sp.dma_start(ln_b[:, :], ln1_b[0].partition_broadcast(P)).then_inc(ln_in, 16)
        with sp.Fori(1, QB // 2) as i:
            for slot in range(2):
                load_x(i, slot, i * 2 + slot, xres_in, z_ready)
        for slot in range(CHUNK):
            load_row(slot, ROW_OUT, w_down[0, slot * P:(slot + 1) * P, :])
        for slot in range(CHUNK):
            load_w(slot, UP_USE[slot] + 1, columns(w_up, (CHUNK + slot) * P))
        sp.wait_ge(ln_done, QB)
        sp.dma_start(ln_g[:, :], ln2_g[0].partition_broadcast(P)).then_inc(ln_in, 16)
        sp.dma_start(ln_b[:, :], ln2_b[0].partition_broadcast(P)).then_inc(ln_in, 16)
        with sp.Fori(0, CHUNKS - 2) as c:
            for slot in range(CHUNK):
                load_w(slot, c + (UP_USE[slot] + 2), columns(w_up, (c * CHUNK + (2 * CHUNK + slot)) * P))
            for slot in range(CHUNK):
                load_row(slot, c + (ROW_OUT + 1), w_down[0, bass.ds((c * CHUNK + (CHUNK + slot)) * P, P), :])
        for slot in range(CHUNK):
            load_row(slot, ROW_OUT + CHUNKS - 1, w_down[0, ((CHUNKS - 1) * CHUNK + slot) * P:((CHUNKS - 1) * CHUNK + slot + 1) * P, :])
        for t in range(QB):
            sp.wait_ge(ln_done, QB + t + 1)
            sp.dma_start(out[0, t * P:(t + 1) * P, :], acc[:, t, :]).then_inc(stored, 16)
        sp.wait_ge(stored, 16 * QB)

    @block.gpsimd
    def _(pool):
        pool.memset(ident[:, :], 0.0).then_inc(pool_step, 1)
        pool.wait_ge(pool_step, 1)
        pool.affine_select(out=ident[:, :], in_=ident[:, :], pattern=[[-1, P]], compare_op=ALU.not_equal,
                           fill=1.0, base=0, channel_multiplier=1).then_inc(const_ready, 1)
        pool.memset(eps[:, :], LN_EPS).then_inc(const_ready, 1)
        pool.memset(seen[:, :], 1.0).then_inc(pool_step, 1)
        for kind in range(2):
            pool.memset(cx[kind][:, :, :, CB - 1:CB], 0.0).then_inc(pool_step, 1)
        pool.wait_ge(pool_step, 2)
        pool.affine_select(out=seen[:, :], in_=seen[:, :], pattern=[[0, 1]], compare_op=ALU.is_ge,
                           fill=0.0, base=-(CMP_LEN - 1), channel_multiplier=1).then_inc(const_ready, 1)

        pool.wait_ge(pos_ready, 1)
        pool.wait_ge(kc_ready, 3)
        pool.wait_ge(product_taken[0], 1)
        pool.wait_ge(vc_ready, 3)
        pool.wait_ge(product_taken[1], 1)
        for kind in range(2):
            for g in range(KV):
                seq = kcs[2 * kind + g][:, :].rearrange("p (c t two) -> p two t c", t=CT // 2, two=2)
                for late in range(2):
                    rows = slice(late * CT // 2, (late + 1) * CT // 2)
                    pos = posT[:, kind * CT + late * CT // 2:kind * CT + (late + 1) * CT // 2]
                    pool.tensor_tensor(cx[kind][:, rows, g, 0:CB - 1], seq[:, 0, :, late:late + CB - 1],
                                       pos.unsqueeze(2).to_broadcast([P, CT // 2, CB - 1]),
                                       ALU.add).then_inc(cx_ready, 1)

        pool.wait_ge(product_done[0], GATE_USE[0])
        pool.iota(t_swa[:, :], [[-1, 2 * P]], base=P, channel_multiplier=1,
                  allow_small_or_imprecise_dtypes=True).then_inc(masks_ready, 1)
        pool.iota(t_slc[:, :], [[-1, SEQ + P]], base=SEQ, channel_multiplier=1,
                  allow_small_or_imprecise_dtypes=True).then_inc(masks_ready, 1)
        pool.iota(t_win[:, :], [[-1, NSA_WINDOW + P]], base=NSA_WINDOW, channel_multiplier=1,
                  allow_small_or_imprecise_dtypes=True).then_inc(masks_ready, 1)
        pool.memset(t_cmp[:, :, :], 0.0).then_inc(masks_ready, 1)
        pool.wait_ge(masks_ready, 4)
        for t, width, back in ((t_swa, 2 * P, P), (t_slc, SEQ + P, SEQ), (t_win, NSA_WINDOW + P, NSA_WINDOW)):
            pool.affine_select(out=t[:, :], in_=t[:, :], pattern=[[-1, width]], compare_op=ALU.is_ge,
                               fill=MASKED, base=back, channel_multiplier=1).then_inc(masks_ready, 1)
        pool.affine_select(out=t_cmp[:, :, :], in_=t_cmp[:, :, :], pattern=[[P, QB], [-CMP_STRIDE, CB]],
                           compare_op=ALU.is_ge, fill=MASKED, base=-(CMP_LEN - 1),
                           channel_multiplier=1).then_inc(masks_ready, 1)
        pool.wait_ge(masks_ready, 8)
        for t, width in ((t_swa, 2 * P), (t_win, NSA_WINDOW + P)):
            pool.affine_select(out=t[:, :], in_=t[:, :], pattern=[[1, width]], compare_op=ALU.is_gt,
                               fill=MASKED, base=0, channel_multiplier=-1).then_inc(masks_ready, 1)

        for u in units:
            p = probs(u)
            for part, segs in enumerate(u["parts"]):
                pool.wait_ge(scale_ready, u["part0"] + part + 1)
                for s in segs:
                    row = p[:, s["r"], s["at"]:s["at"] + s["keys"]]
                    pool.tensor_scalar(row, row, row_s[:, u["number"] % 2, s["column"]:s["column"] + 1], 1.0,
                                       ALU.mult, ALU.mult).then_inc(probs_ready, 1)

        for j in range(KT):
            pool.wait_ge(gated, j * 2 + 2)
            pool.tensor_tensor(merged[:, j, :], sg_a[:, :], sg_b[:, :], ALU.add).then_inc(merged_ready, 1)

        def norm_affine(t, count, done):
            pool.wait_ge(normed, count + 1)
            pool.tensor_tensor(acc[:, t, :], acc[:, t, :], ln_g[:, :], ALU.mult).then_inc(ln_scaled, 1)
            pool.wait_ge(ln_scaled, count + 1)
            pool.tensor_tensor(acc[:, t, :], acc[:, t, :], ln_b[:, :], ALU.add).then_inc(ln_done, 1)

        pool.wait_ge(ln_in, 32)
        for t in range(QB):
            norm_affine(t, t, ln_done)
        for t in range(QB):
            pool.wait_ge(h_turned, t + 1)
            pool.tensor_scalar(acc[:, t, :], acc[:, t, :], ALPHA, 1.0, ALU.mult, ALU.mult).then_inc(residual_ready, 1)

        with pool.Fori(0, CHUNKS) as c:
            for slot in range(CHUNK):
                pool.wait_ge(relu_ready[slot], c + 1)
                pool.wait_ge(ul_ready[slot], c + 1)
                pool.tensor_tensor(usq[slot][:, :], relu[slot][:, :], relu[slot][:, :],
                                   ALU.mult).then_inc(usq_ready[slot], 1)
        pool.wait_ge(ln_in, 64)
        for t in range(QB):
            norm_affine(t, t + QB, ln_done)

    @block.scalar
    def _(act):
        def split_x(n, slot, tile):
            act.wait_ge(x_turned[slot], n + 1)
            act.activation(xh[:, :, bass.ds(tile * P, P)], tiles(4 + 2 * slot), ACT.Copy).then_inc(xh_ready[slot], 1)

        def split_w(slot, n):
            act.wait_ge(w_loaded[slot], (n + 1) * 16)
            at_least(act, product_done[slot], n)
            act.activation(w_hi[slot][:, :, :], w_raw[slot][:, :, :], ACT.Copy).then_inc(w_hi_ready[slot], 1)

        split_x(0, 0, 0)
        split_x(0, 1, 1)
        with act.Fori(1, QB // 2) as i:
            for slot in range(2):
                split_x(i, slot, i * 2 + slot)
        split_w(0, 0)
        split_w(1, 0)
        split_w(0, 1)
        act.wait_ge(product_done[0], 1)
        for g in range(KV):
            rows = slice(g * HEAD_DIM, (g + 1) * HEAD_DIM)
            act.activation(kcs[g][0:HEAD_DIM, :], wide(0)[rows, :], ACT.Copy).then_inc(kc_ready, 1)
            act.activation(kcs[g][HEAD_DIM:P, 0:SEQ - 1], wide(0)[rows, 1:SEQ],
                           ACT.Copy).then_inc(kc_ready if g == 0 else product_taken[0], 1)
        with act.Fori(0, 4) as j:
            split_w(1, j + 1)
            act.wait_ge(product_done[0], j + 2)
            act.activation(qa[:, j, :], wide(0), ACT.Copy).then_inc(product_taken[0], 1)
            split_w(0, j + 2)
        act.wait_ge(hidden_done, 1)
        act.activation(g_in[:, :], ps[:, HIDDEN_BANK, :], ACT.Copy).then_inc(hidden_copied, 1)
        act.wait_ge(gelu_step, 3)
        act.activation(g_u[:, :], g_t[:, :], ACT.Tanh, scale=float(GELU_IN)).then_inc(tanh_done, 1)

        def keys_high(what, slot, n):
            act.wait_ge(product_done[slot], n + 1)
            for g in range(KV):
                rows = slice(g * HEAD_DIM, (g + 1) * HEAD_DIM)
                for to in range(2):
                    act.activation(k_hi[what][to * HEAD_DIM:(to + 1) * HEAD_DIM, g, :], wide(2 * slot)[rows, :],
                                   ACT.Copy).then_inc(kv_hi_ready, 1)

        def values_high(what, i):
            act.wait_ge(v_turned, i + 1)
            for g in range(KV):
                act.activation(v_hl[what][:, :, g, 0:HEAD_DIM], tiles(4)[:, :, g * HEAD_DIM:(g + 1) * HEAD_DIM],
                               ACT.Copy).then_inc(v_hi_ready, 1)

        def values_out(dst, slot, n):
            act.wait_ge(product_done[slot], n + 1)
            act.activation(dst[:, :], wide(2 * slot), ACT.Copy).then_inc(product_taken[slot], 1)

        split_w(1, 5)
        keys_high("slc", 0, 5)
        split_w(0, 6)
        act.wait_ge(cmp_done, 1)
        act.activation(k_hi["cmp"][:, :, :], ps[:, SMALL_BANK, 0:P].rearrange("p (g c) -> p g c", g=KV),
                       ACT.Copy).then_inc(cmp_hi_ready, 1)
        act.activation(v_hl["cmp"][0:CB, 0, :, 0:HEAD_DIM],
                       ps[0:CB, SMALL_BANK, P:2 * P].rearrange("p (g d) -> p g d", g=KV),
                       ACT.Copy).then_inc(cmp_hi_ready, 1)
        values_out(vT, 1, 5)
        split_w(1, 6)
        keys_high("win", 0, 6)
        values_high("slc", 0)
        split_w(0, 7)
        values_out(vT, 1, 6)
        split_w(1, 7)
        keys_high("swa", 0, 7)
        values_high("win", 1)
        split_w(0, 8)
        values_out(vT, 1, 7)
        values_out(gaT, 0, 8)
        values_high("swa", 2)
        act.wait_ge(v_turned, 4)
        act.activation(gate[:, :, :], tiles(4)[:, :, 0:BRANCHES * HEADS], ACT.Sigmoid).then_inc(gate_ready, 1)

        def stage_queries(u):
            step = u["step"]
            at_least(act, scores_done, q_free[step])
            for r in range(R):
                rows = slice((r % 2) * HEAD_DIM, (r % 2 + 1) * HEAD_DIM)
                act.activation(q_st[step % 2][rows, r, :],
                               heads_out(u)[rows, 2 * u["g"] + r // 2, u["qb"] * P:(u["qb"] + 1) * P],
                               ACT.Copy, scale=query_scale(u, r)).then_inc(q_hi_ready, 1)

        def exps(u, part):
            p = probs(u)
            for s in u["parts"][part]:
                n = u["number"] % 2
                c = s["column"]
                act.wait_ge(row_max, s["number"] + 1)
                row = p[:, s["r"], s["at"]:s["at"] + s["keys"]]
                act.activation(row, row, ACT.Exp, scale=-1.0, bias=m_neg[:, n, c:c + 1],
                               accum_out=row_l[:, n, c:c + 1]).then_inc(exp_done, 1)
            if u["kind"] == "swa":
                for s in u["parts"][part]:
                    n, c = u["number"] % 2, s["column"]
                    h = R * u["g"] + s["r"]
                    act.activation(sink_e[:, n, c:c + 1], sink_row[:, h:h + 1], ACT.Exp,
                                   bias=m_neg[:, n, c:c + 1]).then_inc(sink_exp, 1)

        def turned_high(u, i):
            t = u["block0"] + i
            rows = CB if u["blocks"][i][0] == "cmp" else P
            act.wait_ge(probs_turned, t + 1)
            at_least(act, values_done, t - PT_RING + 1)
            act.activation(pt_hi[t % PT_RING][0:rows, :, :], ps[0:rows, TURN[t % 3], :].rearrange("p (r q) -> p r q", r=R),
                           ACT.Copy).then_inc(pt_hi_ready, 1)

        def outputs_low(u):
            act.wait_ge(values_done, u["block0"] + len(u["blocks"]))
            at_least(act, o_ready, 2 * u["step"])
            act.activation(o_sum[0:HEAD_DIM, :, :],
                           ps[HEAD_DIM:P, OUT_BANK, :].rearrange("p (r q) -> p r q", r=R),
                           ACT.Copy).then_inc(o_low_ready, 1)

        act.wait_ge(product_done[0], GATE_USE[0])
        act.wait_ge(sinks_in, 16)
        for what, u, i in in_turn(order, {"exp": ("part", 0.6), "high": ("block", 0.5), "stage": ("step", -3.2),
                                          "outputs": ("step", 2.3)}):
            if what == "stage":
                stage_queries(u)
            elif what == "exp":
                exps(u, i)
            elif what == "high":
                turned_high(u, i)
            else:
                outputs_low(u)

        act.wait_ge(o_ready, 2 * STEPS)
        for tile in range(2):
            split_x(QB // 2, tile, tile)
        with act.Fori(1, QB // 2) as i:
            for slot in range(2):
                split_x(i + QB // 2, slot, i * 2 + slot)
        act.activation(oah[:, :, :], qa[:, :, :], ACT.Copy).then_inc(o_split_hi, 1)
        act.activation(obh[:, :, :], qb_[:, :, :], ACT.Copy).then_inc(o_split_hi, 1)
        split_w(0, GATE_USE[0])

        def merge(j):
            split_w(1, j + GATE_USE[1])
            act.wait_ge(wb_loaded, j * 32 + 32)
            at_least(act, y_done[1], j)
            act.activation(wb_hi[:, :, :], wb_raw[:, :, :], ACT.Copy).then_inc(wb_hi_ready, 1)
            for slot, sg, use in ((0, sg_a, j + GATE_USE[0]), (1, sg_b, j + GATE_USE[1])):
                act.wait_ge(product_done[slot], use + 1)
                at_least(act, merged_ready, j)
                act.activation(sg[:, :], wide(2 * slot), ACT.Sigmoid).then_inc(sg_ready[slot], 1)
                if slot == 0:
                    split_w(0, j + (GATE_USE[0] + 1))

        merge(0)
        with act.Fori(1, KT) as j:
            merge(j)

        def split_row(slot, n, hi):
            act.wait_ge(row_loaded[slot], (n + 1) * 16)
            act.activation(hi, row_raw[slot][:, :], ACT.Copy).then_inc(row_hi_ready[slot], 1)

        def stage_merged(slot, n, tile):
            at_least(act, mix_done[slot], n)
            act.activation(mst_hi[slot][:, :, :], merged[:, :, bass.ds(tile * P, P)],
                           ACT.Copy).then_inc(mst_hi_ready[slot], 1)

        def deviation(slot, count):
            act.wait_ge(var_ready, count + 1)
            act.activation(rstd[:, slot, 0:1], mv[:, slot, 1:2], ACT.Sqrt, bias=eps[:, :]).then_inc(std_ready, 1)

        act.wait_ge(merged_ready, KT)
        act.wait_ge(y_done[1], KT)
        stage_merged(0, 0, 0)
        for kt in range(KT):
            split_row(kt % 2, kt // 2, wo_hi[:, kt, :])
        stage_merged(1, 0, 1)
        with act.Fori(0, QB // 2 - 1) as i:
            for slot in range(2):
                deviation(slot, i * 2 + slot)
                stage_merged(slot, i + 1, (i + 1) * 2 + slot)
        for slot in range(2):
            deviation(slot, QB - 2 + slot)
        split_w(1, UP_USE[1])
        act.wait_ge(mix_done[1], QB // 2)
        for t in range(QB):
            act.wait_ge(h_turned, t + 1)
            act.activation(hh[:, :, t * P:(t + 1) * P], tiles(4 + 2 * (t % 2)), ACT.Copy).then_inc(hh_ready, 1)

        def relu_out(slot, c):
            act.wait_ge(product_done[slot], c + (UP_USE[slot] + 1))
            at_least(act, usq_ready[slot], c)
            act.activation(relu[slot][:, :], wide(2 * slot), ACT.Relu).then_inc(relu_ready[slot], 1)

        def hidden_high(slot, c, parity):
            act.wait_ge(usq_ready[slot], c + 1)
            at_least(act, down_done, (c - 1) * 16)
            act.activation(uh[parity][:, slot, :], usq[slot][:, :], ACT.Copy).then_inc(uh_ready[slot], 1)

        def down_weights(c):
            for slot in range(CHUNK):
                act.wait_ge(row_loaded[slot], (c + (ROW_OUT + 1)) * 16)
                at_least(act, down_done, c * 16)
                act.activation(wd_hi[slot][:, :], row_raw[slot][:, :], ACT.Copy).then_inc(row_hi_ready[slot], 1)

        def mlp_step(c, parity, ups, splits):
            down_weights(c)
            if ups:
                for slot in range(CHUNK):
                    if splits:
                        split_w(slot, c + (UP_USE[slot] + 2))
                    relu_out(slot, c + 1)
                for slot in range(CHUNK):
                    hidden_high(slot, c + 1, 1 - parity)

        for slot in range(CHUNK):
            split_w(slot, UP_USE[slot] + 1)
            relu_out(slot, 0)
        for slot in range(CHUNK):
            hidden_high(slot, 0, 0)
        mlp_step(0, 0, True, True)
        mlp_step(1, 1, True, True)
        with act.Fori(1, CHUNKS // 2 - 1) as i:
            mlp_step(i * 2, 0, True, True)
            mlp_step(i * 2 + 1, 1, True, True)
        mlp_step(CHUNKS - 2, 0, True, False)
        mlp_step(CHUNKS - 1, 1, False, False)
        for t in range(QB):
            deviation(t % 2, QB + t)

    @block.vector
    def _(dve):
        def split_x(n, slot, tile):
            dve.wait_ge(xh_ready[slot], n + 1)
            cols = bass.ds(tile * P, P)
            dve.tensor_tensor(xl[:, :, cols], tiles(4 + 2 * slot), xh[:, :, cols],
                              ALU.subtract).then_inc(xl_ready[slot], 1)

        def split_w(slot, n):
            dve.wait_ge(w_hi_ready[slot], n + 1)
            dve.tensor_tensor(w_lo[slot][:, :, :], w_raw[slot][:, :, :], w_hi[slot][:, :, :],
                              ALU.subtract).then_inc(w_lo_ready[slot], 1)

        dve.wait_ge(pos_turned, 1)
        dve.tensor_copy(posT[:, :], ps[:, SMALL_BANK, 0:2 * CT]).then_inc(pos_ready, 1)
        split_x(0, 0, 0)
        split_x(0, 1, 1)
        with dve.Fori(1, QB // 2) as i:
            for slot in range(2):
                split_x(i, slot, i * 2 + slot)
        split_w(0, 0)
        split_w(1, 0)
        split_w(0, 1)
        dve.wait_ge(product_done[1], 1)
        for g in range(KV):
            rows = slice(g * HEAD_DIM, (g + 1) * HEAD_DIM)
            dve.tensor_copy(kcs[KV + g][0:HEAD_DIM, :], wide(2)[rows, :]).then_inc(vc_ready, 1)
            dve.tensor_copy(kcs[KV + g][HEAD_DIM:P, 0:SEQ - 1],
                            wide(2)[rows, 1:SEQ]).then_inc(vc_ready if g == 0 else product_taken[1], 1)
        with dve.Fori(0, 4) as j:
            split_w(1, j + 1)
            dve.wait_ge(product_done[1], j + 2)
            dve.tensor_copy(qb_[:, j, :], wide(2)).then_inc(product_taken[1], 1)
            split_w(0, j + 2)
        dve.wait_ge(hidden_copied, 1)
        dve.tensor_tensor(g_t[:, :], g_in[:, :], g_in[:, :], ALU.mult).then_inc(gelu_step, 1)
        dve.wait_ge(gelu_step, 1)
        dve.tensor_scalar(g_t[:, :], g_t[:, :], 0.044715, 1.0, ALU.mult, ALU.add).then_inc(gelu_step, 1)
        dve.wait_ge(gelu_step, 2)
        dve.tensor_tensor(g_t[:, :], g_t[:, :], g_in[:, :], ALU.mult).then_inc(gelu_step, 1)
        dve.wait_ge(tanh_done, 1)
        dve.tensor_scalar(g_u[:, :], g_u[:, :], 1.0, 0.5, ALU.add, ALU.mult).then_inc(gelu_step, 1)
        dve.wait_ge(gelu_step, 4)
        dve.tensor_tensor(g_out[:, :, :, :, :].rearrange("p a b g c -> p (a b g c)"), g_u[:, :], g_in[:, :],
                          ALU.mult).then_inc(gelu_ready, 1)

        def keys_low(what, slot, number):
            dve.wait_ge(kv_hi_ready, 4 * number + 4)
            for g in range(KV):
                rows = slice(g * HEAD_DIM, (g + 1) * HEAD_DIM)
                for to in range(2):
                    last = dve.tensor_tensor(k_lo[what][to * HEAD_DIM:(to + 1) * HEAD_DIM, g, :], wide(2 * slot)[rows, :],
                                             k_hi[what][rows, g, :], ALU.subtract)
                    last.then_inc(product_taken[slot] if g and to else kv_lo_ready, 1)

        def values_low(what, number):
            dve.wait_ge(v_hi_ready, 2 * number + 2)
            for g in range(KV):
                dve.tensor_tensor(v_hl[what][:, :, g, HEAD_DIM:P], tiles(4)[:, :, g * HEAD_DIM:(g + 1) * HEAD_DIM],
                                  v_hl[what][:, :, g, 0:HEAD_DIM], ALU.subtract).then_inc(v_lo_ready, 1)

        split_w(1, 5)
        keys_low("slc", 0, 0)
        split_w(0, 6)
        dve.wait_ge(cmp_hi_ready, 2)
        dve.tensor_tensor(k_lo["cmp"][:, :, :], ps[:, SMALL_BANK, 0:P].rearrange("p (g c) -> p g c", g=KV),
                          k_hi["cmp"][:, :, :], ALU.subtract).then_inc(cmp_lo_ready, 1)
        dve.tensor_tensor(v_hl["cmp"][0:CB, 0, :, HEAD_DIM:P],
                          ps[0:CB, SMALL_BANK, P:2 * P].rearrange("p (g d) -> p g d", g=KV),
                          v_hl["cmp"][0:CB, 0, :, 0:HEAD_DIM], ALU.subtract).then_inc(cmp_lo_ready, 1)
        split_w(1, 6)
        keys_low("win", 0, 1)
        values_low("slc", 0)
        split_w(0, 7)
        split_w(1, 7)
        keys_low("swa", 0, 2)
        values_low("win", 1)
        split_w(0, 8)
        values_low("swa", 2)
        dve.wait_ge(const_ready, 3)
        dve.wait_ge(sinks_in, 16)
        dve.tensor_scalar(sink_neg[:, :], sink_row[:, :], -1.0, None, ALU.mult).then_inc(consts_done, 1)
        dve.wait_ge(gate_ready, 1)
        cmp_gates = gate[:, 0, :].rearrange("p (h b) -> p h b", b=BRANCHES)[:, :, 0]
        dve.tensor_scalar(cmp_gates, cmp_gates, seen[:, :], None, ALU.mult).then_inc(consts_done, 1)
        dve.wait_ge(consts_done, 2)

        def stage_queries(u):
            step = u["step"]
            for r in range(R):
                rows = slice((r % 2) * HEAD_DIM, (r % 2 + 1) * HEAD_DIM)
                other = slice((1 - r % 2) * HEAD_DIM, (2 - r % 2) * HEAD_DIM)
                dve.wait_ge(q_hi_ready, R * step + r + 1)
                dve.scalar_tensor_tensor(
                    out=q_st[step % 2][other, r, :],
                    in0=heads_out(u)[rows, 2 * u["g"] + r // 2, u["qb"] * P:(u["qb"] + 1) * P],
                    scalar=query_scale(u, r), in1=q_st[step % 2][rows, r, :],
                    op0=ALU.mult, op1=ALU.subtract).then_inc(q_lo_ready, 1)

        def maxima(u, part):
            p = probs(u)
            at_least(dve, probs_turned, u["buffer_free"])
            dve.wait_ge(scores_done, u["part0"] + part + 1)
            row = score_row(u["part0"] + part)
            for s in u["parts"][part]:
                c, h = s["column"], R * u["g"] + s["r"]
                start = sink_neg[:, h:h + 1] if u["kind"] == "swa" else 3e38
                dve.tensor_tensor_reduce(out=p[:, s["r"], s["at"]:s["at"] + s["keys"]],
                                         in0=row[:, s["score0"]:s["score0"] + s["keys"]],
                                         in1=table(u, s), scale=slope(u, s), scalar=start, op0=ALU.add, op1=ALU.min,
                                         accum_out=m_neg[:, u["number"] % 2, c:c + 1]).then_inc(row_max, 1)

        def scales(u, part):
            n = u["number"] % 2
            segs = u["parts"][part]
            first, count = segs[0]["column"], len(segs)
            dve.wait_ge(exp_done, segs[-1]["number"] + 1)
            total = row_l[:, n, first:first + count]
            scale = row_s[:, n, first:first + count]
            if u["kind"] == "swa":
                dve.wait_ge(sink_exp, u["part0"] + part + 1)
                dve.tensor_tensor(total, total, sink_e[:, n, first:first + count], ALU.add).then_inc(scale_step, 1)
                dve.wait_ge(scale_step, u["part0"] + part + 1)
                dve.reciprocal(scale, total).then_inc(scale_ready, 1)
            else:
                dve.reciprocal(scale, total).then_inc(scale_step, 1)
                dve.wait_ge(scale_step, u["part0"] + part + 1)
                col = BRANCHES * (R * u["g"] + segs[0]["r"])
                gates = gate[:, u["qb"], col + 1:col + 2] if u["kind"] == "slc" else gate[:, u["qb"], col:col + 3:2]
                dve.tensor_tensor(scale, scale, gates, ALU.mult).then_inc(scale_ready, 1)

        def turned_low(u, i):
            t = u["block0"] + i
            rows = CB if u["blocks"][i][0] == "cmp" else P
            dve.wait_ge(pt_hi_ready, t + 1)
            dve.tensor_tensor(pt_lo[t % PT_RING][0:rows, :, :], ps[0:rows, TURN[t % 3], :].rearrange("p (r q) -> p r q", r=R),
                              pt_hi[t % PT_RING][0:rows, :, :], ALU.subtract).then_inc(pt_lo_ready, 1)

        def outputs(u):
            dve.wait_ge(o_low_ready, u["step"] + 1)
            both = ps[0:HEAD_DIM, OUT_BANK, :].rearrange("p (a b q) -> p b a q", b=2, q=P)
            low = o_sum[0:HEAD_DIM, :, :].rearrange("p (a b) q -> p b a q", b=2)
            for odd in range(2):
                dve.tensor_tensor(heads_out(u)[odd * HEAD_DIM:(odd + 1) * HEAD_DIM, 2 * u["g"]:2 * u["g"] + 2,
                                               u["qb"] * P:(u["qb"] + 1) * P],
                                  both[:, odd], low[:, odd], ALU.add).then_inc(o_ready, 1)

        dve.wait_ge(masks_ready, 10)
        for what, u, i in in_turn(order, {"maxima": ("part", 0.2), "scales": ("part", 2.2), "low": ("block", 1.5),
                                          "stage": ("step", -3.1), "outputs": ("step", 2.4)}):
            if what == "stage":
                stage_queries(u)
            elif what == "maxima":
                maxima(u, i)
            elif what == "scales":
                scales(u, i)
            elif what == "low":
                turned_low(u, i)
            else:
                outputs(u)

        for tile in range(2):
            split_x(QB // 2, tile, tile)
        with dve.Fori(1, QB // 2) as i:
            for slot in range(2):
                split_x(i + QB // 2, slot, i * 2 + slot)
        dve.wait_ge(o_split_hi, 2)
        dve.tensor_tensor(oal[:, :, :], qa[:, :, :], oah[:, :, :], ALU.subtract).then_inc(o_split_lo, 1)
        dve.tensor_tensor(obl[:, :, :], qb_[:, :, :], obh[:, :, :], ALU.subtract).then_inc(o_split_lo, 1)
        split_w(0, GATE_USE[0])
        with dve.Fori(0, KT) as j:
            split_w(1, j + GATE_USE[1])
            dve.wait_ge(wb_hi_ready, j + 1)
            dve.tensor_tensor(wb_lo[:, :, :], wb_raw[:, :, :], wb_hi[:, :, :], ALU.subtract).then_inc(wb_lo_ready, 1)
            split_w(0, j + (GATE_USE[0] + 1))
            for slot, sg, bank in ((0, sg_a, Y_A), (1, sg_b, Y_B)):
                dve.wait_ge(sg_ready[slot], j + 1)
                dve.wait_ge(y_done[slot], j + 1)
                dve.tensor_tensor(sg[:, :], sg[:, :], wide(bank), ALU.mult).then_inc(gated, 1)

        def split_row(slot, n, lo, hi):
            dve.wait_ge(row_hi_ready[slot], n + 1)
            dve.tensor_tensor(lo, row_raw[slot][:, :], hi, ALU.subtract).then_inc(row_lo_ready[slot], 1)

        def stage_merged(slot, n, tile):
            dve.wait_ge(mst_hi_ready[slot], n + 1)
            dve.tensor_tensor(mst_lo[slot][:, :, :], merged[:, :, bass.ds(tile * P, P)], mst_hi[slot][:, :, :],
                              ALU.subtract).then_inc(mst_lo_ready[slot], 1)

        STEPS_OF_NORM = 3

        def norm(t, slot, count):
            for half in range(2):
                dve.bn_stats(bn[:, slot, half, :], acc[:, t, half * HALF:(half + 1) * HALF]).then_inc(ln_step, 1)
            dve.wait_ge(ln_step, count * STEPS_OF_NORM + 2)
            dve.bn_aggr(mv[:, slot, :], bn[:, slot, :, :].rearrange("p a b -> p (a b)")).then_inc(var_ready, 1)
            dve.wait_ge(std_ready, count + 1)
            dve.reciprocal(rstd[:, slot, 1:2], rstd[:, slot, 0:1]).then_inc(ln_step, 1)
            dve.wait_ge(ln_step, count * STEPS_OF_NORM + 3)
            dve.tensor_scalar(acc[:, t, :], acc[:, t, :], mv[:, slot, 0:1], rstd[:, slot, 1:2],
                              ALU.subtract, ALU.mult).then_inc(normed, 1)

        def add_residual(slot, n, t):
            dve.wait_ge(xres_in[slot], (n + 1) * 16)
            dve.wait_ge(mix_done[slot], n + 1)
            dve.scalar_tensor_tensor(out=acc[:, t, :], in0=x_raw[slot][:, :], scalar=ALPHA, in1=wide(2 * slot),
                                     op0=ALU.mult, op1=ALU.add).then_inc(z_ready[slot], 1)
            dve.wait_ge(z_ready[slot], n + 1)

        stage_merged(0, 0, 0)
        for kt in range(KT):
            split_row(kt % 2, kt // 2, wo_lo[:, kt, :], wo_hi[:, kt, :])
        stage_merged(1, 0, 1)
        for i in range(QB // 2 - 1):
            for slot in range(2):
                add_residual(slot, i, i * 2 + slot)
                norm(i * 2 + slot, slot, i * 2 + slot)
                stage_merged(slot, i + 1, (i + 1) * 2 + slot)
        for slot in range(2):
            add_residual(slot, QB // 2 - 1, QB - 2 + slot)
            norm(QB - 2 + slot, slot, QB - 2 + slot)
        split_w(1, UP_USE[1])
        for t in range(QB):
            dve.wait_ge(hh_ready, t + 1)
            dve.tensor_tensor(hl[:, :, t * P:(t + 1) * P], tiles(4 + 2 * (t % 2)), hh[:, :, t * P:(t + 1) * P],
                              ALU.subtract).then_inc(hl_ready, 1)

        def hidden_low(slot, c, parity):
            dve.wait_ge(uh_ready[slot], c + 1)
            dve.tensor_tensor(ul[parity][:, slot, :], usq[slot][:, :], uh[parity][:, slot, :],
                              ALU.subtract).then_inc(ul_ready[slot], 1)

        def add_down(c, q):
            dve.wait_ge(down_done, c * 16 + (q + 1))
            cols = acc[:, q // 2, (q % 2) * HALF:(q % 2 + 1) * HALF]
            dve.tensor_tensor(cols, cols, ps[:, 4 + q % 4, :], ALU.add).then_inc(down_added, 1)

        def mlp_step(c, parity, ups, splits):
            for slot in range(CHUNK):
                split_row(slot, c + ROW_OUT, wd_lo[slot][:, :], wd_hi[slot][:, :])
            if splits:
                for slot in range(CHUNK):
                    split_w(slot, c + (UP_USE[slot] + 2))
            if ups:
                hidden_low(0, c + 1, 1 - parity)
            for q in range(16):
                if ups and q == 3:
                    hidden_low(1, c + 1, 1 - parity)
                add_down(c, q)

        for slot in range(CHUNK):
            dve.sem_inc(ul_ready[slot], 1)
        for slot in range(CHUNK):
            split_w(slot, UP_USE[slot] + 1)
        for slot in range(CHUNK):
            hidden_low(slot, 0, 0)
        dve.wait_ge(residual_ready, QB)
        with dve.Fori(0, CHUNKS // 2 - 1) as i:
            mlp_step(i * 2, 0, True, True)
            mlp_step(i * 2 + 1, 1, True, True)
        mlp_step(CHUNKS - 2, 0, True, False)
        mlp_step(CHUNKS - 1, 1, False, False)
        for t in range(QB):
            dve.wait_ge(down_added, 16 * (CHUNKS - 1) + 2 * t + 2)
            norm(t, t % 2, QB + t)

    @block.tensor
    def _(pe):
        def turn_x(n, slot):
            pe.wait_ge(x_in[slot], (n + 1) * 16)
            at_least(pe, xl_ready[slot], n)
            for k in range(KT):
                last = pe.transpose(tiles(4 + 2 * slot)[:, k, :], x_raw[slot][:, k * P:(k + 1) * P], ident[:, :])
            last.then_inc(x_turned[slot], 1)

        def product(slot, n, hi, lo, taken):
            pe.wait_ge(w_lo_ready[slot], n + 1)
            at_least(pe, product_taken[slot], taken)
            for k in range(KT):
                for p, (w, a) in enumerate(((w_hi, hi), (w_hi, lo), (w_lo, hi))):
                    for half in range(2):
                        last = pe.matmul(ps[:, 2 * slot + half, :], w[slot][:, k, :],
                                         a[:, k, half * HALF:(half + 1) * HALF],
                                         start=(k == 0 and p == 0), stop=(k == KT - 1 and p == 2))
            last.then_inc(product_done[slot], 1)

        pe.wait_ge(const_ready, 1)
        pe.wait_ge(small_in, 32)
        pe.transpose(ps[:, SMALL_BANK, 0:2 * CT], pos_nat[:, :], ident[0:2 * CT, 0:2 * CT]).then_inc(pos_turned, 1)
        turn_x(0, 0)
        pe.wait_ge(pos_ready, 1)
        turn_x(0, 1)
        with pe.Fori(1, QB // 2) as i:
            for slot in range(2):
                turn_x(i, slot)
        for slot in range(2):
            pe.wait_ge(xl_ready[slot], QB // 2)
        product(0, 0, xh, xl, 0)
        product(1, 0, xh, xl, 0)
        with pe.Fori(0, 4) as j:
            for slot in range(2):
                product(slot, j + 1, xh, xl, j + 1)

        pe.wait_ge(cx_ready, 8)
        pe.wait_ge(pool_step, 4)
        pe.wait_ge(cmp_w_in, 80)
        for kind in range(2):
            for f in range(2):
                col = (2 * kind + f) * P
                for t in range(CT):
                    last = pe.matmul(ps[:, HIDDEN_BANK, col:col + P], cw1[kind][:, t, f * P:(f + 1) * P],
                                     cx[kind][:, t, :, :].rearrange("p g c -> p (g c)"),
                                     start=(t == 0), stop=(t == CT - 1))
        last.then_inc(hidden_done, 1)
        product(0, 5, xh, xl, 5)
        pe.wait_ge(gelu_ready, 1)
        for f in range(2):
            pe.matmul(ps[:, SMALL_BANK, 0:P], cw2k[:, f, :, :].rearrange("p a d -> p (a d)"),
                      g_out[:, 0, f, :, :].rearrange("p g c -> p (g c)"), start=(f == 0), stop=(f == 1))
        for g in range(KV):
            for f in range(2):
                last = pe.matmul(ps[0:CB, SMALL_BANK, P + g * HEAD_DIM:P + (g + 1) * HEAD_DIM],
                                 g_out[:, 1, f, g, :], cw2v[:, f, :], start=(f == 0), stop=(f == 1))
        last.then_inc(cmp_done, 1)

        def turn_values(src, number, slot, n):
            pe.wait_ge(product_taken[slot], n + 1)
            at_least(pe, v_lo_ready, 2 * number)
            for k in range(QB):
                last = pe.transpose(tiles(4)[:, k, :], src[:, k * P:(k + 1) * P], ident[:, :])
            last.then_inc(v_turned, 1)

        product(1, 5, xh, xl, 5)
        product(0, 6, xh, xl, 6)
        turn_values(vT, 0, 1, 5)
        product(1, 6, xh, xl, 6)
        product(0, 7, xh, xl, 7)
        turn_values(vT, 1, 1, 6)
        product(1, 7, xh, xl, 7)
        product(0, 8, xh, xl, 8)
        turn_values(vT, 2, 1, 7)
        turn_values(gaT, 3, 0, 8)

        def in_banks(start, count):
            edges = [start] + [e for e in (HALF, 2 * HALF) if start < e < start + count] + [start + count]
            return [(a - start, b - a) for a, b in zip(edges, edges[1:])]

        def scores(u, part):
            number = u["part0"] + part
            row = score_row(number)
            pe.wait_ge(q_lo_ready, R * (u["step"] + 1))
            at_least(pe, row_max, scores_free[number])
            for s in u["parts"][part]:
                for c, n in in_banks(s["score0"], s["keys"]):
                    for k in (k_hi, k_lo):
                        last = pe.matmul(row[:, s["score0"] + c:s["score0"] + c + n],
                                         q_st[u["step"] % 2][:, s["r"], :],
                                         k[s["what"]][:, u["g"], s["key0"] + c:s["key0"] + c + n],
                                         start=(k is k_hi), stop=(k is k_lo))
            last.then_inc(scores_done, 1)

        def turn_probs(u, i):
            t = u["block0"] + i
            what, _, at = u["blocks"][i]
            rows = CB if what == "cmp" else P
            pe.wait_ge(probs_ready, u["seg0"] + len(u["segs"]))
            at_least(pe, pt_lo_ready, t - 2)
            for r in range(R):
                last = pe.transpose(ps[0:rows, TURN[t % 3], r * P:(r + 1) * P], probs(u)[:, r, at:at + rows],
                                    ident[:, :])
            last.then_inc(probs_turned, 1)

        def weigh_values(u, i):
            t = u["block0"] + i
            what, kb, _ = u["blocks"][i]
            rows = CB if what == "cmp" else P
            pe.wait_ge(pt_lo_ready, t + 1)
            first = u["first_of_step"] and i == 0
            if first:
                at_least(pe, o_ready, 2 * u["step"])
            last_block = u["last_of_step"] and i == len(u["blocks"]) - 1
            for n, pt in enumerate((pt_hi, pt_lo)):
                last = pe.matmul(ps[:, OUT_BANK, :], v_hl[what][0:rows, kb, u["g"], :],
                                 pt[t % PT_RING][0:rows, :, :].rearrange("p r q -> p (r q)"),
                                 start=(first and n == 0), stop=(last_block and n == 1))
            last.then_inc(values_done, 1)

        pe.wait_ge(kv_lo_ready, 9)
        pe.wait_ge(cmp_lo_ready, 2)
        pe.wait_ge(v_lo_ready, 6)
        pe.wait_ge(gate_ready, 1)
        pe.wait_ge(product_taken[0], GATE_USE[0])
        pe.wait_ge(product_taken[1], GATE_USE[1])
        for what, u, i in in_turn(order, {"scores": ("part", 0), "turn": ("block", 0), "weigh": ("block", 2.1)}):
            if what == "scores":
                scores(u, i)
            elif what == "turn":
                turn_probs(u, i)
            else:
                weigh_values(u, i)

        pe.wait_ge(o_ready, 2 * STEPS)
        pe.wait_ge(pt_lo_ready, BLOCKS)
        pe.wait_ge(row_max, SEGS)
        for slot in range(2):
            turn_x(QB // 2, slot)
        with pe.Fori(1, QB // 2) as i:
            for slot in range(2):
                turn_x(i + QB // 2, slot)
        for slot in range(2):
            pe.wait_ge(xl_ready[slot], QB)
        pe.wait_ge(o_split_lo, 2)

        def merge(j):
            at_least(pe, sg_ready[0], j)
            product(0, j + GATE_USE[0], xh, xl, 0)
            at_least(pe, sg_ready[1], j)
            product(1, j + GATE_USE[1], xh, xl, 0)
            pe.wait_ge(wb_lo_ready, j + 1)
            at_least(pe, gated, j * 2)
            for side, (bank, hi, lo) in enumerate(((Y_A, oah, oal), (Y_B, obh, obl))):
                for k in range(4):
                    for p, (w, a) in enumerate(((wb_hi, hi), (wb_hi, lo), (wb_lo, hi))):
                        for half in range(2):
                            last = pe.matmul(ps[:, bank + half, :], w[:, 4 * side + k, :],
                                             a[:, k, half * HALF:(half + 1) * HALF],
                                             start=(k == 0 and p == 0), stop=(k == 3 and p == 2))
                last.then_inc(y_done[side], 1)

        merge(0)
        with pe.Fori(1, KT) as j:
            merge(j)

        def mix(n, slot):
            pe.wait_ge(mst_lo_ready[slot], n + 1)
            at_least(pe, z_ready[slot], n)
            for k in range(KT):
                for p, (a, w) in enumerate(((mst_hi, wo_hi), (mst_hi, wo_lo), (mst_lo, wo_hi))):
                    for half in range(2):
                        last = pe.matmul(ps[:, 2 * slot + half, :], a[slot][:, k, :],
                                         w[:, k, half * HALF:(half + 1) * HALF],
                                         start=(k == 0 and p == 0), stop=(k == KT - 1 and p == 2))
            last.then_inc(mix_done[slot], 1)

        for slot in range(2):
            pe.wait_ge(sg_ready[slot], KT)
            pe.wait_ge(row_lo_ready[slot], KT // 2)
        mix(0, 0)
        mix(0, 1)
        with pe.Fori(1, QB // 2) as i:
            for slot in range(2):
                mix(i, slot)
        for t in range(QB):
            pe.wait_ge(ln_done, t + 1)
            at_least(pe, hl_ready, t - 1)
            for k in range(KT):
                last = pe.transpose(tiles(4 + 2 * (t % 2))[:, k, :], acc[:, t, k * P:(k + 1) * P], ident[:, :])
            last.then_inc(h_turned, 1)

        def up(c):
            for slot in range(CHUNK):
                at_least(pe, relu_ready[slot], c)
                product(slot, c + UP_USE[slot], hh, hl, 0)

        def down(c, parity):
            for slot in range(CHUNK):
                pe.wait_ge(row_lo_ready[slot], c + (ROW_OUT + 1))
                pe.wait_ge(ul_ready[slot], c + 2)
            for q in range(16):
                if q >= 4:
                    pe.wait_ge(down_added, c * 16 + (q - 3))
                else:
                    at_least(pe, down_added, c * 16 + (q - 3) if not isinstance(c, int) or c else 0)
                tile, half = q // 2, q % 2
                for f in range(CHUNK):
                    for p, (a, w) in enumerate(((uh, wd_hi), (uh, wd_lo), (ul, wd_hi))):
                        last = pe.matmul(ps[:, 4 + q % 4, :], a[parity][:, f, tile * P:(tile + 1) * P],
                                         w[f][:, half * HALF:(half + 1) * HALF],
                                         start=(f == 0 and p == 0), stop=(f == CHUNK - 1 and p == 2))
                last.then_inc(down_done, 1)

        pe.wait_ge(hl_ready, QB)
        for slot in range(2):
            pe.wait_ge(z_ready[slot], QB // 2)
        up(0)
        up(1)
        down(0, 0)
        up(2)
        down(1, 1)
        with pe.Fori(1, CHUNKS // 2 - 1) as i:
            up(i * 2 + 1)
            down(i * 2, 0)
            up(i * 2 + 2)
            down(i * 2 + 1, 1)
        up(CHUNKS - 1)
        down(CHUNKS - 2, 0)
        down(CHUNKS - 1, 1)

    ctx.close()


_INS = ["x", "w_in", "cmp_pos_k", "cmp_w1_k", "cmp_w2_k", "cmp_pos_v", "cmp_w1_v", "cmp_w2_v", "sink_logits",
        "w_branch_a", "w_branch_b", "w_out", "ln1_g", "ln1_b", "w_up", "w_down", "ln2_g", "ln2_b"]


def kernel(**inputs):
    import concourse.bacc as bacc
    from concourse.bass_utils import run_bass_kernel_spmd

    nc = bacc.Bacc("TRN2", target_bir_lowering=False, num_devices=1)
    arrays = {f"in_{name}": np.ascontiguousarray(inputs[name]) for name in _INS}
    args = [nc.dram_tensor(name, a.shape, mybir.dt.from_np(a.dtype), kind="ExternalInput").ap()
            for name, a in arrays.items()]
    args.append(nc.dram_tensor("out_h", (1, SEQ, D_MODEL), F32, kind="ExternalOutput").ap())
    layer(nc, *args)
    return run_bass_kernel_spmd(nc, [arrays], core_ids=[0]).results[0]["out_h"]
```

```python
from contextlib import ExitStack

import numpy as np
import concourse.bass as bass
from concourse import mybir

F32 = mybir.dt.float32
F32R = mybir.dt.float32r
ALU = mybir.AluOpType
ACT = mybir.ActivationFunctionType

P = 128
SEQ = 1024
D_MODEL = 1024
HEAD_DIM = 64
HEADS = 8
KV = 2
R = HEADS // KV
CMP_LEN = 32
CMP_STRIDE = 16
CMP_HIDDEN = 4 * HEAD_DIM
SWA_WINDOW = 128
NSA_WINDOW = 512
D_FF = 4 * D_MODEL
LN_EPS = 1e-5
MASKED = 2.0 ** 100
ALPHA = 2.0 ** 0.25
QB = SEQ // P
KT = D_MODEL // P
HALF = 512
CB = 64
CT = CMP_LEN * HEAD_DIM // P
BRANCHES = 3
CHUNK = 2
CHUNKS = D_FF // (CHUNK * P)

KVW = KV * HEAD_DIM
COL_QA = 0
COL_KC = HEADS * HEAD_DIM
COL_VC = COL_KC + KVW
COL_KS = COL_VC + KVW
COL_VS = COL_KS + KVW
COL_KW = COL_VS + KVW
COL_VW = COL_KW + KVW
COL_GA = COL_VW + KVW
COL_QB = COL_GA + BRANCHES * HEADS
COL_KB = COL_QB + HEADS * HEAD_DIM
COL_VB = COL_KB + KVW
COL_GATE_A = COL_VB + KVW
COL_GATE_B = COL_GATE_A + D_MODEL

SLOPES = [2.0 ** (-8.0 * (i + 1) / (2 * HEADS)) for i in range(2 * HEADS)]
SHIFTED_BY_POOL = QB - 1
GATES = 2 * D_MODEL // P
TURNS = {"swa": 1, "nsa": 3}
PT_RING = 4
EAGER = {"sums": 0.14, "stage_high": -0.22}
HANDOVER = 0.15
GELU_IN = (2.0 / np.pi) ** 0.5


def mixer(u):
    return "swa" if u["kind"] == "swa" else "nsa"


def at_least(engine, sem, count):
    if not (isinstance(count, int) and count <= 0):
        engine.wait_ge(sem, count)


def attention_units():
    units, step, part, seg, block = [], 0, 0, 0, 0
    for kind, g, qb in ([("swa", g, qb) for g in range(KV) for qb in range(QB)]
                        + [(kind, g, qb) for g in range(KV) for qb in range(QB) for kind in ("slc", "wc")]):
        u = {"kind": kind, "g": g, "qb": qb, "step": step, "number": len(units), "parts": [], "blocks": []}
        if kind == "swa":
            first = max(0, qb - SWA_WINDOW // P)
            keys = (qb + 1 - first) * P
            u["parts"] = [[{"r": r, "what": "swa", "key0": first * P, "keys": keys, "score0": 0,
                            "table0": 2 * P - keys, "at": 0}] for r in range(R)]
            u["blocks"] = [("swa", kb, (kb - first) * P) for kb in range(first, qb + 1)]
        elif kind == "slc":
            keys = (qb + 1) * P
            u["parts"] = [[{"r": r, "what": "slc", "key0": 0, "keys": keys, "score0": 0,
                            "table0": SEQ + P - keys, "at": 0}] for r in range(R)]
            u["blocks"] = [("slc", kb, kb * P) for kb in range(qb + 1)]
        else:
            first = max(0, qb - NSA_WINDOW // P)
            keys = (qb + 1 - first) * P
            width = NSA_WINDOW + P
            u["parts"] = [[{"r": r, "what": "cmp", "key0": 0, "keys": CB, "score0": keys,
                            "table0": 0, "at": width},
                           {"r": r, "what": "win", "key0": first * P, "keys": keys, "score0": 0,
                            "table0": width - keys, "at": 0}] for r in range(R)]
            u["blocks"] = [("win", kb, (kb - first) * P) for kb in range(first, qb + 1)] + [("cmp", 0, width)]
        u["part0"], u["seg0"], u["block0"] = part, seg, block
        part += len(u["parts"])
        for segs in u["parts"]:
            for s in segs:
                s["number"], s["column"] = seg, seg - u["seg0"]
                seg += 1
        block += len(u["blocks"])
        u["segs"] = [s for segs in u["parts"] for s in segs]
        u["first_of_step"] = kind != "wc"
        u["last_of_step"] = kind != "slc"
        step += u["last_of_step"]
        units.append(u)
    return units, step, seg, block


def attention_orders(units, which, q_free, score_free, block_free):
    def cost(kind, u, i):
        if kind in ("scores", "maxima", "exp", "scale"):
            keys = [s["keys"] for s in u["parts"][i]]
            return {"scores": sum(2 * max(0.11, n / 2400) for n in keys), "maxima": sum(0.07 + n / 960 for n in keys),
                    "exp": sum(0.31 + n / 1200 for n in keys), "scale": sum(0.25 + n / 1200 for n in keys)}[kind]
        return {"stage_high": 0.85, "stage_low": 0.85, "sinks": 0.1, "sums": 0.08, "turn": 0.43, "high": 0.5,
                "low": 0.62, "weigh": 0.43, "out_low": 0.5, "out": 0.7, "split_high": 1.0, "split_low": 1.15,
                "branch_high": 1.0, "branch_low": 1.15,
                "gate_piece": 1.3, "gate_out": 1.1}[kind]

    engines = {"pe": ("weigh", "turn", "scores", "gate_piece"),
               "act": ("split_high", "gate_out", "out_low", "high", "exp", "stage_high"),
               "dve": ("split_low", "out", "low", "sums", "stage_low", "maxima"),
               "pool": ("scale", "sinks")}
    if which == "nsa":
        engines = {"pe": ("turn", "weigh", "scores"),
                   "act": ("out_low", "high", "exp", "stage_high", "branch_high"),
                   "dve": ("out", "low", "sums", "maxima", "stage_low", "branch_low"), "pool": ("scale",)}
    steps = [u for u in units if u["first_of_step"]]
    parts = [(u, i) for u in units for i in range(len(u["parts"]))]
    blocks = [(u, i) for u in units for i in range(len(u["blocks"]))]
    swa = [u for u in units if u["kind"] == "swa"]
    ends_of_step = [u for u in units if u["last_of_step"]]
    work = {"stage_high": [(u, 0) for u in steps], "stage_low": [(u, 0) for u in steps],
            "out_low": [(u, 0) for u in ends_of_step], "out": [(u, 0) for u in ends_of_step], "sinks": [(u, 0) for u in swa],
            **{k: parts for k in ("scores", "maxima", "exp", "sums", "scale")},
            **{k: blocks for k in ("turn", "high", "low", "weigh")}, "gate_piece": [(None, n) for n in range(GATES * KT)],
            "gate_out": [(None, b) for b in range(GATES)],
            "split_high": [(None, b) for b in range(GATES + 2)], "split_low": [(None, b) for b in range(GATES + 2)]}
    turns = TURNS[which]
    if which == "swa":
        ends = {kind: [0.0] * (2 if kind.startswith("split") else 0) for kind in work}
        work = {kind: [x for x in items if x[0] is None or x[0]["kind"] == "swa"] for kind, items in work.items()}
    else:
        ends = {kind: [0.0] * sum(x[0] is None or x[0]["kind"] == "swa" for x in items) for kind, items in work.items()}
        work.update(branch_high=[(None, 0)], branch_low=[(None, 0)])
        ends.update(branch_high=[], branch_low=[])

    def needs(kind, u, i, n):
        if u is None:
            u = {"number": 0, "part0": 0, "parts": [], "block0": 0, "blocks": [], "step": 0, "kind": None}
        return {"stage_high": {"scores": q_free[min(n, len(q_free) - 1)]}, "stage_low": {"stage_high": n + 1},
                "scores": {"stage_low": u["step"] + 1, "maxima": score_free[min(n, len(score_free) - 1)]},
                "maxima": {"scores": n + 1, "turn": block_free[u["number"]]},
                "sinks": {"turn": block_free[u["number"]]},
                "exp": {"maxima": n + 1, "sinks": u["step"] + 1 if u["kind"] == "swa" else 0},
                "sums": {"exp": n + 1}, "scale": {"sums": n + 1},
                "turn": {"scale": u["part0"] + len(u["parts"]), "low": n + 1 - turns}, "high": {"turn": n + 1, "weigh": n + 1 - PT_RING},
                "low": {"high": n + 1}, "weigh": {"low": n + 1, "out": u["step"]},
                "branch_high": {}, "branch_low": {"branch_high": 1},
                "split_high": {"gate_piece": KT * (n - 1)}, "split_low": {"split_high": n + 1},
                "gate_piece": {"split_low": n // KT + 1, "gate_out": n // KT - 1}, "gate_out": {"gate_piece": KT * (n + 1)},
                "out_low": {"weigh": u["block0"] + len(u["blocks"]), "out": n}, "out": {"out_low": n + 1}}[kind]

    free = dict.fromkeys(engines, 0.0)
    orders = {engine: [] for engine in engines}
    while any(len(ends[kind]) < len(work[kind]) for kind in work):
        ready = []
        for engine, kinds in engines.items():
            for rank, kind in enumerate(kinds):
                n = len(ends[kind])
                if n == len(work[kind]):
                    continue
                need = needs(kind, *work[kind][n], n)
                if all(len(ends[k]) >= count for k, count in need.items()):
                    start = max([free[engine]] + [ends[k][count - 1] + HANDOVER for k, count in need.items() if count > 0])
                    ready.append((start - EAGER.get(kind, 0.0), rank, engine, kind, n, start))
        _, _, engine, kind, n, start = min(ready)
        u, i = work[kind][n]
        free[engine] = start + cost(kind, u, i)
        ends[kind].append(free[engine])
        orders[engine].append((kind, u, i))
    return orders


def layer(nc, x, w_in, pos_k, w1_k, w2_k, pos_v, w1_v, w2_v, sinks, w_branch_a, w_branch_b, w_out,
          ln1_g, ln1_b, w_up, w_down, ln2_g, ln2_b, out):
    ctx = ExitStack()
    kb_ = 1024
    base = 16512

    def sb(name, at, shape, dt=F32):
        return nc.alloc_sbuf_tensor_at(name, shape, dt, offset=base + int(at * kb_))

    def sem(name):
        return ctx.enter_context(nc.semaphore(name))

    ident = sb("ident", 0, [P, P])
    sink_row = sb("sink_row", 0.5625, [P, HEADS])
    sink_neg = sb("sink_neg", 0.59375, [P, HEADS])
    eps = sb("eps", 0.625, [P, 1])
    bn = sb("bn", 0.75, [P, 2, 2, 6])
    mv = sb("mv", 0.875, [P, 2, 2])
    rstd = sb("rstd", 0.9375, [P, 2, 2])
    seen = sb("seen", 1.0, [P, 1])
    posT = sb("posT", 1.125, [P, 2 * CT])
    pos_nat = sb("pos_nat", 1.25, [2 * CT, P])
    qa = sb("qa", 2, [P, 4, SEQ])
    qb_ = sb("qb", 18, [P, 4, SEQ])
    merged = sb("merged", 2, [P, KT, SEQ])
    uh = [sb(f"uh{i}", 2 + 16 * i, [P, CHUNK, SEQ], F32R) for i in range(2)]
    ul = [sb(f"ul{i}", 10 + 16 * i, [P, CHUNK, SEQ], F32R) for i in range(2)]
    w_raw = [sb(f"w_raw{i}", 34 + 4 * i, [P, KT, P]) for i in range(2)]
    w_hi = [sb(f"w_hi{i}", 42 + 4 * i, [P, KT, P], F32R) for i in range(2)]
    w_lo = [sb(f"w_lo{i}", 50 + 4 * i, [P, KT, P], F32R) for i in range(2)]
    wd_last_hi = [sb(f"wd_last_hi{i}", 42 + 4 * i, [P, D_MODEL], F32R) for i in range(2)]
    wd_last_lo = [sb(f"wd_last_lo{i}", 50 + 4 * i, [P, D_MODEL], F32R) for i in range(2)]
    xh = sb("xh", 58, [P, KT, SEQ], F32R)
    xl = sb("xl", 90, [P, KT, SEQ], F32R)
    t_slc = sb("t_slc", 58, [P, SEQ + P])
    t_win = sb("t_win", 205, [P, NSA_WINDOW + P])
    t_cmp = sb("t_cmp", 66, [P, QB, CB])
    p_slc = sb("p_slc", 68, [P, R, SEQ])
    p_wc = sb("p_wc", 84, [P, R, NSA_WINDOW + 2 * P])
    pt_hi, pt_lo, q_st, o_sum, m_neg, row_l, row_s = {}, {}, {}, {}, {}, {}, {}
    for m, pt_at, q_at, small_at in (("swa", 2, 122, 137.5), ("nsa", 96, 112, 118)):
        pt_hi[m] = [sb(f"pt_hi_{m}{i}", pt_at + 4 * i, [P, R, P], F32R) for i in range(PT_RING)]
        pt_lo[m] = [sb(f"pt_lo_{m}{i}", pt_at + 2 + 4 * i, [P, R, P], F32R) for i in range(PT_RING)]
        q_st[m] = [sb(f"q_st_{m}{i}", q_at + 2 * i, [P, R, P], F32R) for i in range(2)]
        o_sum[m] = sb(f"o_sum_{m}", q_at + 4, [P, R, P])
        m_neg[m] = sb(f"m_neg_{m}", small_at, [P, 2, 8])
        row_l[m] = sb(f"row_l_{m}", small_at + 0.0625, [P, 2, 8])
        row_s[m] = sb(f"row_s_{m}", small_at + 0.125, [P, 2, 8])
    p_swa = [sb(f"p_swa{i}", 128 + 4.25 * i, [P, R, 2 * P + 1]) for i in range(2)]
    t_swa = sb("t_swa", 136.5, [P, 2 * P])
    wo_hi = sb("wo_hi", 58, [P, KT, D_MODEL], F32R)
    wo_lo = sb("wo_lo", 90, [P, KT, D_MODEL], F32R)
    hh = sb("hh", 58, [P, KT, SEQ], F32R)
    hl = sb("hl", 90, [P, KT, SEQ], F32R)
    kcs = [sb(f"kcs{i}", 122 + 4 * i, [P, SEQ]) for i in range(2 * KV)]
    cx = [sb(f"cx{i}", 138 + 8 * i, [P, CT, KV, CB]) for i in range(2)]
    cw1 = [sb(f"cw1{i}", 154 + 16 * i, [P, CT, CMP_HIDDEN]) for i in range(2)]
    cw2k = sb("cw2k", 186, [P, 2, 2, HEAD_DIM])
    cw2v = sb("cw2v", 187, [P, 2, HEAD_DIM])
    k_hi, k_lo, v_hl = {}, {}, {}
    for i, what in enumerate(("slc", "win", "swa")):
        k_hi[what] = sb(f"k_hi_{what}", 122 + 16 * i, [P, KV, SEQ], F32R)
        k_lo[what] = sb(f"k_lo_{what}", 130 + 16 * i, [P, KV, SEQ], F32R)
        v_hl[what] = sb(f"v_hl_{what}", 170 + 8 * i, [P, QB, KV, 2 * HEAD_DIM], F32R)
    oah = sb("oah", 122, [P, 4, SEQ], F32R)
    oal = sb("oal", 138, [P, 4, SEQ], F32R)
    obh = sb("obh", 154, [P, 4, SEQ], F32R)
    obl = sb("obl", 186, [P, 4, SEQ], F32R)
    gate_raw = [sb(f"gate_raw{i}", 170 + 4 * i, [P, SEQ]) for i in range(2)]
    sg = [sb(f"sg{i}", 170 + 8 * i, [P, 2, SEQ]) for i in range(2)]
    acc = sb("acc", 122, [P, QB, D_MODEL])
    mst_hi = [sb(f"mst_hi{i}", 154 + 4 * i, [P, KT, P], F32R) for i in range(2)]
    mst_lo = [sb(f"mst_lo{i}", 162 + 4 * i, [P, KT, P], F32R) for i in range(2)]
    relu = [sb(f"relu{i}", 154 + 4 * i, [P, SEQ]) for i in range(2)]
    usq = [sb(f"usq{i}", 162 + 4 * i, [P, SEQ]) for i in range(2)]
    row_raw = [sb(f"row_raw{i}", 170 + 4 * i, [P, D_MODEL]) for i in range(2)]
    ln_g = sb("ln_g", 178, [P, D_MODEL])
    ln_b = sb("ln_b", 182, [P, D_MODEL])
    wd_hi = [sb(f"wd_hi{i}", 186 + 4 * i, [P, D_MODEL], F32R) for i in range(2)]
    x_raw = [sb(f"x_raw{i}", 194 + 4 * i, [P, D_MODEL]) for i in range(2)]
    x_first = x_raw + [sb(f"x_first{i}", 170 + 4 * i, [P, D_MODEL]) for i in range(2)]
    g_in = sb("g_in", 194, [P, 2 * 2 * P])
    g_t = sb("g_t", 196, [P, 2 * 2 * P])
    g_u = sb("g_u", 198, [P, 2 * 2 * P])
    g_out = sb("g_out", 200, [P, 2, 2, KV, CB])
    vT = sb("vT", 194, [P, SEQ])
    gaT = sb("gaT", 198, [P, SEQ])
    wd_lo = [sb(f"wd_lo{i}", 194 + 4 * i, [P, D_MODEL], F32R) for i in range(2)]
    k_hi["cmp"] = sb("k_hi_cmp", 202, [P, KV, CB], F32R)
    k_lo["cmp"] = sb("k_lo_cmp", 202.5, [P, KV, CB], F32R)
    v_hl["cmp"] = sb("v_hl_cmp", 203, [P, 1, KV, 2 * HEAD_DIM], F32R)
    gate = sb("gate", 204, [P, QB, BRANCHES * HEADS])
    wo_raw = sb("wo_raw", 202, [P, D_MODEL])
    gates_dram = nc.dram_tensor("gates", [2, KT, P, SEQ], F32, kind="Internal").ap()
    sums2 = sb("sums2", 202, [P, QB, 2])
    mv2 = sb("mv2", 202.125, [P, QB, 2])
    rstd2 = sb("rstd2", 202.25, [P, QB, 3])
    squares = sb("squares", 203, [P, D_MODEL])

    ps = ctx.enter_context(nc.psum_tensor("ps", [P, 8, HALF], F32))

    def wide(bank):
        return ps[:, bank:bank + 2, :].rearrange("p a b -> p (a b)")

    def score_row(part):
        first, banks = score_bank[part]
        return ps[:, first:first + banks, :].rearrange("p a b -> p (a b)")

    def tiles(bank):
        return ps[:, bank:bank + 2, :].rearrange("p a (b c) -> p (a b) c", c=P)

    SCORE_BANKS = {"swa": (4, 5), "nsa": (0, 1, 2, 3)}
    TURN_BANKS = {"swa": (6,), "nsa": (4, 5, 6)}
    OUT_BANK = 7
    HIDDEN_BANK, SMALL_BANK = 6, 7
    POS_BANK = 3
    H_BANK = (4, 6, 2, 4, 6, 4, 6, 4)
    Y_BANK = ((0, 2), (4, 6))

    const_ready = sem("const_ready")
    window_masks_ready = sem("window_masks_ready")
    masks_ready = sem("masks_ready")
    fills_done = sem("fills_done")
    small_in = sem("small_in")
    sinks_in = sem("sinks_in")
    cmp_w_in = sem("cmp_w_in")
    x_in = [sem(f"x_in{i}") for i in range(4)]
    x_turned = [sem(f"x_turned{i}") for i in range(2)]
    xh_ready = [sem(f"xh_ready{i}") for i in range(2)]
    xl_ready = [sem(f"xl_ready{i}") for i in range(2)]
    w_loaded = [sem(f"w_loaded{i}") for i in range(2)]
    w_hi_ready = [sem(f"w_hi_ready{i}") for i in range(2)]
    w_lo_ready = [sem(f"w_lo_ready{i}") for i in range(2)]
    product_done = [sem(f"product_done{i}") for i in range(2)]
    product_taken = [sem(f"product_taken{i}") for i in range(2)]
    pos_turned = sem("pos_turned")
    pos_ready = sem("pos_ready")
    kc_ready = sem("kc_ready")
    vc_ready = sem("vc_ready")
    cx_ready = sem("cx_ready")
    hidden_done = sem("hidden_done")
    hidden_copied = sem("hidden_copied")
    tanh_done = sem("tanh_done")
    gelu_step = sem("gelu_step")
    gelu_ready = sem("gelu_ready")
    cmp_done = sem("cmp_done")
    cmp_hi_ready = sem("cmp_hi_ready")
    cmp_lo_ready = sem("cmp_lo_ready")
    kv_hi_ready = sem("kv_hi_ready")
    kv_lo_ready = sem("kv_lo_ready")
    v_turned = sem("v_turned")
    v_hi_ready = sem("v_hi_ready")
    v_lo_ready = sem("v_lo_ready")
    gate_ready = sem("gate_ready")
    gate_fixed = sem("gate_fixed")
    consts_done = sem("consts_done")
    q_hi_ready = sem("q_hi_ready")
    q_lo_ready = sem("q_lo_ready")
    scores_done = sem("scores_done")
    row_max = sem("row_max")
    exp_done = sem("exp_done")
    sinks_placed = sem("sinks_placed")
    scale_ready = sem("scale_ready")
    probs_ready = sem("probs_ready")
    probs_turned = sem("probs_turned")
    pt_hi_ready = sem("pt_hi_ready")
    pt_lo_ready = sem("pt_lo_ready")
    values_done = sem("values_done")
    o_low_ready = sem("o_low_ready")
    o_ready = sem("o_ready")
    oa_hi_ready = sem("oa_hi_ready")
    oa_lo_ready = sem("oa_lo_ready")
    ob_hi_ready = sem("ob_hi_ready")
    ob_lo_ready = sem("ob_lo_ready")
    ob_lo_late = sem("ob_lo_late")
    gate_copied = [sem(f"gate_copied{i}") for i in range(2)]
    gate_stored = [sem(f"gate_stored{i}") for i in range(2)]
    gates_back = [sem(f"gates_back{i}") for i in range(2)]
    wb_loaded = [sem(f"wb_loaded{i}") for i in range(2)]
    wb_hi_ready = [sem(f"wb_hi_ready{i}") for i in range(2)]
    wb_lo_ready = [sem(f"wb_lo_ready{i}") for i in range(2)]
    sg_ready = [sem(f"sg_ready{i}") for i in range(2)]
    y_done = [sem(f"y_done{i}") for i in range(2)]
    gated = [sem(f"gated{i}") for i in range(2)]
    merged_ready = sem("merged_ready")
    wo_loaded = sem("wo_loaded")
    wo_hi_ready = sem("wo_hi_ready")
    wo_lo_ready = sem("wo_lo_ready")
    row_loaded = [sem(f"row_loaded{i}") for i in range(2)]
    row_hi_ready = [sem(f"row_hi_ready{i}") for i in range(2)]
    row_lo_ready = [sem(f"row_lo_ready{i}") for i in range(2)]
    mst_head_hi = sem("mst_head_hi")
    mst_head_lo = sem("mst_head_lo")
    mst_hi_ready = [sem(f"mst_hi_ready{i}") for i in range(2)]
    mst_lo_ready = [sem(f"mst_lo_ready{i}") for i in range(2)]
    mix_done = [sem(f"mix_done{i}") for i in range(2)]
    xres_in = [sem(f"xres_in{i}") for i in range(2)]
    z_ready = [sem(f"z_ready{i}") for i in range(2)]
    ln_step = sem("ln_step")
    var_ready = sem("var_ready")
    std_ready = sem("std_ready")
    normed = sem("normed")
    ln_scaled = sem("ln_scaled")
    ln_done = sem("ln_done")
    ln_in = sem("ln_in")
    mean2_ready = sem("mean2_ready")
    var2_ready = sem("var2_ready")
    std2_ready = sem("std2_ready")
    rstd2_step = sem("rstd2_step")
    shift_ready = sem("shift_ready")
    normed2 = sem("normed2")
    scaled2 = sem("scaled2")
    out_ready = sem("out_ready")
    late_out_ready = sem("late_out_ready")
    h_turned = sem("h_turned")
    hh_ready = sem("hh_ready")
    hl_ready = sem("hl_ready")
    residual_ready = sem("residual_ready")
    relu_ready = [sem(f"relu_ready{i}") for i in range(2)]
    usq_ready = [sem(f"usq_ready{i}") for i in range(2)]
    uh_ready = [sem(f"uh_ready{i}") for i in range(2)]
    ul_ready = [sem(f"ul_ready{i}") for i in range(2)]
    down_done = sem("down_done")
    down_added = sem("down_added")
    stored = sem("stored")

    units, STEPS, SEGS, BLOCKS = attention_units()
    last_unit_of = {}
    for u in units:
        u["buffer"] = {"swa": f"swa{u['step'] % 2}", "slc": "slc", "wc": "wc"}[u["kind"]]
        before = last_unit_of.get(u["buffer"])
        u["buffer_free"] = before["block0"] + len(before["blocks"]) if before else 0
        last_unit_of[u["buffer"]] = u

    parts_of = [sum(len(u["parts"]) for u in units if u["step"] <= step) for step in range(STEPS)]
    q_free = [0, 0] + parts_of[:STEPS - 2]

    score_bank, scores_free = [], []
    for m, banks in SCORE_BANKS.items():
        holds, at_bank = [(0, 0)] * len(banks), 0
        for u in units:
            for p in u["parts"] if mixer(u) == m else []:
                wanted = -(-max(s["score0"] + s["keys"] for s in p) // HALF)
                at_bank = at_bank % len(banks) + at_bank % wanted
                at_bank %= len(banks)
                score_bank.append((banks[at_bank], wanted))
                scores_free.append(max(holds[at_bank:at_bank + wanted], key=lambda h: h[0]))
                holds[at_bank:at_bank + wanted] = [(len(scores_free), p[-1]["number"] + 1)] * wanted
                at_bank += wanted
    orders = {m: attention_orders(units, m, q_free, [parts for parts, _ in scores_free],
                                  [u["buffer_free"] for u in units]) for m in SCORE_BANKS}
    SWA_STEPS = sum(u["kind"] == "swa" for u in units)
    SWA_BLOCKS = sum(len(u["blocks"]) for u in units if u["kind"] == "swa")
    SWA_SEGS = sum(len(u["segs"]) for u in units if u["kind"] == "swa")

    def probs(u):
        return {"swa": p_swa[u["step"] % 2], "slc": p_slc, "wc": p_wc}[u["kind"]]

    def slope(u, s):
        return float(SLOPES[(0 if u["kind"] == "swa" else HEADS) + R * u["g"] + s["r"]])

    def turn_bank(u, t):
        return TURN_BANKS[mixer(u)][t % TURNS[mixer(u)]]

    def query_scale(u, r):
        return float(np.float32(-HEAD_DIM ** -0.5 / slope(u, {"r": r})))

    def table(u, s):
        if s["what"] == "cmp":
            return t_cmp[:, u["qb"], :]
        t = {"slc": t_slc, "win": t_win, "swa": t_swa}[s["what"]]
        return t[:, s["table0"]:s["table0"] + s["keys"]]

    def heads_out(u):
        return qb_ if u["kind"] == "swa" else qa

    W_COLS = ([COL_QB, COL_QB + P, COL_KB, COL_VB, COL_QB + 2 * P, COL_QB + 3 * P]
              + [col + j * P for j in range(KT) for col in (COL_GATE_A, COL_GATE_B)]
              + [COL_KC, COL_VC] + [COL_QA + j * P for j in range(4)] + [COL_KS, COL_VS, COL_KW, COL_VW, COL_GA])
    GATE_USE = 3
    NSA_USE = GATE_USE + KT
    UP_USE = ((len(W_COLS) + 1) // 2, len(W_COLS) // 2)

    def wait_taken(engine, slot, uses):
        if GATE_USE < uses <= NSA_USE:
            engine.wait_ge(gate_copied[slot], uses - GATE_USE)
        elif uses > 0:
            engine.wait_ge(product_taken[slot], uses if uses <= GATE_USE else uses - KT)

    def columns(w, col):
        return w[0, :, bass.ds(col, P)].rearrange("(k p) c -> p k c", p=P)

    block = ctx.enter_context(nc.Block())

    @block.sync
    def _(sp):
        def load_x(n, slot, tile, loaded, used):
            at_least(sp, used[slot], n)
            sp.dma_start(x_raw[slot][:, :], x[0, bass.ds(tile * P, P), :]).then_inc(loaded[slot], 16)

        def load_w(slot, n, src):
            at_least(sp, w_lo_ready[slot], n)
            sp.dma_start(w_raw[slot][:, :, :], src).then_inc(w_loaded[slot], 16)

        def load_row(slot, n, src):
            at_least(sp, row_lo_ready[slot], n)
            sp.dma_start(row_raw[slot][:, :], src).then_inc(row_loaded[slot], 16)

        def load_block(b):
            load_w(b % 2, b // 2, columns(w_in, W_COLS[b]))

        for t in range(QB):
            if t >= 4:
                sp.wait_ge(x_turned[t % 2], (t - 4) // 2 + 1)
            sp.dma_start(x_first[t % 4][:, :], x[0, t * P:(t + 1) * P, :]).then_inc(x_in[t % 4], 16)
            if t == 3:
                load_block(0)
                load_block(1)
                sp.dma_start(pos_nat[0:CT, :], pos_k[0].rearrange("(t l) d -> t (l d)", l=2)).then_inc(small_in, 16)
                sp.dma_start(pos_nat[CT:2 * CT, :], pos_v[0].rearrange("(t l) d -> t (l d)", l=2)).then_inc(small_in, 16)
        sp.dma_start(sink_row[:, :], sinks[0].partition_broadcast(P)).then_inc(sinks_in, 16)
        for b in range(2, 2 * GATE_USE + 2):
            load_block(b)

        def store_gates(j):
            for side in range(2):
                sp.wait_ge(gate_copied[side], j + 1)
                sp.dma_start(gates_dram[side, j, :, :], gate_raw[side][:, :]).then_inc(gate_stored[side], 16)

        for j in range(KT - 1):
            load_w(0, j + GATE_USE + 1, columns(w_in, (j + 1) * P + COL_GATE_A))
            load_w(1, j + GATE_USE + 1, columns(w_in, (j + 1) * P + COL_GATE_B))
            store_gates(j)
        for b in range(2 * NSA_USE, 2 * NSA_USE + 2):
            load_block(b)
        store_gates(KT - 1)
        for b in range(2 * NSA_USE + 2, 2 * NSA_USE + 4):
            load_block(b)
        sp.wait_ge(values_done, SWA_BLOCKS)
        for side in range(2):
            sp.wait_ge(gate_stored[side], 16 * KT)
        for kind, w1 in enumerate((w1_k, w1_v)):
            sp.dma_start(cw1[kind][:, :, :], w1[0].rearrange("(t l) d f -> (l d) t f", l=2)).then_inc(cmp_w_in, 16)
        for copy in range(2):
            sp.dma_start(cw2k[:, :, copy, :], w2_k[0].rearrange("(a f) d -> f a d", f=P)).then_inc(cmp_w_in, 16)
        sp.dma_start(cw2v[:, :, :], w2_v[0].rearrange("(a f) d -> f a d", f=P)).then_inc(cmp_w_in, 16)
        for b in range(2 * NSA_USE + 4, len(W_COLS)):
            load_block(b)

        def load_branches(j):
            slot = j % 2
            for side, w in enumerate((w_branch_a, w_branch_b)):
                sp.dma_start(w_raw[slot][:, 4 * side:4 * side + 4, :], columns(w, j * P)).then_inc(wb_loaded[slot], 16)

        def load_gates(j):
            for side in range(2):
                sp.dma_start(sg[j % 2][:, side, :], gates_dram[side, j, :, :]).then_inc(gates_back[j % 2], 16)

        for j in (1, 0):
            sp.wait_ge(w_lo_ready[j], UP_USE[j])
            load_branches(j)
        sp.wait_ge(values_done, BLOCKS)
        sp.wait_ge(probs_ready, SEGS)
        load_gates(0)
        load_gates(1)
        for j in range(KT):
            if 1 <= j < KT - 1:
                sp.wait_ge(wb_lo_ready[(j + 1) % 2], (j + 1) // 2)
                load_branches(j + 1)
            at_least(sp, wo_lo_ready, j)
            sp.dma_start(wo_raw[:, :], w_out[0, j * P:(j + 1) * P, :]).then_inc(wo_loaded, 16)
            if 1 <= j < KT - 1:
                sp.wait_ge(merged_ready, j)
                load_gates(j + 1)
        for slot in range(2):
            sp.wait_ge(wb_lo_ready[slot], KT // 2)
            load_w(slot, UP_USE[slot], columns(w_up, slot * P))
        sp.wait_ge(merged_ready, KT)
        sp.wait_ge(y_done[1], KT)
        load_x(0, 0, 0, xres_in, z_ready)
        load_x(0, 1, 1, xres_in, z_ready)
        sp.dma_start(ln_g[:, :], ln1_g[0].partition_broadcast(P)).then_inc(ln_in, 16)
        sp.dma_start(ln_b[:, :], ln1_b[0].partition_broadcast(P)).then_inc(ln_in, 16)
        with sp.Fori(1, QB // 2) as i:
            for slot in range(2):
                load_x(i, slot, i * 2 + slot, xres_in, z_ready)
        for slot in range(CHUNK):
            load_row(slot, 0, w_down[0, slot * P:(slot + 1) * P, :])
        for slot in range(CHUNK):
            load_w(slot, UP_USE[slot] + 1, columns(w_up, (CHUNK + slot) * P))
        sp.wait_ge(ln_done, QB)
        sp.dma_start(ln_g[:, :], ln2_g[0].partition_broadcast(P)).then_inc(ln_in, 16)
        sp.dma_start(ln_b[:, :], ln2_b[0].partition_broadcast(P)).then_inc(ln_in, 16)
        with sp.Fori(0, CHUNKS - 2) as c:
            for slot in range(CHUNK):
                load_w(slot, c + (UP_USE[slot] + 2), columns(w_up, (c * CHUNK + (2 * CHUNK + slot)) * P))
            for slot in range(CHUNK):
                load_row(slot, c + 1, w_down[0, bass.ds((c * CHUNK + (CHUNK + slot)) * P, P), :])
        for slot in range(CHUNK):
            load_row(slot, CHUNKS - 1, w_down[0, ((CHUNKS - 1) * CHUNK + slot) * P:((CHUNKS - 1) * CHUNK + slot + 1) * P, :])
        for t in range(QB):
            if t < SHIFTED_BY_POOL:
                sp.wait_ge(out_ready, t + 1)
            else:
                sp.wait_ge(late_out_ready, t - SHIFTED_BY_POOL + 1)
            sp.dma_start(out[0, t * P:(t + 1) * P, :], acc[:, t, :]).then_inc(stored, 16)
        sp.wait_ge(stored, 16 * QB)

    @block.gpsimd
    def _(pool):
        pool.memset(ident[:, :], 0.0).then_inc(fills_done, 1)
        pool.wait_ge(fills_done, 1)
        pool.affine_select(out=ident[:, :], in_=ident[:, :], pattern=[[-1, P]], compare_op=ALU.not_equal,
                           fill=1.0, base=0, channel_multiplier=1).then_inc(const_ready, 1)
        pool.memset(eps[:, :], LN_EPS).then_inc(const_ready, 1)
        pool.memset(seen[:, :], 1.0).then_inc(fills_done, 1)
        for kind in range(2):
            pool.memset(cx[kind][:, :, :, CB - 1:CB], 0.0).then_inc(fills_done, 1)
        pool.wait_ge(fills_done, 2)
        pool.affine_select(out=seen[:, :], in_=seen[:, :], pattern=[[0, 1]], compare_op=ALU.is_ge,
                           fill=0.0, base=-(CMP_LEN - 1), channel_multiplier=1).then_inc(const_ready, 1)

        for t, back in ((t_swa, P), (t_win, NSA_WINDOW)):
            pool.iota(t[:, :], [[-1, back + P]], base=back, channel_multiplier=1,
                      allow_small_or_imprecise_dtypes=True).then_inc(window_masks_ready, 1)
        for n, (t, back) in enumerate(((t_swa, P), (t_win, NSA_WINDOW))):
            pool.wait_ge(window_masks_ready, 2 + 2 * n)
            pool.affine_select(out=t[:, :], in_=t[:, :], pattern=[[-1, back + P]], compare_op=ALU.is_ge,
                               fill=MASKED, base=back, channel_multiplier=1).then_inc(window_masks_ready, 1)
            pool.wait_ge(window_masks_ready, 3 + 2 * n)
            pool.affine_select(out=t[:, :], in_=t[:, :], pattern=[[1, back + P]], compare_op=ALU.is_gt,
                               fill=MASKED, base=0, channel_multiplier=-1).then_inc(window_masks_ready, 1)

        def place_sinks(u):
            at_least(pool, probs_turned, u["buffer_free"])
            keys = u["parts"][0][0]["keys"]
            pool.tensor_copy(probs(u)[:, :, keys], sink_neg[:, R * u["g"]:R * (u["g"] + 1)]).then_inc(sinks_placed, 1)

        def scale_probs(u, part):
            pool.wait_ge(scale_ready, u["part0"] + part + 1)
            for s in u["parts"][part]:
                row = probs(u)[:, s["r"], s["at"]:s["at"] + s["keys"]]
                gate_col = BRANCHES * (R * u["g"] + s["r"]) + {"cmp": 0, "slc": 1, "win": 2, "swa": 0}[s["what"]]
                pool.tensor_scalar(row, row, row_s[mixer(u)][:, u["number"] % 2, s["column"]:s["column"] + 1],
                                   1.0 if u["kind"] == "swa" else gate[:, u["qb"], gate_col:gate_col + 1],
                                   ALU.mult, ALU.mult).then_inc(probs_ready, 1)

        pool.wait_ge(consts_done, 1)
        for what, u, i in orders["swa"]["pool"]:
            if what == "sinks":
                place_sinks(u)
            else:
                scale_probs(u, i)

        pool.wait_ge(pos_ready, 1)
        pool.wait_ge(kc_ready, 3)
        wait_taken(pool, 0, NSA_USE + 1)
        pool.wait_ge(vc_ready, 3)
        wait_taken(pool, 1, NSA_USE + 1)
        for kind in range(2):
            for g in range(KV):
                seq = kcs[2 * kind + g][:, :].rearrange("p (c t two) -> p two t c", t=CT // 2, two=2)
                for late in range(2):
                    rows = slice(late * CT // 2, (late + 1) * CT // 2)
                    pos = posT[:, kind * CT + late * CT // 2:kind * CT + (late + 1) * CT // 2]
                    pool.tensor_tensor(cx[kind][:, rows, g, 0:CB - 1], seq[:, 0, :, late:late + CB - 1],
                                       pos.unsqueeze(2).to_broadcast([P, CT // 2, CB - 1]),
                                       ALU.add).then_inc(cx_ready, 1)

        pool.wait_ge(product_done[0], UP_USE[0])
        pool.iota(t_slc[:, :], [[-1, SEQ + P]], base=SEQ, channel_multiplier=1,
                  allow_small_or_imprecise_dtypes=True).then_inc(masks_ready, 1)
        pool.memset(t_cmp[:, :, :], 0.0).then_inc(masks_ready, 1)
        pool.wait_ge(masks_ready, 2)
        pool.affine_select(out=t_slc[:, :], in_=t_slc[:, :], pattern=[[-1, SEQ + P]], compare_op=ALU.is_ge,
                           fill=MASKED, base=SEQ, channel_multiplier=1).then_inc(masks_ready, 1)
        pool.affine_select(out=t_cmp[:, :, :], in_=t_cmp[:, :, :], pattern=[[P, QB], [-CMP_STRIDE, CB]],
                           compare_op=ALU.is_ge, fill=MASKED, base=-(CMP_LEN - 1),
                           channel_multiplier=1).then_inc(masks_ready, 1)

        pool.wait_ge(v_turned, 4)
        pool.wait_ge(ob_hi_ready, 1)
        pool.tensor_tensor(obl[:, 2:4, :], qb_[:, 2:4, :], obh[:, 2:4, :], ALU.subtract).then_inc(ob_lo_late, 1)
        pool.wait_ge(consts_done, 2)
        for what, u, i in orders["nsa"]["pool"]:
            scale_probs(u, i)

        for j in range(KT - 1):
            pool.wait_ge(gated[j % 2], j // 2 * 2 + 2)
            pool.tensor_tensor(merged[:, j, :], sg[j % 2][:, 0, :], sg[j % 2][:, 1, :], ALU.add).then_inc(merged_ready, 1)

        def norm_affine(t):
            pool.wait_ge(normed, t + 1)
            pool.tensor_tensor(acc[:, t, :], acc[:, t, :], ln_g[:, :], ALU.mult).then_inc(ln_scaled, 1)
            pool.wait_ge(ln_scaled, t + 1)
            pool.tensor_tensor(acc[:, t, :], acc[:, t, :], ln_b[:, :], ALU.add).then_inc(ln_done, 1)

        pool.wait_ge(ln_in, 32)
        for t in range(QB):
            norm_affine(t)
        for t in range(QB):
            pool.wait_ge(h_turned, t + 1)
            pool.tensor_scalar(acc[:, t, :], acc[:, t, :], ALPHA, 1.0, ALU.mult, ALU.mult).then_inc(residual_ready, 1)

        with pool.Fori(0, CHUNKS) as c:
            for slot in range(CHUNK):
                pool.wait_ge(relu_ready[slot], c + 1)
                pool.wait_ge(ul_ready[slot], c + 1)
                pool.tensor_tensor(usq[slot][:, :], relu[slot][:, :], relu[slot][:, :],
                                   ALU.mult).then_inc(usq_ready[slot], 1)
        for t in range(SHIFTED_BY_POOL):
            pool.wait_ge(scaled2, t + 1)
            pool.tensor_tensor(acc[:, t, :], acc[:, t, :], ln_b[:, :], ALU.add).then_inc(out_ready, 1)

    @block.scalar
    def _(act):
        def split_x(n, slot, tile):
            act.wait_ge(x_turned[slot], n + 1)
            act.activation(xh[:, :, bass.ds(tile * P, P)], tiles(4 + 2 * slot), ACT.Copy).then_inc(xh_ready[slot], 1)

        def split_w(slot, n):
            act.wait_ge(w_loaded[slot], (n + 1) * 16)
            at_least(act, product_done[slot], n)
            act.activation(w_hi[slot][:, :, :], w_raw[slot][:, :, :], ACT.Copy).then_inc(w_hi_ready[slot], 1)

        for tile in range(QB):
            split_x(tile // 2, tile % 2, tile)
            if tile in (3, 4):
                split_w(tile - 3, 0)
        def keys_high(what, slot, n):
            act.wait_ge(product_done[slot], n + 1)
            for g in range(KV):
                rows = slice(g * HEAD_DIM, (g + 1) * HEAD_DIM)
                for to in range(2):
                    act.activation(k_hi[what][to * HEAD_DIM:(to + 1) * HEAD_DIM, g, :], wide(2 * slot)[rows, :],
                                   ACT.Copy).then_inc(kv_hi_ready, 1)

        def values_high(what, i):
            act.wait_ge(v_turned, i + 1)
            for g in range(KV):
                act.activation(v_hl[what][:, :, g, 0:HEAD_DIM], tiles(4)[:, :, g * HEAD_DIM:(g + 1) * HEAD_DIM],
                               ACT.Copy).then_inc(v_hi_ready, 1)

        def product_out(dst, slot, n):
            act.wait_ge(product_done[slot], n + 1)
            act.activation(dst, wide(2 * slot), ACT.Copy).then_inc(product_taken[slot], 1)

        split_w(0, 1)
        product_out(qb_[:, 0, :], 0, 0)
        split_w(1, 1)
        split_w(0, 2)
        keys_high("swa", 0, 1)
        split_w(1, 2)
        product_out(vT[:, :], 1, 1)
        split_w(0, 3)
        product_out(qb_[:, 2, :], 0, 2)
        values_high("swa", 0)
        split_w(1, 3)

        def stage_queries(u):
            step = u["step"]
            at_least(act, scores_done, q_free[step])
            for r in range(R):
                rows = slice((r % 2) * HEAD_DIM, (r % 2 + 1) * HEAD_DIM)
                act.activation(q_st[mixer(u)][step % 2][rows, r, :],
                               heads_out(u)[rows, 2 * u["g"] + r // 2, u["qb"] * P:(u["qb"] + 1) * P],
                               ACT.Copy, scale=query_scale(u, r)).then_inc(q_hi_ready, 1)

        def exps(u, part):
            p, m = probs(u), mixer(u)
            for s in u["parts"][part]:
                n = u["number"] % 2
                c = s["column"]
                act.wait_ge(row_max, s["number"] + 1)
                if u["kind"] == "swa":
                    act.wait_ge(sinks_placed, u["step"] + 1)
                row = p[:, s["r"], s["at"]:s["at"] + s["keys"] + (u["kind"] == "swa")]
                act.activation(row, row, ACT.Exp, scale=-1.0, bias=m_neg[m][:, n, c:c + 1],
                               accum_out=row_l[m][:, n, c:c + 1]).then_inc(exp_done, 1)

        def turned_high(u, i):
            t, m = u["block0"] + i, mixer(u)
            rows = CB if u["blocks"][i][0] == "cmp" else P
            act.wait_ge(probs_turned, t + 1)
            at_least(act, values_done, t - PT_RING + 1)
            act.activation(pt_hi[m][t % PT_RING][0:rows, :, :],
                           ps[0:rows, turn_bank(u, t), :].rearrange("p (r q) -> p r q", r=R),
                           ACT.Copy).then_inc(pt_hi_ready, 1)

        def outputs_low(u):
            act.wait_ge(values_done, u["block0"] + len(u["blocks"]))
            at_least(act, o_ready, 2 * u["step"])
            act.activation(o_sum[mixer(u)][0:HEAD_DIM, :, :],
                           ps[HEAD_DIM:P, OUT_BANK, :].rearrange("p (r q) -> p r q", r=R),
                           ACT.Copy).then_inc(o_low_ready, 1)

        def branch_high(slot, i):
            act.wait_ge(wb_loaded[slot], i * 32 + 32)
            at_least(act, y_done[0], i * 2 + (slot - 1) if not isinstance(i, int) or i else 0)
            act.activation(w_hi[slot][:, :, :], w_raw[slot][:, :, :], ACT.Copy).then_inc(wb_hi_ready[slot], 1)

        def gate_out(b):
            side, j = b % 2, b // 2
            act.wait_ge(product_done[side], GATE_USE + j + 1)
            at_least(act, gate_stored[side], 16 * j)
            act.activation(gate_raw[side][:, :], wide(2 * side), ACT.Copy).then_inc(gate_copied[side], 1)

        def attention(m):
            for n, (what, u, i) in enumerate(orders[m]["act"]):
                if m == "nsa" and n == 2:
                    act.wait_ge(v_turned, 4)
                    act.activation(gate[:, :, :], tiles(4)[:, :, 0:BRANCHES * HEADS], ACT.Sigmoid).then_inc(gate_ready, 1)
                if what == "stage_high":
                    stage_queries(u)
                elif what == "exp":
                    exps(u, i)
                elif what == "high":
                    turned_high(u, i)
                elif what == "out_low":
                    outputs_low(u)
                elif what == "split_high":
                    split_w(i % 2, GATE_USE + i // 2)
                elif what == "branch_high":
                    branch_high(0, 0)
                else:
                    gate_out(i)

        attention("swa")

        split_w(0, NSA_USE + 1)
        act.wait_ge(o_ready, 2 * SWA_STEPS)
        act.wait_ge(product_done[0], NSA_USE + 1)
        for g in range(KV):
            rows = slice(g * HEAD_DIM, (g + 1) * HEAD_DIM)
            act.activation(kcs[g][0:HEAD_DIM, :], wide(0)[rows, :], ACT.Copy).then_inc(kc_ready, 1)
            act.activation(kcs[g][HEAD_DIM:P, 0:SEQ - 1], wide(0)[rows, 1:SEQ],
                           ACT.Copy).then_inc(kc_ready if g == 0 else product_taken[0], 1)
        split_w(1, NSA_USE + 1)
        for i in range(2):
            product_out(qa[:, 2 * i, :], 0, NSA_USE + 1 + i)
            split_w(0, NSA_USE + 2 + i)
            split_w(1, NSA_USE + 2 + i)
        act.wait_ge(hidden_done, 1)
        act.activation(g_in[:, :], ps[:, HIDDEN_BANK, :], ACT.Copy).then_inc(hidden_copied, 1)
        act.wait_ge(gelu_step, 3)
        act.activation(g_u[:, :], g_t[:, :], ACT.Tanh, scale=float(GELU_IN)).then_inc(tanh_done, 1)
        act.wait_ge(hidden_done, 1)
        act.activation(obh[:, :, :], qb_[:, :, :], ACT.Copy).then_inc(ob_hi_ready, 1)
        keys_high("slc", 0, NSA_USE + 3)
        split_w(0, NSA_USE + 4)
        act.wait_ge(cmp_done, 1)
        act.activation(k_hi["cmp"][:, :, :], ps[:, SMALL_BANK, 0:P].rearrange("p (g c) -> p g c", g=KV),
                       ACT.Copy).then_inc(cmp_hi_ready, 1)
        act.activation(v_hl["cmp"][0:CB, 0, :, 0:HEAD_DIM],
                       ps[0:CB, SMALL_BANK, P:2 * P].rearrange("p (g d) -> p g d", g=KV),
                       ACT.Copy).then_inc(cmp_hi_ready, 1)
        product_out(vT[:, :], 1, NSA_USE + 3)
        split_w(1, NSA_USE + 4)
        keys_high("win", 0, NSA_USE + 4)
        values_high("slc", 1)
        split_w(0, NSA_USE + 5)
        product_out(vT[:, :], 1, NSA_USE + 4)
        act.wait_ge(product_done[1], UP_USE[1])
        branch_high(1, 0)
        product_out(gaT[:, :], 0, NSA_USE + 5)
        values_high("win", 2)

        act.wait_ge(product_done[0], UP_USE[0])
        attention("nsa")

        def merge(i, more):
            for slot in range(2):
                act.wait_ge(gates_back[slot], i * 32 + 32)
                act.activation(sg[slot][:, :, :], sg[slot][:, :, :], ACT.Sigmoid).then_inc(sg_ready[slot], 1)
                act.wait_ge(wo_loaded, i * 32 + 16 * (slot + 1))
                act.activation(wo_hi[:, i * 2 + slot, :], wo_raw[:, :], ACT.Copy).then_inc(wo_hi_ready, 1)
                if more:
                    branch_high(slot, i + 1)

        act.wait_ge(o_ready, 2 * STEPS)
        act.wait_ge(values_done, BLOCKS)
        for half in range(2):
            act.activation(oah[:, 2 * half:2 * half + 2, :], qa[:, 2 * half:2 * half + 2, :],
                           ACT.Copy).then_inc(oa_hi_ready, 1)
        merge(0, True)
        with act.Fori(1, KT // 2 - 1) as i:
            merge(i, True)
        merge(KT // 2 - 1, False)

        def stage_merged(slot, n, tile):
            at_least(act, mix_done[slot], n)
            act.activation(mst_hi[slot][:, :, :], merged[:, :, bass.ds(tile * P, P)],
                           ACT.Copy).then_inc(mst_hi_ready[slot], 1)

        def deviation(slot, count):
            act.wait_ge(var_ready, count + 1)
            act.activation(rstd[:, slot, 0:1], mv[:, slot, 1:2], ACT.Sqrt, bias=eps[:, :]).then_inc(std_ready, 1)

        act.wait_ge(y_done[1], KT)
        act.wait_ge(merged_ready, KT - 1)
        for slot in range(2):
            act.activation(mst_hi[slot][:, 0:KT - 1, :], merged[:, 0:KT - 1, slot * P:(slot + 1) * P],
                           ACT.Copy).then_inc(mst_head_hi, 1)
        act.wait_ge(merged_ready, KT)
        for slot in range(2):
            act.activation(mst_hi[slot][:, KT - 1, :], merged[:, KT - 1, slot * P:(slot + 1) * P],
                           ACT.Copy).then_inc(mst_hi_ready[slot], 1)
        act.wait_ge(y_done[0], KT)
        split_w(0, UP_USE[0])
        split_w(1, UP_USE[1])
        with act.Fori(0, QB // 2 - 1) as i:
            for slot in range(2):
                deviation(slot, i * 2 + slot)
                stage_merged(slot, i + 1, (i + 1) * 2 + slot)
        def split_h(t):
            act.wait_ge(h_turned, t + 1)
            act.activation(hh[:, :, t * P:(t + 1) * P], tiles(H_BANK[t]), ACT.Copy).then_inc(hh_ready, 1)

        deviation(0, QB - 2)
        act.wait_ge(mix_done[1], QB // 2)
        split_h(0)
        split_h(1)
        deviation(1, QB - 1)
        for t in range(2, QB):
            split_h(t)

        def relu_out(slot, c):
            act.wait_ge(product_done[slot], c + (UP_USE[slot] + 1))
            at_least(act, usq_ready[slot], c)
            act.activation(relu[slot][:, :], wide(2 * slot), ACT.Relu).then_inc(relu_ready[slot], 1)

        def hidden_high(slot, c, parity):
            act.wait_ge(usq_ready[slot], c + 1)
            at_least(act, down_done, (c - 1) * 16)
            act.activation(uh[parity][:, slot, :], usq[slot][:, :], ACT.Copy).then_inc(uh_ready[slot], 1)

        def down_weights(c):
            for slot in range(CHUNK):
                act.wait_ge(row_loaded[slot], (c + 1) * 16)
                at_least(act, down_done, c * 16)
                act.activation(wd_hi[slot][:, :], row_raw[slot][:, :], ACT.Copy).then_inc(row_hi_ready[slot], 1)

        def mlp_step(c, parity, ups, splits):
            down_weights(c)
            if ups:
                for slot in range(CHUNK):
                    if splits:
                        split_w(slot, c + (UP_USE[slot] + 2))
                    relu_out(slot, c + 1)
                for slot in range(CHUNK):
                    hidden_high(slot, c + 1, 1 - parity)

        for slot in range(CHUNK):
            split_w(slot, UP_USE[slot] + 1)
            relu_out(slot, 0)
        for slot in range(CHUNK):
            hidden_high(slot, 0, 0)
        mlp_step(0, 0, True, True)
        mlp_step(1, 1, True, True)
        with act.Fori(1, CHUNKS // 2 - 1) as i:
            mlp_step(i * 2, 0, True, True)
            mlp_step(i * 2 + 1, 1, True, True)
        mlp_step(CHUNKS - 2, 0, True, False)
        for slot in range(CHUNK):
            act.wait_ge(row_loaded[slot], CHUNKS * 16)
            act.wait_ge(product_done[slot], UP_USE[slot] + CHUNKS)
            act.activation(wd_last_hi[slot][:, :], row_raw[slot][:, :], ACT.Copy).then_inc(row_hi_ready[slot], 1)
        def deviation2(t):
            act.wait_ge(mean2_ready, t + 1)
            act.activation(squares[:, :], acc[:, t, :], ACT.Square, bias=mv2[:, t, 0:1],
                           accum_out=mv2[:, t, 1:2]).then_inc(var2_ready, 1)
            act.wait_ge(var2_ready, t + 1)
            act.activation(rstd2[:, t, 0:1], mv2[:, t, 1:2], ACT.Sqrt, scale=1.0 / D_MODEL,
                           bias=eps[:, :]).then_inc(std2_ready, 1)

        def normalise2(t):
            act.wait_ge(shift_ready, t + 1)
            act.activation(acc[:, t, :], acc[:, t, :], ACT.Identity, scale=rstd2[:, t, 1:2],
                           bias=rstd2[:, t, 2:3]).then_inc(normed2, 1)

        for t in range(QB):
            deviation2(t)
            if t >= 1:
                normalise2(t - 1)
        normalise2(QB - 1)

    @block.vector
    def _(dve):
        def split_x(n, slot, tile):
            dve.wait_ge(xh_ready[slot], n + 1)
            cols = bass.ds(tile * P, P)
            dve.tensor_tensor(xl[:, :, cols], tiles(4 + 2 * slot), xh[:, :, cols],
                              ALU.subtract).then_inc(xl_ready[slot], 1)

        def split_w(slot, n):
            dve.wait_ge(w_hi_ready[slot], n + 1)
            dve.tensor_tensor(w_lo[slot][:, :, :], w_raw[slot][:, :, :], w_hi[slot][:, :, :],
                              ALU.subtract).then_inc(w_lo_ready[slot], 1)

        for tile in range(QB):
            split_x(tile // 2, tile % 2, tile)
            if tile in (3, 4):
                split_w(tile - 3, 0)
        dve.wait_ge(pos_turned, 1)
        dve.tensor_copy(posT[:, :], ps[:, POS_BANK, 0:2 * CT]).then_inc(pos_ready, 1)
        def keys_low(what, slot, number):
            dve.wait_ge(kv_hi_ready, 4 * number + 4)
            for g in range(KV):
                rows = slice(g * HEAD_DIM, (g + 1) * HEAD_DIM)
                for to in range(2):
                    last = dve.tensor_tensor(k_lo[what][to * HEAD_DIM:(to + 1) * HEAD_DIM, g, :], wide(2 * slot)[rows, :],
                                             k_hi[what][rows, g, :], ALU.subtract)
                    last.then_inc(product_taken[slot] if g and to else kv_lo_ready, 1)

        def values_low(what, number):
            dve.wait_ge(v_hi_ready, 2 * number + 2)
            for g in range(KV):
                dve.tensor_tensor(v_hl[what][:, :, g, HEAD_DIM:P], tiles(4)[:, :, g * HEAD_DIM:(g + 1) * HEAD_DIM],
                                  v_hl[what][:, :, g, 0:HEAD_DIM], ALU.subtract).then_inc(v_lo_ready, 1)

        def product_out(dst, slot, n):
            dve.wait_ge(product_done[slot], n + 1)
            dve.tensor_copy(dst, wide(2 * slot)).then_inc(product_taken[slot], 1)

        split_w(0, 1)
        dve.wait_ge(sinks_in, 16)
        dve.tensor_scalar(sink_neg[:, :], sink_row[:, :], -1.0, None, ALU.mult).then_inc(consts_done, 1)
        product_out(qb_[:, 1, :], 1, 0)
        split_w(1, 1)
        split_w(0, 2)
        keys_low("swa", 0, 0)
        split_w(1, 2)
        split_w(0, 3)
        values_low("swa", 0)
        product_out(qb_[:, 3, :], 1, 2)
        split_w(1, 3)
        dve.wait_ge(consts_done, 1)

        def stage_queries(u):
            step = u["step"]
            for r in range(R):
                rows = slice((r % 2) * HEAD_DIM, (r % 2 + 1) * HEAD_DIM)
                other = slice((1 - r % 2) * HEAD_DIM, (2 - r % 2) * HEAD_DIM)
                dve.wait_ge(q_hi_ready, R * step + r + 1)
                dve.scalar_tensor_tensor(
                    out=q_st[mixer(u)][step % 2][other, r, :],
                    in0=heads_out(u)[rows, 2 * u["g"] + r // 2, u["qb"] * P:(u["qb"] + 1) * P],
                    scalar=query_scale(u, r), in1=q_st[mixer(u)][step % 2][rows, r, :],
                    op0=ALU.mult, op1=ALU.subtract).then_inc(q_lo_ready, 1)

        def maxima(u, part):
            p = probs(u)
            at_least(dve, probs_turned, u["buffer_free"])
            dve.wait_ge(scores_done, u["part0"] + part + 1)
            row = score_row(u["part0"] + part)
            for s in u["parts"][part]:
                c, h = s["column"], R * u["g"] + s["r"]
                start = sink_neg[:, h:h + 1] if u["kind"] == "swa" else 3e38
                dve.tensor_tensor_reduce(out=p[:, s["r"], s["at"]:s["at"] + s["keys"]],
                                         in0=row[:, s["score0"]:s["score0"] + s["keys"]],
                                         in1=table(u, s), scale=slope(u, s), scalar=start, op0=ALU.add, op1=ALU.min,
                                         accum_out=m_neg[mixer(u)][:, u["number"] % 2, c:c + 1]).then_inc(row_max, 1)

        def one_over_sums(u, part):
            n, segs = u["number"] % 2, u["parts"][part]
            dve.wait_ge(exp_done, segs[-1]["number"] + 1)
            cols = slice(segs[0]["column"], segs[-1]["column"] + 1)
            dve.reciprocal(row_s[mixer(u)][:, n, cols], row_l[mixer(u)][:, n, cols]).then_inc(scale_ready, 1)

        def turned_low(u, i):
            t = u["block0"] + i
            rows = CB if u["blocks"][i][0] == "cmp" else P
            dve.wait_ge(pt_hi_ready, t + 1)
            dve.tensor_tensor(pt_lo[mixer(u)][t % PT_RING][0:rows, :, :], ps[0:rows, turn_bank(u, t), :].rearrange("p (r q) -> p r q", r=R),
                              pt_hi[mixer(u)][t % PT_RING][0:rows, :, :], ALU.subtract).then_inc(pt_lo_ready, 1)

        def outputs(u):
            dve.wait_ge(o_low_ready, u["step"] + 1)
            both = ps[0:HEAD_DIM, OUT_BANK, :].rearrange("p (a b q) -> p b a q", b=2, q=P)
            low = o_sum[mixer(u)][0:HEAD_DIM, :, :].rearrange("p (a b) q -> p b a q", b=2)
            for odd in range(2):
                dve.tensor_tensor(heads_out(u)[odd * HEAD_DIM:(odd + 1) * HEAD_DIM, 2 * u["g"]:2 * u["g"] + 2,
                                               u["qb"] * P:(u["qb"] + 1) * P],
                                  both[:, odd], low[:, odd], ALU.add).then_inc(o_ready, 1)

        def branch_low(slot, i):
            dve.wait_ge(wb_hi_ready[slot], i + 1)
            dve.tensor_tensor(w_lo[slot][:, :, :], w_raw[slot][:, :, :], w_hi[slot][:, :, :],
                              ALU.subtract).then_inc(wb_lo_ready[slot], 1)

        def attention(m):
            for n, (what, u, i) in enumerate(orders[m]["dve"]):
                if m == "nsa" and n == 2:
                    dve.wait_ge(const_ready, 3)
                    dve.wait_ge(gate_ready, 1)
                    cmp_gates = gate[:, 0, :].rearrange("p (h b) -> p h b", b=BRANCHES)[:, :, 0]
                    dve.tensor_scalar(cmp_gates, cmp_gates, seen[:, :], None, ALU.mult).then_inc(consts_done, 1)
                    dve.wait_ge(masks_ready, 4)
                if what == "stage_low":
                    stage_queries(u)
                elif what == "maxima":
                    maxima(u, i)
                elif what == "sums":
                    one_over_sums(u, i)
                elif what == "low":
                    turned_low(u, i)
                elif what == "out":
                    outputs(u)
                elif what == "split_low":
                    split_w(i % 2, GATE_USE + i // 2)
                else:
                    branch_low(0, 0)

        dve.wait_ge(window_masks_ready, 6)
        attention("swa")

        split_w(0, NSA_USE + 1)
        dve.wait_ge(product_done[1], NSA_USE + 1)
        for g in range(KV):
            rows = slice(g * HEAD_DIM, (g + 1) * HEAD_DIM)
            dve.tensor_copy(kcs[KV + g][0:HEAD_DIM, :], wide(2)[rows, :]).then_inc(vc_ready, 1)
            dve.tensor_copy(kcs[KV + g][HEAD_DIM:P, 0:SEQ - 1],
                            wide(2)[rows, 1:SEQ]).then_inc(vc_ready if g == 0 else product_taken[1], 1)
        split_w(1, NSA_USE + 1)
        for i in range(2):
            split_w(0, NSA_USE + 2 + i)
            product_out(qa[:, 2 * i + 1, :], 1, NSA_USE + 1 + i)
            split_w(1, NSA_USE + 2 + i)
        dve.wait_ge(hidden_copied, 1)
        dve.tensor_tensor(g_t[:, :], g_in[:, :], g_in[:, :], ALU.mult).then_inc(gelu_step, 1)
        dve.wait_ge(gelu_step, 1)
        dve.tensor_scalar(g_t[:, :], g_t[:, :], 0.044715, 1.0, ALU.mult, ALU.add).then_inc(gelu_step, 1)
        dve.wait_ge(gelu_step, 2)
        dve.tensor_tensor(g_t[:, :], g_t[:, :], g_in[:, :], ALU.mult).then_inc(gelu_step, 1)
        dve.wait_ge(tanh_done, 1)
        dve.tensor_scalar(g_u[:, :], g_u[:, :], 1.0, 0.5, ALU.add, ALU.mult).then_inc(gelu_step, 1)
        dve.wait_ge(gelu_step, 4)
        dve.tensor_tensor(g_out[:, :, :, :, :].rearrange("p a b g c -> p (a b g c)"), g_u[:, :], g_in[:, :],
                          ALU.mult).then_inc(gelu_ready, 1)

        keys_low("slc", 0, 1)
        split_w(0, NSA_USE + 4)
        dve.wait_ge(cmp_hi_ready, 2)
        dve.tensor_tensor(k_lo["cmp"][:, :, :], ps[:, SMALL_BANK, 0:P].rearrange("p (g c) -> p g c", g=KV),
                          k_hi["cmp"][:, :, :], ALU.subtract).then_inc(cmp_lo_ready, 1)
        dve.tensor_tensor(v_hl["cmp"][0:CB, 0, :, HEAD_DIM:P],
                          ps[0:CB, SMALL_BANK, P:2 * P].rearrange("p (g d) -> p g d", g=KV),
                          v_hl["cmp"][0:CB, 0, :, 0:HEAD_DIM], ALU.subtract).then_inc(cmp_lo_ready, 1)
        split_w(1, NSA_USE + 4)
        keys_low("win", 0, 2)
        values_low("slc", 1)
        split_w(0, NSA_USE + 5)
        dve.wait_ge(cmp_done, 1)
        dve.wait_ge(ob_hi_ready, 1)
        dve.tensor_tensor(obl[:, 0:2, :], qb_[:, 0:2, :], obh[:, 0:2, :], ALU.subtract).then_inc(ob_lo_ready, 1)
        branch_low(1, 0)
        values_low("win", 2)
        attention("nsa")

        def merged_heads_low():
            for slot in range(2):
                dve.wait_ge(mst_head_hi, slot + 1)
                dve.tensor_tensor(mst_lo[slot][:, 0:KT - 1, :], merged[:, 0:KT - 1, slot * P:(slot + 1) * P],
                                  mst_hi[slot][:, 0:KT - 1, :], ALU.subtract).then_inc(mst_head_lo, 1)

        def merge(i, more):
            for slot in range(2):
                dve.wait_ge(wo_hi_ready, i * 2 + (slot + 1))
                dve.tensor_tensor(wo_lo[:, i * 2 + slot, :], wo_raw[:, :], wo_hi[:, i * 2 + slot, :],
                                  ALU.subtract).then_inc(wo_lo_ready, 1)
                dve.wait_ge(sg_ready[slot], i + 1)
                for side in (1, 0):
                    if side == 0 and slot == 1 and not more:
                        merged_heads_low()
                    dve.wait_ge(y_done[side], i * 2 + (slot + 1))
                    dve.tensor_tensor(sg[slot][:, side, :], sg[slot][:, side, :], wide(Y_BANK[slot][side]),
                                      ALU.mult).then_inc(gated[slot], 1)
                if more:
                    branch_low(slot, i + 1)

        for half in range(2):
            dve.wait_ge(oa_hi_ready, half + 1)
            rows = slice(2 * half, 2 * half + 2)
            dve.tensor_tensor(oal[:, rows, :], qa[:, rows, :], oah[:, rows, :], ALU.subtract).then_inc(oa_lo_ready, 1)
        merge(0, True)
        with dve.Fori(1, KT // 2 - 1) as i:
            merge(i, True)
        merge(KT // 2 - 1, False)

        def split_row(slot, n, lo, hi):
            dve.wait_ge(row_hi_ready[slot], n + 1)
            dve.tensor_tensor(lo, row_raw[slot][:, :], hi, ALU.subtract).then_inc(row_lo_ready[slot], 1)

        def stage_merged(slot, n, tile):
            dve.wait_ge(mst_hi_ready[slot], n + 1)
            dve.tensor_tensor(mst_lo[slot][:, :, :], merged[:, :, bass.ds(tile * P, P)], mst_hi[slot][:, :, :],
                              ALU.subtract).then_inc(mst_lo_ready[slot], 1)

        STEPS_OF_NORM = 3

        def norm(t, slot, count):
            for half in range(2):
                dve.bn_stats(bn[:, slot, half, :], acc[:, t, half * HALF:(half + 1) * HALF]).then_inc(ln_step, 1)
            dve.wait_ge(ln_step, count * STEPS_OF_NORM + 2)
            dve.bn_aggr(mv[:, slot, :], bn[:, slot, :, :].rearrange("p a b -> p (a b)")).then_inc(var_ready, 1)
            dve.wait_ge(std_ready, count + 1)
            dve.reciprocal(rstd[:, slot, 1:2], rstd[:, slot, 0:1]).then_inc(ln_step, 1)
            dve.wait_ge(ln_step, count * STEPS_OF_NORM + 3)
            dve.tensor_scalar(acc[:, t, :], acc[:, t, :], mv[:, slot, 0:1], rstd[:, slot, 1:2],
                              ALU.subtract, ALU.mult).then_inc(normed, 1)

        def add_residual(slot, n, t):
            dve.wait_ge(xres_in[slot], (n + 1) * 16)
            dve.wait_ge(mix_done[slot], n + 1)
            dve.scalar_tensor_tensor(out=acc[:, t, :], in0=x_raw[slot][:, :], scalar=ALPHA, in1=wide(2 * slot),
                                     op0=ALU.mult, op1=ALU.add).then_inc(z_ready[slot], 1)
            dve.wait_ge(z_ready[slot], n + 1)

        dve.wait_ge(gated[1], KT)
        dve.tensor_tensor(merged[:, KT - 1, :], sg[1][:, 0, :], sg[1][:, 1, :], ALU.add).then_inc(merged_ready, 1)
        for slot in range(2):
            dve.wait_ge(mst_hi_ready[slot], 1)
            dve.tensor_tensor(mst_lo[slot][:, KT - 1, :], merged[:, KT - 1, slot * P:(slot + 1) * P],
                              mst_hi[slot][:, KT - 1, :], ALU.subtract).then_inc(mst_lo_ready[slot], 1)
        split_w(0, UP_USE[0])
        split_w(1, UP_USE[1])
        for i in range(QB // 2 - 1):
            for slot in range(2):
                add_residual(slot, i, i * 2 + slot)
                norm(i * 2 + slot, slot, i * 2 + slot)
                stage_merged(slot, i + 1, (i + 1) * 2 + slot)
        def split_h(t):
            dve.wait_ge(hh_ready, t + 1)
            dve.tensor_tensor(hl[:, :, t * P:(t + 1) * P], tiles(H_BANK[t]), hh[:, :, t * P:(t + 1) * P],
                              ALU.subtract).then_inc(hl_ready, 1)

        add_residual(0, QB // 2 - 1, QB - 2)
        norm(QB - 2, 0, QB - 2)
        add_residual(1, QB // 2 - 1, QB - 1)
        split_h(0)
        split_h(1)
        norm(QB - 1, 1, QB - 1)
        for t in range(2, QB):
            split_h(t)

        def hidden_low(slot, c, parity):
            dve.wait_ge(uh_ready[slot], c + 1)
            dve.tensor_tensor(ul[parity][:, slot, :], usq[slot][:, :], uh[parity][:, slot, :],
                              ALU.subtract).then_inc(ul_ready[slot], 1)

        def add_down(c, q):
            dve.wait_ge(down_done, c * 16 + (q + 1))
            cols = acc[:, q // 2, (q % 2) * HALF:(q % 2 + 1) * HALF]
            dve.tensor_tensor(cols, cols, ps[:, 4 + q % 4, :], ALU.add).then_inc(down_added, 1)

        def mlp_step(c, parity, ups, splits):
            for slot in range(CHUNK):
                split_row(slot, c, wd_lo[slot][:, :], wd_hi[slot][:, :])
            if splits:
                for slot in range(CHUNK):
                    split_w(slot, c + (UP_USE[slot] + 2))
            if ups:
                hidden_low(0, c + 1, 1 - parity)
            for q in range(16):
                if ups and q == 3:
                    hidden_low(1, c + 1, 1 - parity)
                if ups and not splits and q == 6:
                    for slot in range(CHUNK):
                        split_row(slot, CHUNKS - 1, wd_last_lo[slot][:, :], wd_last_hi[slot][:, :])
                add_down(c, q)

        for slot in range(CHUNK):
            dve.sem_inc(ul_ready[slot], 1)
        for slot in range(CHUNK):
            split_w(slot, UP_USE[slot] + 1)
        for slot in range(CHUNK):
            hidden_low(slot, 0, 0)
        dve.wait_ge(residual_ready, QB)
        with dve.Fori(0, CHUNKS // 2 - 1) as i:
            mlp_step(i * 2, 0, True, True)
            mlp_step(i * 2 + 1, 1, True, True)
        mlp_step(CHUNKS - 2, 0, True, False)
        def add_last(q):
            dve.wait_ge(down_done, (CHUNKS - 1) * 16 + (q + 1))
            cols = acc[:, q // 2, (q % 2) * HALF:(q % 2 + 1) * HALF]
            dve.tensor_tensor_reduce(out=cols, in0=ps[:, 4 + q % 4, :], in1=cols, scale=1.0, scalar=0.0,
                                     op0=ALU.add, op1=ALU.add,
                                     accum_out=sums2[:, q // 2, q % 2:q % 2 + 1]).then_inc(down_added, 1)

        def minus_mean(t):
            dve.wait_ge(down_added, 16 * (CHUNKS - 1) + 2 * t + 2)
            dve.tensor_scalar(mv2[:, t, 0:1], sums2[:, t, 0:1], sums2[:, t, 1:2], -1.0 / D_MODEL,
                              ALU.add, ALU.mult).then_inc(mean2_ready, 1)

        def scale_and_shift(t):
            dve.wait_ge(std2_ready, t + 1)
            dve.reciprocal(rstd2[:, t, 1:2], rstd2[:, t, 0:1]).then_inc(rstd2_step, 1)
            dve.wait_ge(rstd2_step, t + 1)
            dve.tensor_scalar(rstd2[:, t, 2:3], mv2[:, t, 0:1], rstd2[:, t, 1:2], 1.0,
                              ALU.mult, ALU.mult).then_inc(shift_ready, 1)

        def scale_rows(t):
            dve.wait_ge(normed2, t + 1)
            dve.tensor_tensor(acc[:, t, :], acc[:, t, :], ln_g[:, :], ALU.mult).then_inc(scaled2, 1)

        def shift_rows(t):
            dve.wait_ge(scaled2, t + 1)
            dve.tensor_tensor(acc[:, t, :], acc[:, t, :], ln_b[:, :], ALU.add).then_inc(late_out_ready, 1)

        dve.wait_ge(ln_in, 64)
        for t in range(QB):
            add_last(2 * t)
            add_last(2 * t + 1)
            if t >= 1:
                scale_and_shift(t - 1)
            minus_mean(t)
            if t >= 2:
                scale_rows(t - 2)
        scale_and_shift(QB - 1)
        scale_rows(QB - 2)
        scale_rows(QB - 1)
        shift_rows(QB - 1)

    @block.tensor
    def _(pe):
        def turn_x(t):
            pe.wait_ge(x_in[t % 4], 16 * (t // 4 + 1))
            at_least(pe, xl_ready[t % 2], t // 2)
            for k in range(KT):
                last = pe.transpose(tiles(4 + 2 * (t % 2))[:, k, :], x_first[t % 4][:, k * P:(k + 1) * P], ident[:, :])
            last.then_inc(x_turned[t % 2], 1)

        def product_piece(slot, n, k, hi, lo, taken):
            if k == 0:
                pe.wait_ge(w_lo_ready[slot], n + 1)
                if taken:
                    wait_taken(pe, slot, taken)
            for p, (w, a) in enumerate(((w_hi, hi), (w_hi, lo), (w_lo, hi))):
                for half in range(2):
                    last = pe.matmul(ps[:, 2 * slot + half, :], w[slot][:, k, :],
                                     a[:, k, half * HALF:(half + 1) * HALF],
                                     start=(k == 0 and p == 0), stop=(k == KT - 1 and p == 2))
            if k == KT - 1:
                last.then_inc(product_done[slot], 1)

        def part_product(slot, tokens, tiles_of_k, hi, lo):
            for k in tiles_of_k:
                for p, (w, a) in enumerate(((w_hi, hi), (w_hi, lo), (w_lo, hi))):
                    last = pe.matmul(wide(2 * slot)[:, tokens], w[slot][:, k, :], a[:, k, tokens],
                                     start=(k == 0 and p == 0), stop=(k == KT - 1 and p == 2))
            return last

        def product(slot, n, hi, lo, taken):
            for k in range(KT):
                product_piece(slot, n, k, hi, lo, taken)

        def project(slot, n):
            product(slot, n, xh, xl, n)

        pe.wait_ge(const_ready, 1)
        for t in range(4):
            turn_x(t)
        pe.wait_ge(small_in, 32)
        pe.transpose(ps[:, POS_BANK, 0:2 * CT], pos_nat[:, :], ident[0:2 * CT, 0:2 * CT]).then_inc(pos_turned, 1)
        for slot in range(2):
            pe.wait_ge(xl_ready[slot], 2)
        for slot in range(2):
            pe.wait_ge(w_lo_ready[slot], 1)
            for part in range(2):
                turn_x(4 + 2 * slot + part)
                part_product(slot, slice(0, HALF), range(part * KT // 2, (part + 1) * KT // 2), xh, xl)
        for slot in range(2):
            pe.wait_ge(xl_ready[slot], QB // 2)
        pe.wait_ge(pos_ready, 1)
        for slot in range(2):
            part_product(slot, slice(HALF, SEQ), range(KT), xh, xl).then_inc(product_done[slot], 1)
        project(0, 1)
        project(1, 1)
        project(0, 2)
        def turn_values(src, number, slot, n):
            wait_taken(pe, slot, n + 1)
            at_least(pe, v_lo_ready, 2 * number)
            for k in range(QB):
                last = pe.transpose(tiles(4)[:, k, :], src[:, k * P:(k + 1) * P], ident[:, :])
            last.then_inc(v_turned, 1)

        turn_values(vT, 0, 1, 1)
        project(1, 2)

        def in_banks(start, count):
            edges = [start] + [e for e in (HALF, 2 * HALF) if start < e < start + count] + [start + count]
            return [(a - start, b - a) for a, b in zip(edges, edges[1:])]

        def scores(u, part):
            number = u["part0"] + part
            row = score_row(number)
            pe.wait_ge(q_lo_ready, R * (u["step"] + 1))
            at_least(pe, row_max, scores_free[number][1])
            for s in u["parts"][part]:
                for c, n in in_banks(s["score0"], s["keys"]):
                    for k in (k_hi, k_lo):
                        last = pe.matmul(row[:, s["score0"] + c:s["score0"] + c + n],
                                         q_st[mixer(u)][u["step"] % 2][:, s["r"], :],
                                         k[s["what"]][:, u["g"], s["key0"] + c:s["key0"] + c + n],
                                         start=(k is k_hi), stop=(k is k_lo))
            last.then_inc(scores_done, 1)

        def turn_probs(u, i):
            t = u["block0"] + i
            what, _, at = u["blocks"][i]
            rows = CB if what == "cmp" else P
            pe.wait_ge(probs_ready, u["seg0"] + len(u["segs"]))
            if t == SWA_BLOCKS:
                pe.wait_ge(v_lo_ready, 6)
                pe.wait_ge(gate_ready, 1)
            at_least(pe, pt_lo_ready, t + 1 - TURNS[mixer(u)])
            for r in range(R):
                last = pe.transpose(ps[0:rows, turn_bank(u, t), r * P:(r + 1) * P], probs(u)[:, r, at:at + rows],
                                    ident[:, :])
            last.then_inc(probs_turned, 1)

        def weigh_values(u, i):
            t = u["block0"] + i
            what, kb, _ = u["blocks"][i]
            rows = CB if what == "cmp" else P
            pe.wait_ge(pt_lo_ready, t + 1)
            first = u["first_of_step"] and i == 0
            if first:
                at_least(pe, o_ready, 2 * u["step"])
            last_block = u["last_of_step"] and i == len(u["blocks"]) - 1
            for n, pt in enumerate((pt_hi, pt_lo)):
                last = pe.matmul(ps[:, OUT_BANK, :], v_hl[what][0:rows, kb, u["g"], :],
                                 pt[mixer(u)][t % PT_RING][0:rows, :, :].rearrange("p r q -> p (r q)"),
                                 start=(first and n == 0), stop=(last_block and n == 1))
            last.then_inc(values_done, 1)

        def attention(m):
            for what, u, i in orders[m]["pe"]:
                if what == "scores":
                    scores(u, i)
                elif what == "turn":
                    turn_probs(u, i)
                elif what == "weigh":
                    weigh_values(u, i)
                else:
                    b, k = divmod(i, KT)
                    n = GATE_USE + b // 2
                    product_piece(b % 2, n, k, xh, xl, n)

        pe.wait_ge(kv_lo_ready, 3)
        pe.wait_ge(v_lo_ready, 2)
        attention("swa")

        for i in range(3):
            for slot in range(2):
                project(slot, NSA_USE + i)
        pe.wait_ge(o_ready, 2 * SWA_STEPS)
        pe.wait_ge(row_max, SWA_SEGS)
        pe.wait_ge(pt_lo_ready, SWA_BLOCKS)
        pe.wait_ge(cx_ready, 8)
        pe.wait_ge(fills_done, 4)
        pe.wait_ge(cmp_w_in, 80)
        for kind in range(2):
            for f in range(2):
                col = (2 * kind + f) * P
                for t in range(CT):
                    last = pe.matmul(ps[:, HIDDEN_BANK, col:col + P], cw1[kind][:, t, f * P:(f + 1) * P],
                                     cx[kind][:, t, :, :].rearrange("p g c -> p (g c)"),
                                     start=(t == 0), stop=(t == CT - 1))
        last.then_inc(hidden_done, 1)
        project(0, NSA_USE + 3)
        pe.wait_ge(gelu_ready, 1)
        for f in range(2):
            pe.matmul(ps[:, SMALL_BANK, 0:P], cw2k[:, f, :, :].rearrange("p a d -> p (a d)"),
                      g_out[:, 0, f, :, :].rearrange("p g c -> p (g c)"), start=(f == 0), stop=(f == 1))
        for g in range(KV):
            for f in range(2):
                last = pe.matmul(ps[0:CB, SMALL_BANK, P + g * HEAD_DIM:P + (g + 1) * HEAD_DIM],
                                 g_out[:, 1, f, g, :], cw2v[:, f, :], start=(f == 0), stop=(f == 1))
        last.then_inc(cmp_done, 1)

        project(1, NSA_USE + 3)
        project(0, NSA_USE + 4)
        turn_values(vT, 1, 1, NSA_USE + 3)
        project(1, NSA_USE + 4)
        project(0, NSA_USE + 5)
        turn_values(vT, 2, 1, NSA_USE + 4)
        turn_values(gaT, 3, 0, NSA_USE + 5)

        pe.wait_ge(kv_lo_ready, 9)
        pe.wait_ge(cmp_lo_ready, 2)
        for slot in range(2):
            wait_taken(pe, slot, UP_USE[slot])
        attention("nsa")

        pe.wait_ge(o_ready, 2 * STEPS)
        pe.wait_ge(pt_lo_ready, BLOCKS)
        pe.wait_ge(row_max, SEGS)
        pe.wait_ge(ob_lo_ready, 1)
        pe.wait_ge(ob_lo_late, 1)

        def merge(i):
            for slot in range(2):
                pe.wait_ge(wb_lo_ready[slot], i + 1)
                at_least(pe, gated[slot], i * 2)
                for side, hi, lo in ((1, obh, obl), (0, oah, oal)):
                    if side == 0 and slot == 0:
                        pe.wait_ge(oa_lo_ready, 2)
                    for k in range(4):
                        for p, (w, a) in enumerate(((w_hi, hi), (w_hi, lo), (w_lo, hi))):
                            for half in range(2):
                                last = pe.matmul(ps[:, Y_BANK[slot][side] + half, :], w[slot][:, 4 * side + k, :],
                                                 a[:, k, half * HALF:(half + 1) * HALF],
                                                 start=(k == 0 and p == 0), stop=(k == 3 and p == 2))
                    last.then_inc(y_done[side], 1)

        merge(0)
        with pe.Fori(1, KT // 2) as i:
            merge(i)

        def mix(n, slot, head_first=False):
            if head_first:
                pe.wait_ge(mst_head_lo, slot + 1)
            else:
                pe.wait_ge(mst_lo_ready[slot], n + 1)
            at_least(pe, z_ready[slot], n)
            for k in range(KT):
                if head_first and k == KT - 1:
                    pe.wait_ge(mst_lo_ready[slot], 1)
                for p, (a, w) in enumerate(((mst_hi, wo_hi), (mst_hi, wo_lo), (mst_lo, wo_hi))):
                    for half in range(2):
                        last = pe.matmul(ps[:, 2 * slot + half, :], a[slot][:, k, :],
                                         w[:, k, half * HALF:(half + 1) * HALF],
                                         start=(k == 0 and p == 0), stop=(k == KT - 1 and p == 2))
            last.then_inc(mix_done[slot], 1)

        pe.wait_ge(gated[0], KT)
        pe.wait_ge(wo_lo_ready, KT)
        mix(0, 0, True)
        mix(0, 1, True)
        with pe.Fori(1, QB // 2) as i:
            for slot in range(2):
                mix(i, slot)
        def turn_h(t):
            pe.wait_ge(ln_done, t + 1)
            before = [b for b in range(t) if H_BANK[b] == H_BANK[t]]
            if before:
                pe.wait_ge(hl_ready, before[-1] + 1)
            elif t == 2:
                pe.wait_ge(z_ready[1], QB // 2)
            for k in range(KT):
                last = pe.transpose(tiles(H_BANK[t])[:, k, :], acc[:, t, k * P:(k + 1) * P], ident[:, :])
            last.then_inc(h_turned, 1)

        for t in range(QB - 3):
            turn_h(t)

        def up(c):
            for slot in range(CHUNK):
                at_least(pe, relu_ready[slot], c)
                product(slot, c + UP_USE[slot], hh, hl, 0)

        def down(c, parity, wd_hi=wd_hi, wd_lo=wd_lo):
            for slot in range(CHUNK):
                pe.wait_ge(row_lo_ready[slot], c + 1)
                pe.wait_ge(ul_ready[slot], c + 2)
            for q in range(16):
                if q >= 4:
                    pe.wait_ge(down_added, c * 16 + (q - 3))
                else:
                    at_least(pe, down_added, c * 16 + (q - 3) if not isinstance(c, int) or c else 0)
                tile, half = q // 2, q % 2
                for f in range(CHUNK):
                    for p, (a, w) in enumerate(((uh, wd_hi), (uh, wd_lo), (ul, wd_hi))):
                        last = pe.matmul(ps[:, 4 + q % 4, :], a[parity][:, f, tile * P:(tile + 1) * P],
                                         w[f][:, half * HALF:(half + 1) * HALF],
                                         start=(f == 0 and p == 0), stop=(f == CHUNK - 1 and p == 2))
                last.then_inc(down_done, 1)

        for slot in range(2):
            pe.wait_ge(w_lo_ready[slot], UP_USE[slot] + 1)
        pe.wait_ge(z_ready[0], QB // 2)
        for turned, quarter, slot in ((2, 0, 0), (4, 1, 0), (4, 0, 1), (4, 1, 1), (6, 2, 0), (6, 2, 1), (8, 3, 0), (8, 3, 1)):
            pe.wait_ge(hl_ready, turned)
            last = part_product(slot, slice(quarter * 2 * P, (quarter + 1) * 2 * P), range(KT), hh, hl)
            if quarter == 3:
                last.then_inc(product_done[slot], 1)
            t = {(0, 0): QB - 3, (1, 0): QB - 2, (0, 1): QB - 1}.get((quarter, slot))
            if t:
                turn_h(t)
        up(1)
        down(0, 0)
        up(2)
        down(1, 1)
        with pe.Fori(1, CHUNKS // 2 - 1) as i:
            up(i * 2 + 1)
            down(i * 2, 0)
            up(i * 2 + 2)
            down(i * 2 + 1, 1)
        up(CHUNKS - 1)
        down(CHUNKS - 2, 0)
        down(CHUNKS - 1, 1, wd_last_hi, wd_last_lo)

    ctx.close()


_INS = ["x", "w_in", "cmp_pos_k", "cmp_w1_k", "cmp_w2_k", "cmp_pos_v", "cmp_w1_v", "cmp_w2_v", "sink_logits",
        "w_branch_a", "w_branch_b", "w_out", "ln1_g", "ln1_b", "w_up", "w_down", "ln2_g", "ln2_b"]


def kernel(**inputs):
    import concourse.bacc as bacc
    from concourse.bass_utils import run_bass_kernel_spmd

    nc = bacc.Bacc("TRN2", target_bir_lowering=False, num_devices=1)
    arrays = {f"in_{name}": np.ascontiguousarray(inputs[name]) for name in _INS}
    args = [nc.dram_tensor(name, a.shape, mybir.dt.from_np(a.dtype), kind="ExternalInput").ap()
            for name, a in arrays.items()]
    args.append(nc.dram_tensor("out_h", (1, SEQ, D_MODEL), F32, kind="ExternalOutput").ap())
    layer(nc, *args)
    return run_bass_kernel_spmd(nc, [arrays], core_ids=[0]).results[0]["out_h"]
```
